# Optimizing a Trainium2 kernel written in Bass

```python
import math
import jax, jax.numpy as jnp
from jax import lax
import numpy as np

D_MODEL = 1024
BATCH = 1
SEQ = 256
DEPTH = 1

ATTN_HEADS = 8
ATTN_HEAD_DIM = 64
ATTN_WIDTH = ATTN_HEADS * ATTN_HEAD_DIM
KV_RANK = 256
IDX_HEADS = 8
IDX_DIM = 64
TOPK_MAX = 256
ATTN_QBLOCK = 64
N_BUCKETS = 32
MAX_DISTANCE = 128
SSM_HEADS = 16
SSM_HEAD_DIM = 64
SSM_INNER = SSM_HEADS * SSM_HEAD_DIM
SSM_GROUPS = 2
SSM_STATE = 128
CONV_WIDTH = 4
CONV_CH = SSM_INNER + 2 * SSM_GROUPS * SSM_STATE
SSD_CHUNK = 128
N_EXPERTS = 32
TOP_K = 4
D_EXPERT = D_MODEL
SWIGLU_LIMIT = 7.0
SWIGLU_ALPHA = 1.702
MOE_BLOCK = 128
EPS = 1e-6

SPLIT_SIZES = (ATTN_WIDTH, KV_RANK, IDX_HEADS * IDX_DIM, IDX_DIM, IDX_HEADS, SSM_INNER, CONV_CH, SSM_HEADS, 2 * D_MODEL)
D_IN = sum(SPLIT_SIZES)


def _rms(x, g, eps=EPS):
    xf = x.astype(jnp.float32)
    y = xf * lax.rsqrt(jnp.mean(xf * xf, axis=-1, keepdims=True) + eps)
    return (y * g.astype(jnp.float32)).astype(x.dtype)

def _layernorm(x, g, b, eps=EPS):
    xf = x.astype(jnp.float32)
    mu = jnp.mean(xf, axis=-1, keepdims=True)
    var = jnp.mean(jnp.square(xf - mu), axis=-1, keepdims=True)
    y = (xf - mu) * lax.rsqrt(var + eps) * g.astype(jnp.float32) + b.astype(jnp.float32)
    return y.astype(x.dtype)

def _t5_bucket(dist):
    n = jnp.maximum(dist, 0)
    max_exact = N_BUCKETS // 2
    nf = jnp.maximum(n, 1).astype(jnp.float32)
    large = max_exact + (jnp.log(nf / max_exact) / math.log(MAX_DISTANCE / max_exact) * (N_BUCKETS - max_exact)).astype(jnp.int32)
    large = jnp.minimum(large, N_BUCKETS - 1)
    return jnp.where(n < max_exact, n, large)

def _split(proj):
    idx = [int(i) for i in np.cumsum(SPLIT_SIZES)[:-1]]
    return jnp.split(proj, idx, axis=-1)

def _dsa_attention(q, k, v, q_idx, w_idx, k_idx, rel_bias):
    Bsz, L = q.shape[0], q.shape[1]
    topk = min(TOPK_MAX, L // 4)
    nblk = L // ATTN_QBLOCK
    scale = ATTN_HEAD_DIM ** -0.5
    key_pos = jnp.arange(L, dtype=jnp.int32)

    def to_blocks(a):
        return jnp.moveaxis(a.reshape(Bsz, nblk, ATTN_QBLOCK, *a.shape[2:]), 1, 0)

    def block(args):
        qb, qib, wib, start = args
        t = start + jnp.arange(ATTN_QBLOCK, dtype=jnp.int32)
        dots = jnp.einsum('bqhd,bsd->bqhs', qib, k_idx)
        score = jnp.einsum('bqh,bqhs->bqs', wib, jax.nn.relu(dots)).astype(jnp.float32)
        causal = key_pos[None, :] <= t[:, None]
        score = jnp.where(causal[None], score, -jnp.inf)
        _, sel = lax.top_k(score, topk)
        kg = jax.vmap(lambda kk, ii: kk[ii])(k, sel)
        vg = jax.vmap(lambda vv, ii: vv[ii])(v, sel)
        dist = t[None, :, None] - sel
        bias = jnp.moveaxis(rel_bias[_t5_bucket(dist)], -1, 2).astype(jnp.float32)
        logits = jnp.einsum('bqhd,bqkhd->bqhk', qb, kg).astype(jnp.float32) * scale + bias
        logits = jnp.where((dist >= 0)[:, :, None, :], logits, -jnp.inf)
        p = jax.nn.softmax(logits, axis=-1).astype(vg.dtype)
        return jnp.einsum('bqhk,bqkhd->bqhd', p, vg)

    starts = jnp.arange(nblk, dtype=jnp.int32) * ATTN_QBLOCK
    out = lax.map(block, (to_blocks(q), to_blocks(q_idx), to_blocks(w_idx), starts))
    return jnp.moveaxis(out, 0, 1).reshape(Bsz, L, ATTN_WIDTH)

def _mamba2_ssd(z, xbc, dt_raw, conv_w, conv_b, dt_bias, a_log, d_skip, norm_w):
    Bsz, L = xbc.shape[0], xbc.shape[1]
    nc = L // SSD_CHUNK
    hg = SSM_HEADS // SSM_GROUPS
    xbc = lax.conv_general_dilated(xbc, conv_w[:, None, :].astype(xbc.dtype), window_strides=(1,),
                                   padding=[(CONV_WIDTH - 1, 0)], dimension_numbers=('NWC', 'WIO', 'NWC'),
                                   feature_group_count=CONV_CH) + conv_b
    xbc = jax.nn.silu(xbc).astype(jnp.float32)
    xs, bm, cm = jnp.split(xbc, [SSM_INNER, SSM_INNER + SSM_GROUPS * SSM_STATE], axis=-1)
    dt = jax.nn.softplus(dt_raw.astype(jnp.float32) + dt_bias.astype(jnp.float32))
    a = -jnp.exp(a_log.astype(jnp.float32)).reshape(SSM_GROUPS, hg)

    def chunks(arr, *tail):
        return jnp.moveaxis(arr.reshape(Bsz, nc, SSD_CHUNK, *tail), 1, 0)

    x_c = chunks(xs, SSM_GROUPS, hg, SSM_HEAD_DIM)
    dt_c = chunks(dt, SSM_GROUPS, hg)
    b_c = chunks(bm, SSM_GROUPS, SSM_STATE)
    c_c = chunks(cm, SSM_GROUPS, SSM_STATE)
    causal = jnp.tril(jnp.ones((SSD_CHUNK, SSD_CHUNK), dtype=bool))[None, :, :, None, None]

    def step(state, inp):
        xc, dtc, bc, cc = inp
        acum = jnp.cumsum(dtc * a, axis=1)
        seg = acum[:, :, None] - acum[:, None, :]
        lmat = jnp.exp(jnp.where(causal, seg, -jnp.inf))
        cb = jnp.einsum('bign,bjgn->bijg', cc, bc)
        wmat = cb[..., None] * lmat * dtc[:, None]
        y = jnp.einsum('bijgh,bjghp->bighp', wmat, xc)
        y = y + jnp.einsum('bign,bghpn->bighp', cc, state) * jnp.exp(acum)[..., None]
        decay = jnp.exp(acum[:, -1:] - acum) * dtc
        state = state * jnp.exp(acum[:, -1])[..., None, None] + jnp.einsum('bjgn,bjgh,bjghp->bghpn', bc, decay, xc)
        return state, y

    h0 = jnp.zeros((Bsz, SSM_GROUPS, hg, SSM_HEAD_DIM, SSM_STATE), jnp.float32)
    _, ys = lax.scan(step, h0, (x_c, dt_c, b_c, c_c))
    y = jnp.moveaxis(ys, 0, 1).reshape(Bsz, L, SSM_HEADS, SSM_HEAD_DIM)
    y = y + d_skip.astype(jnp.float32)[:, None] * xs.reshape(Bsz, L, SSM_HEADS, SSM_HEAD_DIM)
    y = y.reshape(Bsz, L, SSM_INNER) * jax.nn.silu(z.astype(jnp.float32))
    yg = y.reshape(Bsz, L, SSM_GROUPS, SSM_INNER // SSM_GROUPS)
    yg = yg * lax.rsqrt(jnp.mean(yg * yg, axis=-1, keepdims=True) + EPS)
    y = yg.reshape(Bsz, L, SSM_INNER) * norm_w.astype(jnp.float32)
    return y.astype(z.dtype)

def _moe(h, w_router, b_router, w_gu, b_gu, w_dn, b_dn):
    Bsz, L, D = h.shape
    T = Bsz * L
    hf = h.reshape(T, D)
    logits = (hf @ w_router + b_router).astype(jnp.float32)
    top_val, top_idx = lax.top_k(logits, TOP_K)
    gates = jax.nn.softmax(top_val, axis=-1)
    n_assign = T * TOP_K
    e_flat = top_idx.reshape(n_assign)
    g_flat = gates.reshape(n_assign)
    tok_flat = jnp.arange(n_assign, dtype=jnp.int32) // TOP_K
    order = jnp.argsort(e_flat)
    e_sorted = e_flat[order]
    counts = jnp.bincount(e_flat, length=N_EXPERTS)
    padded = (counts + MOE_BLOCK - 1) // MOE_BLOCK * MOE_BLOCK
    pad_end = jnp.cumsum(padded)
    pad_start = pad_end - padded
    start = jnp.cumsum(counts) - counts
    rank = jnp.arange(n_assign, dtype=jnp.int32) - start[e_sorted]
    dest = pad_start[e_sorted] + rank
    n_rows = n_assign + N_EXPERTS * MOE_BLOCK
    row_tok = jnp.full((n_rows,), T, dtype=jnp.int32).at[dest].set(tok_flat[order])
    row_gate = jnp.zeros((n_rows,), jnp.float32).at[dest].set(g_flat[order])
    n_blk = n_rows // MOE_BLOCK
    blk_start = jnp.arange(n_blk, dtype=jnp.int32) * MOE_BLOCK
    blk_exp = jnp.minimum(jnp.sum(blk_start[:, None] >= pad_end[None, :], axis=1), N_EXPERTS - 1)
    h_pad = jnp.concatenate([hf, jnp.zeros((1, D), hf.dtype)], axis=0)

    def run_block(args):
        toks, e = args
        xb = h_pad[toks]
        gu = xb @ w_gu[e] + b_gu[e]
        g, u = gu[:, :D_EXPERT], gu[:, D_EXPERT:]
        g = jnp.minimum(g, SWIGLU_LIMIT)
        u = jnp.clip(u, -SWIGLU_LIMIT, SWIGLU_LIMIT)
        act = (u + 1.0) * (g * jax.nn.sigmoid(SWIGLU_ALPHA * g))
        return act @ w_dn[e] + b_dn[e]

    out = lax.map(run_block, (row_tok.reshape(n_blk, MOE_BLOCK), blk_exp))
    out = out.reshape(n_rows, D) * row_gate[:, None].astype(out.dtype)
    y = jax.ops.segment_sum(out, row_tok, num_segments=T + 1)[:T]
    return y.reshape(Bsz, L, D)

def first_inputs(seed: int = 0) -> dict:
    key = jax.random.key(seed)
    ks = jax.random.split(key, 32)
    f32 = jnp.float32

    def nrm(k, shape, scale):
        return jax.random.normal(k, shape, f32) * scale

    def gain(k, shape):
        return 1.0 + 0.05 * jax.random.normal(k, shape, f32)

    dt = jnp.exp(jax.random.uniform(ks[17], (DEPTH, SSM_HEADS), f32, math.log(1e-3), math.log(1e-1)))
    return {
        'x': nrm(ks[0], (BATCH, SEQ, D_MODEL), 1.0),
        'c': nrm(ks[1], (BATCH, D_MODEL), 1.0),
        'rel_bias': nrm(ks[2], (N_BUCKETS, ATTN_HEADS), 0.5),
        'w_ada': nrm(ks[3], (DEPTH, D_MODEL, 6 * D_MODEL), 0.5 * D_MODEL ** -0.5),
        'b_ada': nrm(ks[4], (DEPTH, 6 * D_MODEL), 0.02),
        'norm_mix': gain(ks[5], (DEPTH, D_MODEL)),
        'norm_ffn': gain(ks[6], (DEPTH, D_MODEL)),
        'w_in': nrm(ks[7], (DEPTH, D_MODEL, D_IN), D_MODEL ** -0.5),
        'kv_norm': gain(ks[8], (DEPTH, KV_RANK)),
        'w_kv_up': nrm(ks[9], (DEPTH, KV_RANK, 2 * ATTN_WIDTH), KV_RANK ** -0.5),
        'q_norm': gain(ks[10], (DEPTH, ATTN_HEAD_DIM)),
        'k_norm': gain(ks[11], (DEPTH, ATTN_HEAD_DIM)),
        'idx_k_ln_w': gain(ks[12], (DEPTH, IDX_DIM)),
        'idx_k_ln_b': nrm(ks[13], (DEPTH, IDX_DIM), 0.02),
        'w_attn_o': nrm(ks[14], (DEPTH, ATTN_WIDTH, D_MODEL), ATTN_WIDTH ** -0.5),
        'conv_w': nrm(ks[15], (DEPTH, CONV_WIDTH, CONV_CH), CONV_WIDTH ** -0.5),
        'conv_b': nrm(ks[16], (DEPTH, CONV_CH), 0.02),
        'dt_bias': dt + jnp.log(-jnp.expm1(-dt)),
        'a_log': jnp.log(jax.random.uniform(ks[18], (DEPTH, SSM_HEADS), f32, 1.0, 16.0)),
        'd_skip': gain(ks[19], (DEPTH, SSM_HEADS)),
        'ssm_norm': gain(ks[20], (DEPTH, SSM_INNER)),
        'w_ssm_o': nrm(ks[21], (DEPTH, SSM_INNER, D_MODEL), SSM_INNER ** -0.5),
        'w_out': nrm(ks[22], (DEPTH, D_MODEL, D_MODEL), D_MODEL ** -0.5),
        'w_router': nrm(ks[23], (DEPTH, D_MODEL, N_EXPERTS), D_MODEL ** -0.5),
        'b_router': nrm(ks[24], (DEPTH, N_EXPERTS), 0.01),
        'w_gu': nrm(ks[25], (DEPTH, N_EXPERTS, D_MODEL, 2 * D_EXPERT), D_MODEL ** -0.5),
        'b_gu': nrm(ks[26], (DEPTH, N_EXPERTS, 2 * D_EXPERT), 0.02),
        'w_dn': nrm(ks[27], (DEPTH, N_EXPERTS, D_EXPERT, D_MODEL), D_EXPERT ** -0.5),
        'b_dn': nrm(ks[28], (DEPTH, N_EXPERTS, D_MODEL), 0.02),
    }

def first_block(x, c, rel_bias, w_ada, b_ada, norm_mix, norm_ffn, w_in, kv_norm, w_kv_up, q_norm, k_norm,
              idx_k_ln_w, idx_k_ln_b, w_attn_o, conv_w, conv_b, dt_bias, a_log, d_skip, ssm_norm, w_ssm_o,
              w_out, w_router, b_router, w_gu, b_gu, w_dn, b_dn):
    Bsz, L, _ = x.shape
    cond = jax.nn.silu(c)
    for l in range(DEPTH):
        mod = cond @ w_ada[l] + b_ada[l]
        sh_m, sc_m, g_m, sh_f, sc_f, g_f = jnp.split(mod[:, None, :], 6, axis=-1)
        h = _rms(x, norm_mix[l]) * (1.0 + sc_m) + sh_m
        proj = h @ w_in[l]
        q, kv_lat, q_i, k_i, w_i, z, xbc, dt_raw, gate_logits = _split(proj)
        q = _rms(q.reshape(Bsz, L, ATTN_HEADS, ATTN_HEAD_DIM), q_norm[l])
        kv = _rms(kv_lat, kv_norm[l]) @ w_kv_up[l]
        k, v = jnp.split(kv, 2, axis=-1)
        k = _rms(k.reshape(Bsz, L, ATTN_HEADS, ATTN_HEAD_DIM), k_norm[l])
        v = v.reshape(Bsz, L, ATTN_HEADS, ATTN_HEAD_DIM)
        q_i = q_i.reshape(Bsz, L, IDX_HEADS, IDX_DIM) * (IDX_DIM ** -0.5)
        w_i = w_i * (IDX_HEADS ** -0.5)
        k_i = _layernorm(k_i, idx_k_ln_w[l], idx_k_ln_b[l])
        y_attn = _dsa_attention(q, k, v, q_i, w_i, k_i, rel_bias) @ w_attn_o[l]
        y_ssd = _mamba2_ssd(z, xbc, dt_raw, conv_w[l], conv_b[l], dt_bias[l], a_log[l], d_skip[l], ssm_norm[l]) @ w_ssm_o[l]
        g_attn, g_ssd = jnp.split(gate_logits, 2, axis=-1)
        mixed = jax.nn.sigmoid(g_attn) * y_attn + jax.nn.sigmoid(g_ssd) * y_ssd
        x = x + g_m * (mixed @ w_out[l])
        h = _rms(x, norm_ffn[l]) * (1.0 + sc_f) + sh_f
        x = x + g_f * _moe(h, w_router[l], b_router[l], w_gu[l], b_gu[l], w_dn[l], b_dn[l])
    return x


DEPTH_2 = 2

D_MIX = D_MODEL
ATTN_WIDTH_2 = D_MIX // 2
ATTN_HEADS_2 = ATTN_WIDTH_2 // ATTN_HEAD_DIM
DILATED_PATTERNS = ((128, 1), (512, 4), (2048, 16))
ROPE_THETA = 10000.0
MLSTM_WIDTH = D_MIX - ATTN_WIDTH_2
MLSTM_HEADS = 4
MLSTM_HEAD_DIM = MLSTM_WIDTH // MLSTM_HEADS
MLSTM_CHUNK = 128
MLSTM_CONV = 5
PROJ_COLS = 3 * ATTN_WIDTH_2 + 4 * MLSTM_WIDTH + 4 * MLSTM_HEADS
D_FF = ((8 * D_MODEL // 3 + 255) // 256) * 256
FFN_CONV = 3
NORM_EPS = 1e-6
NEG_INF = -1e30


def rms_norm(x, g):
    xf = x.astype(jnp.float32)
    y = xf * lax.rsqrt(jnp.mean(xf * xf, axis=-1, keepdims=True) + NORM_EPS)
    return (y * g.astype(jnp.float32)).astype(x.dtype)

def depthwise_conv_centred(x, w, b):
    k = w.shape[0]
    pad = k // 2
    s = x.shape[1]
    xp = jnp.pad(x, ((0, 0), (pad, pad), (0, 0)))
    out = xp[:, 0:s] * w[0]
    for j in range(1, k):
        out = out + xp[:, j:j + s] * w[j]
    return out + b

def apply_rotary(t):
    s, dh = t.shape[2], t.shape[3]
    inv_freq = ROPE_THETA ** (-jnp.arange(0, dh, 2, dtype=jnp.float32) / dh)
    ang = jnp.arange(s, dtype=jnp.float32)[:, None] * inv_freq[None, :]
    cos, sin = jnp.cos(ang), jnp.sin(ang)
    t1, t2 = t[..., :dh // 2], t[..., dh // 2:]
    return jnp.concatenate([t1 * cos - t2 * sin, t2 * cos + t1 * sin], axis=-1)

def dilated_window_branch(q, k, v, window, dilation):
    b, h, s, dh = q.shape
    half = window // (2 * dilation)
    blk = half
    n_sub = s // dilation
    nb = -(-n_sub // blk)
    lp = nb * blk

    def to_sub(t):
        return jnp.swapaxes(t.reshape(b, h, n_sub, dilation, dh), 2, 3)

    qs = jnp.pad(to_sub(q), ((0, 0), (0, 0), (0, 0), (0, lp - n_sub), (0, 0)))
    kpad = ((0, 0), (0, 0), (0, 0), (blk, lp - n_sub + blk), (0, 0))
    ks = jnp.pad(to_sub(k), kpad)
    vs = jnp.pad(to_sub(v), kpad)

    def band(t):
        return jnp.concatenate(
            [t[:, :, :, i * blk:i * blk + lp].reshape(b, h, dilation, nb, blk, dh) for i in range(3)], axis=4)

    qb = qs.reshape(b, h, dilation, nb, blk, dh)
    kb, vb = band(ks), band(vs)
    scores = jnp.einsum('bhrnqe,bhrnke->bhrnqk', qb, kb) * (dh ** -0.5)
    qi = jnp.arange(nb)[:, None] * blk + jnp.arange(blk)[None, :]
    ki = jnp.arange(nb)[:, None] * blk - blk + jnp.arange(3 * blk)[None, :]
    off = ki[:, None, :] - qi[:, :, None]
    valid = (jnp.abs(off) <= half) & (ki[:, None, :] >= 0) & (ki[:, None, :] < n_sub)
    scores = jnp.where(valid, scores, NEG_INF)
    m = jnp.max(scores, axis=-1, keepdims=True)
    p = jnp.exp(scores - m)
    den = jnp.sum(p, axis=-1)
    out = jnp.einsum('bhrnqk,bhrnke->bhrnqe', p, vb) / den[..., None]
    lse = m[..., 0] + jnp.log(den)
    out = jnp.swapaxes(out.reshape(b, h, dilation, lp, dh)[:, :, :, :n_sub], 2, 3).reshape(b, h, s, dh)
    lse = jnp.swapaxes(lse.reshape(b, h, dilation, lp)[:, :, :, :n_sub], 2, 3).reshape(b, h, s)
    return out, lse

def dilated_attention(q, k, v):
    outs, lses = [], []
    for window, dilation in DILATED_PATTERNS:
        o, l = dilated_window_branch(q, k, v, window, dilation)
        outs.append(o)
        lses.append(l)
    wts = jax.nn.softmax(jnp.stack(lses, axis=0), axis=0)
    out = wts[0][..., None] * outs[0]
    for i in range(1, len(outs)):
        out = out + wts[i][..., None] * outs[i]
    return out

def mlstm_direction(q, k, v, log_i, log_f):
    b, h, s, dh = q.shape
    ch = MLSTM_CHUNK
    nc = s // ch
    k = k * (dh ** -0.5)

    def chunks(t):
        return jnp.moveaxis(t.reshape(b, h, nc, ch, *t.shape[3:]), 2, 0)

    causal = jnp.tril(jnp.ones((ch, ch), dtype=bool))

    def step(carry, xs):
        c_st, n_st, m_st = carry
        qc, kc, vc, lic, lfc = xs
        bcum = jnp.cumsum(lfc, axis=-1)
        dlog = bcum[..., :, None] - bcum[..., None, :] + lic[..., None, :]
        dlog = jnp.where(causal, dlog, NEG_INF)
        inter = bcum + m_st[..., None]
        m_t = jnp.maximum(inter, jnp.max(dlog, axis=-1))
        sc = jnp.einsum('bhte,bhse->bhts', qc, kc) * jnp.exp(dlog - m_t[..., None])
        g = jnp.exp(inter - m_t)
        num = jnp.einsum('bhts,bhsf->bhtf', sc, vc) + g[..., None] * jnp.einsum('bhte,bhef->bhtf', qc, c_st)
        den = jnp.sum(sc, axis=-1) + g * jnp.einsum('bhte,bhe->bht', qc, n_st)
        h_t = num / jnp.maximum(jnp.abs(den), jnp.exp(-m_t))[..., None]
        b_last = bcum[..., -1]
        wlog = b_last[..., None] - bcum + lic
        m_new = jnp.maximum(b_last + m_st, jnp.max(wlog, axis=-1))
        wexp = jnp.exp(wlog - m_new[..., None])
        decay = jnp.exp(b_last + m_st - m_new)
        c_new = decay[..., None, None] * c_st + jnp.einsum('bhs,bhse,bhsf->bhef', wexp, kc, vc)
        n_new = decay[..., None] * n_st + jnp.einsum('bhs,bhse->bhe', wexp, kc)
        return (c_new, n_new, m_new), h_t

    init = (jnp.zeros((b, h, dh, dh), jnp.float32), jnp.zeros((b, h, dh), jnp.float32),
            jnp.zeros((b, h), jnp.float32))
    _, hs = lax.scan(step, init, (chunks(q), chunks(k), chunks(v), chunks(log_i), chunks(log_f)))
    return jnp.moveaxis(hs, 0, 2).reshape(b, h, s, dh)

def hybrid_mixer(hn, w_in, mlstm_conv_w, mlstm_conv_b, mlstm_gate_b, mlstm_head_g, w_out):
    b, s, _ = hn.shape
    f32 = jnp.float32
    sizes = [ATTN_WIDTH_2] * 3 + [MLSTM_WIDTH] * 4 + [4 * MLSTM_HEADS]
    split_at = np.cumsum(sizes)[:-1].tolist()
    aq, ak, av, mq, mk, mv, mo, gates = jnp.split(hn @ w_in, split_at, axis=-1)

    def heads(t, n):
        return jnp.transpose(t.astype(f32).reshape(b, s, n, -1), (0, 2, 1, 3))

    q = apply_rotary(heads(aq, ATTN_HEADS_2))
    k = apply_rotary(heads(ak, ATTN_HEADS_2))
    v = heads(av, ATTN_HEADS_2)
    attn = dilated_attention(q, k, v)
    attn = jnp.transpose(attn, (0, 2, 1, 3)).reshape(b, s, ATTN_WIDTH_2).astype(hn.dtype)

    qk = jax.nn.silu(depthwise_conv_centred(jnp.concatenate([mq, mk], axis=-1), mlstm_conv_w, mlstm_conv_b))
    mq, mk = jnp.split(qk, 2, axis=-1)
    q = heads(mq, MLSTM_HEADS)
    k = heads(mk, MLSTM_HEADS)
    v = heads(mv, MLSTM_HEADS)
    g = (gates + mlstm_gate_b).astype(f32).reshape(b, s, 4, MLSTM_HEADS)
    g = jnp.transpose(g, (2, 0, 3, 1))
    h_fwd = mlstm_direction(q, k, v, g[0], jax.nn.log_sigmoid(g[1]))
    flip = lambda t: jnp.flip(t, axis=2)
    h_bwd = flip(mlstm_direction(flip(q), flip(k), flip(v), flip(g[2]), flip(jax.nn.log_sigmoid(g[3]))))
    hm = h_fwd + h_bwd
    hm = hm * lax.rsqrt(jnp.mean(hm * hm, axis=-1, keepdims=True) + NORM_EPS)
    hm = jnp.transpose(hm, (0, 2, 1, 3)).reshape(b, s, MLSTM_WIDTH)
    mlstm = (hm * mlstm_head_g.astype(f32) * jax.nn.sigmoid(mo.astype(f32))).astype(hn.dtype)

    return jnp.concatenate([attn, mlstm], axis=-1) @ w_out

def conv_ffn(hn, w_up, conv_w, conv_b, w_down):
    u = depthwise_conv_centred(hn @ w_up, conv_w, conv_b)
    gate, val = jnp.split(u, 2, axis=-1)
    return (jax.nn.gelu(gate, approximate=True) * val) @ w_down

def second_inputs(seed: int = 0) -> dict:
    key = jax.random.key(seed)
    ks = jax.random.split(key, 16)

    def nrm(k, shape, scale):
        return jax.random.normal(k, shape, jnp.float32) * scale

    base = jnp.stack([jnp.zeros((MLSTM_HEADS,), jnp.float32),
                      jnp.linspace(3.0, 6.0, MLSTM_HEADS, dtype=jnp.float32)], axis=0)
    gate_b = (nrm(ks[5], (DEPTH_2, 2, 2, MLSTM_HEADS), 0.1) + base[None, None]).reshape(DEPTH_2, 4 * MLSTM_HEADS)
    return {
        'x': nrm(ks[0], (BATCH, SEQ, D_MODEL), 1.0),
        'mix_pre_g': 1.0 + nrm(ks[1], (DEPTH_2, D_MODEL), 0.02),
        'w_in': nrm(ks[2], (DEPTH_2, D_MODEL, PROJ_COLS), D_MODEL ** -0.5),
        'mlstm_conv_w': nrm(ks[3], (DEPTH_2, MLSTM_CONV, 2 * MLSTM_WIDTH), MLSTM_CONV ** -0.5),
        'mlstm_conv_b': nrm(ks[4], (DEPTH_2, 2 * MLSTM_WIDTH), 0.02),
        'mlstm_gate_b': gate_b,
        'mlstm_head_g': 1.0 + nrm(ks[6], (DEPTH_2, MLSTM_WIDTH), 0.02),
        'w_out': nrm(ks[7], (DEPTH_2, D_MIX, D_MODEL), D_MIX ** -0.5),
        'mix_post_g': 1.0 + nrm(ks[8], (DEPTH_2, D_MODEL), 0.02),
        'ffn_pre_g': 1.0 + nrm(ks[9], (DEPTH_2, D_MODEL), 0.02),
        'w_up': nrm(ks[10], (DEPTH_2, D_MODEL, 2 * D_FF), D_MODEL ** -0.5),
        'ffn_conv_w': nrm(ks[11], (DEPTH_2, FFN_CONV, 2 * D_FF), FFN_CONV ** -0.5),
        'ffn_conv_b': nrm(ks[12], (DEPTH_2, 2 * D_FF), 0.02),
        'w_down': nrm(ks[13], (DEPTH_2, D_FF, D_MODEL), D_FF ** -0.5),
        'ffn_post_g': 1.0 + nrm(ks[14], (DEPTH_2, D_MODEL), 0.02),
    }

def second_block(x, mix_pre_g, w_in, mlstm_conv_w, mlstm_conv_b, mlstm_gate_b, mlstm_head_g, w_out,
              mix_post_g, ffn_pre_g, w_up, ffn_conv_w, ffn_conv_b, w_down, ffn_post_g):
    for l in range(DEPTH_2):
        mixed = hybrid_mixer(rms_norm(x, mix_pre_g[l]), w_in[l], mlstm_conv_w[l], mlstm_conv_b[l],
                             mlstm_gate_b[l], mlstm_head_g[l], w_out[l])
        x = x + rms_norm(mixed, mix_post_g[l])
        ff = conv_ffn(rms_norm(x, ffn_pre_g[l]), w_up[l], ffn_conv_w[l], ffn_conv_b[l], w_down[l])
        x = x + rms_norm(ff, ffn_post_g[l])
    return x


def setup_inputs(seed=0):
    out = dict(first_inputs(seed))
    for name, value in second_inputs(seed + 1).items():
        if name != "x":
            out[name + "_2"] = value
    return out


def reference(
    x, c, rel_bias, w_ada, b_ada, norm_mix, norm_ffn, w_in, kv_norm, w_kv_up, q_norm, k_norm,
    idx_k_ln_w, idx_k_ln_b, w_attn_o, conv_w, conv_b, dt_bias, a_log, d_skip, ssm_norm, w_ssm_o,
    w_out, w_router, b_router, w_gu, b_gu, w_dn, b_dn, mix_pre_g_2, w_in_2, mlstm_conv_w_2,
    mlstm_conv_b_2, mlstm_gate_b_2, mlstm_head_g_2, w_out_2, mix_post_g_2, ffn_pre_g_2, w_up_2,
    ffn_conv_w_2, ffn_conv_b_2, w_down_2, ffn_post_g_2,
):
    x = first_block(
        x, c, rel_bias, w_ada, b_ada, norm_mix, norm_ffn, w_in, kv_norm, w_kv_up, q_norm,
        k_norm, idx_k_ln_w, idx_k_ln_b, w_attn_o, conv_w, conv_b, dt_bias, a_log, d_skip,
        ssm_norm, w_ssm_o, w_out, w_router, b_router, w_gu, b_gu, w_dn, b_dn,
    )
    return second_block(
        x, mix_pre_g_2, w_in_2, mlstm_conv_w_2, mlstm_conv_b_2, mlstm_gate_b_2, mlstm_head_g_2,
        w_out_2, mix_post_g_2, ffn_pre_g_2, w_up_2, ffn_conv_w_2, ffn_conv_b_2, w_down_2,
        ffn_post_g_2,
    )


_drawn_inputs = setup_inputs


def setup_inputs(seed=0):
    import zlib

    import numpy as np

    out = dict(_drawn_inputs(seed))
    spreads = {}
    factors = {'kv_norm': 3.515,
     'q_norm': 8.0,
     'k_norm': 7.725,
     'idx_k_ln_w': 4.987,
     'idx_k_ln_b': 6.881,
     'd_skip': 11.408,
     'b_gu': 5.946,
     'b_dn': 5.345,
     'mlstm_conv_b_2': 3.071,
     'ffn_post_g_2': 3.568,
     'conv_b': 4.06,
     'b_router': 3.035,
     'mlstm_head_g_2': 2.694}
    for name, (base, spread) in spreads.items():
        noise = np.random.default_rng([zlib.crc32(name.encode()), seed]).standard_normal(out[name].shape)
        drawn = base * np.exp(spread * noise) if base else spread * noise
        out[name] = __import__('jax').numpy.asarray(drawn.astype(out[name].dtype))
    for name, factor in factors.items():
        out[name] = (out[name] * factor).astype(out[name].dtype)
    return out
```

```python
from contextlib import ExitStack
import math

import numpy as np

import concourse.bass as bass
from concourse import mybir

F32 = mybir.dt.float32
I32 = mybir.dt.int32
ACT = mybir.ActivationFunctionType
ALU = mybir.AluOpType
AX = mybir.AxisListType

P = 128
D = 1024
L = 256
KC = D // P
NT = L // P
HEADS, HD = 8, 64
AW = HEADS * HD
TOPK = min(256, L // 4)
BUCKETS, MAX_DIST = 32, 128
SH, SG, SN = 16, 2, 128
SI = SH * 64
CONV_CH = SI + 2 * SG * SN
NX = CONV_CH // P
E, TOP_K, DE = 32, 4, 1024
PAIRS = E // 2
CAP = 64
ROUNDS = L // CAP
LIMIT, ALPHA = 7.0, 1.702
EPS = 1e-6
LAYERS = 2
MH = 4
FF = ((8 * D // 3 + 255) // 256) * 256
FC = FF // P
SLOT = 4096
SLOTS = 4
BANKS = 8
FAR = -3.0e38
NEG = -1.0e30

C_Q, C_KV, C_QI, C_KI = 0, 512, 768, 1280
C_Z, C_XBC, C_DT, C_GATE = 1352, 2376, 3912, 3928
D_IN = C_GATE + 2 * D


class Layout:

    def __init__(self, parts):
        self.at, self.n = {}, 0
        for name, n in parts:
            self.at[name] = (self.n, n)
            self.n += n

    def of(self, ap, name, rows=P):
        a, n = self.at[name]
        return ap[0:rows, a:a + n]


CONSTS = Layout([("ident", P), ("tri_le", P), ("tri_ge", P), ("ones", 2 * P), ("ssd_mask", P), ("causal", NT * L),
                 ("mask_fwd", P), ("mask_bwd", P), ("log_count", NT * L), ("cos", NT * 32), ("sin", NT * 32),
                 ("bucket", 384), ("slot_no", CAP), ("pair_row", P)])
PARAMS = Layout([("c", KC), ("norm_mix", KC), ("norm_ffn", KC), ("b_ada", 48), ("conv_w", NX * 4), ("conv_b", NX),
                 ("kv_norm", 2), ("q_norm", 1), ("k_norm", 1), ("ln_w", 1), ("ln_b", 1), ("ssm_norm", KC),
                 ("dt_bias", SH), ("a_log", SH), ("d_skip", SH), ("b_router", E), ("rel_bias", HEADS)])
PARAMS2 = Layout([("mix_pre", KC), ("mix_post", KC), ("ffn_pre", KC), ("ffn_post", KC), ("conv_w", 8 * 5),
                  ("conv_b", 8), ("head_g", MH), ("ffn_w", 2 * FC * 3), ("ffn_b", 2 * FC), ("gate_b", 16)])


def constants():
    out = np.zeros((P, CONSTS.n), np.float32)

    def put(name, v):
        a, n = CONSTS.at[name]
        v = np.asarray(v, np.float32)
        out[:v.shape[0], a:a + n] = v.reshape(v.shape[0], n)

    i, j = np.arange(P)[:, None], np.arange(P)[None, :]
    put("ident", i == j)
    put("tri_le", i <= j)
    put("tri_ge", i >= j)
    put("ones", np.ones((P, 2 * P)))
    put("ssd_mask", np.where(i <= j, 0.0, NEG))
    q = np.arange(L).reshape(NT, P).T[:, :, None]
    k = np.arange(L)[None, None, :]
    put("causal", np.where(k <= q, 0.0, FAR))
    put("mask_fwd", np.where(j <= i, 0.0, NEG))
    put("mask_bwd", np.where(j >= i, 0.0, NEG))
    off = np.abs(q - k)
    count = (off <= 64) * 1 + (off % 4 == 0) * (off // 4 <= 64) + (off % 16 == 0) * (off // 16 <= 64)
    put("log_count", np.where(count > 0, np.log(np.maximum(count, 1)), NEG))
    inv = (10000.0 ** (-np.arange(0, 64, 2, dtype=np.float32) / np.float32(64))).astype(np.float32)
    ang = (np.arange(L, dtype=np.float32)[:, None] * inv[None, :]).astype(np.float32).reshape(NT, P, 32)
    put("cos", np.cos(ang).transpose(1, 0, 2))
    put("sin", np.sin(ang).transpose(1, 0, 2))
    n = np.maximum(L - 1 - np.arange(384), 0)
    exact = BUCKETS // 2
    large = exact + (np.log(np.maximum(n, 1).astype(np.float32) / exact)
                     / math.log(MAX_DIST / exact) * (BUCKETS - exact)).astype(np.int32)
    bucket = np.where(n < exact, n, np.minimum(large, BUCKETS - 1))
    put("bucket", np.arange(BUCKETS)[:, None] == bucket[None, :])
    put("slot_no", np.broadcast_to(np.arange(CAP), (P, CAP)))
    put("pair_row", np.arange(2)[:, None] == (np.arange(P)[None, :] // CAP))
    return out


class Uses:

    def __init__(self, full, free, names, inc=1, base=None, twice=(), credit=0):
        n = len(full)
        self.credit = credit
        self.full, self.free, self.inc = full, free, inc
        self.base = list(base or [0] * n)
        self.at = {}
        self.per, self.fills_per, self.filled = [0] * n, [0] * n, {}
        for i, name in enumerate(names):
            assert name not in self.at, name
            self.at[name] = (i % n, self.per[i % n])
            self.per[i % n] += 1
            self.fills_per[i % n] += 2 if name in twice else 1
            self.filled[name] = self.fills_per[i % n]

    def no(self, name):
        return self.at[name][0]

    def _value(self, name, it):
        b, u = self.at[name]
        return it * self.per[b] + (self.base[b] + u + self.credit)

    def empty(self, *name, it=0):
        return self.free[self.at[name][0]], self._value(name, it)

    def ready(self, *name, it=0):
        b = self.at[name][0]
        return self.full[b], it * (self.fills_per[b] * self.inc) + (self.base[b] + self.filled[name]) * self.inc

    def released(self, *name, it=0):
        return self.free[self.at[name][0]], self._value(name, it) + 1

    def fills(self, *name):
        return self.full[self.at[name][0]], self.inc

    def frees(self, *name):
        return self.free[self.at[name][0]], 1

    def after(self, passes=1):
        return [b + passes * p for b, p in zip(self.base, self.per)]


class Steps:

    def __init__(self, eng, sem):
        self.eng, self.sem, self.n = eng, sem, 0

    def __call__(self, ins):
        self.n += 1
        ins.then_inc(self.sem, 1)
        self.eng.wait_ge(self.sem, self.n)

    def restart(self):
        self.eng.sem_clear(self.sem)
        self.n = 0


def front_banks():
    u = [("m", j) for j in range(4)] + [("ss", 1)]
    u += [("q", t) for t in range(NT)] + [("kv", t) for t in range(NT)]
    u += [("qi", p) for p in range(2)] + [("kw", t) for t in range(NT)]
    u += [("xbc", p) for p in range(NX // 2)] + [("dt",), ("bvec",)]
    u += [("kvT",), ("qT", 0), ("qT", 1), ("kiT",)]
    u += [("z", s, t) for s in range(2) for t in range(NT)]
    u += [("kv_up", s, t) for s in range(2) for t in range(NT)]
    u += [("dots", t, g) for t in range(NT) for g in range(4)]
    u += [("kT", t) for t in range(NT)]
    u += [("ga", 0), ("ga", 1), ("m", 4), ("ga", 2), ("ga", 3), ("m", 5)]
    for t in range(NT):
        u += [("S", t, g) for g in range(4)]
        u += [("ga", 4 + 2 * t), ("ga", 5 + 2 * t), ("m", 6 + t)]
        u += [("PT", t, j) for j in range(2 * (t + 1))] + [("O", t)]
    u += [("m", 8)]
    u += [("xT", t, j) for t in range(NT) for j in range(2)] + [("BT",), ("acum",), ("m", 9)]
    u += [("cb", c) for c in range(2)] + [("row", 0, j) for j in range(4)]
    u += [("state", g) for g in range(SG)]
    u += [("yi", 0, g) for g in range(SG)] + [("row", 1, j) for j in range(4)]
    u += [("yx", g) for g in range(SG)] + [("yi", 1, g) for g in range(SG)]
    u += [("yT", t, j) for t in range(NT) for j in range(2)]
    u += [("m", 10)] + [("ya", p) for p in range(4)] + [("ys", p) for p in range(4)] + [("m", 11)]
    u += [("x1", p) for p in range(4)] + [("ss", 2)]
    u += [("tok", t, j) for t in range(NT) for j in range(2)]
    u += [("rl",), ("cum",), ("GT",)] + [("yb", p) for p in range(4)] + [("hg", j) for j in range(2)]
    return u


def front_slots():
    s = [("ada", j) for j in range(4)] + [("win", j) for j in range(8)] + [("wkv",)]
    s += [("gate", 0), ("ada", 4), ("gate", 1), ("ada", 5), ("gate", 2), ("ada", 6), ("gate", 3), ("ada", 7)]
    s += [("ada", 8), ("ada", 9), ("ada", 10), ("wo",), ("wso", 0), ("wso", 1)]
    s += [("wout", 0), ("wout", 1), ("ada", 11)]
    return s


WIN_LAST = [("q", 1), ("qi", 0), ("kw", 1), ("xbc", 1), ("xbc", 3), ("xbc", 5), ("z", 0, 1), ("z", 1, 1)]
PAIR_BANKS = [("g", 0), ("u", 0), ("g", 1), ("u", 1), ("sT",), ("aT", 0), ("dn", 0), ("dn", 1), ("aT", 1),
              ("hg", 0), ("hg", 1)] + [("y", p) for p in range(4)]
PAIR_SLOTS = [(w, half, e) for half in range(2) for w in ("wg", "wu") for e in range(2)] + \
             [("wd", kh, e) for kh in range(2) for e in range(2)]


def layer_banks():
    u = [("ss", 0)]
    u += [(n, t) for n in ("aq", "ak", "av") for t in range(NT)]
    u += [("mqk", p) for p in range(4)] + [("gates",)] + [("mv", t) for t in range(NT)]
    u += [("mo", p) for p in range(2)] + [("bc",)]
    u += [(n, t) for t in range(NT) for n in ("qT", "kT")]
    u += [("S", 0, g) for g in range(4)]
    u += [("qk", c) for c in range(2)] + [("kt", t) for t in range(NT)]
    u += [("PT", 0, j) for j in range(4)] + [("O", 0)]
    u += [("S", 1, g) for g in range(4)]
    u += [("r", 0, d) for d in range(2)]
    u += [("PT", 1, j) for j in range(4)] + [("O", 1)]
    u += [("cT", 0, d) for d in range(2)]
    u += [("num", 0, j) for j in range(4)] + [("st", j) for j in range(4)]
    u += [("r", 1, d) for d in range(2)]
    u += [("cT", 1, d) for d in range(2)]
    u += [("num", 1, j) for j in range(4)] + [("ix", j) for j in range(4)]
    u += [("hT", t) for t in range(NT)]
    u += [("mix", p) for p in range(4)] + [("ss", 1), ("ss", 2)]
    u += [("up", c) for c in range(FC)]
    u += [("down", c) for c in range(KC)] + [("ss", 3)]
    return u


LAYER_SLOTS = [("win", j) for j in range(7)] + [("wout", j) for j in range(2)] + \
              [("up", j) for j in range(11)] + [("down", c, h) for c in range(4) for h in range(2)]
assert len(PAIR_SLOTS) % SLOTS == 0 and len(LAYER_SLOTS) % SLOTS == 0


def col(v):
    v = np.asarray(v)
    return np.moveaxis(v.reshape(*v.shape[:-1], -1, P), -1, 0).reshape(P, -1)


def lay_out(i):
    i = {k: np.asarray(v) for k, v in i.items()}
    rows = lambda v: np.broadcast_to(v.reshape(1, -1), (P, v.size))
    two = lambda v: np.concatenate([v, v]).reshape(P, 1)
    rel = np.zeros((P, HEADS), np.float32)
    rel[:BUCKETS] = i["rel_bias"]
    params = np.concatenate(
        [col(i["c"][0]), col(i["norm_mix"][0]), col(i["norm_ffn"][0]), col(i["b_ada"][0]),
         i["conv_w"][0].reshape(4, NX, P).transpose(2, 1, 0).reshape(P, -1), col(i["conv_b"][0]),
         col(i["kv_norm"][0]), two(i["q_norm"][0]), two(i["k_norm"][0]), two(i["idx_k_ln_w"][0]),
         two(i["idx_k_ln_b"][0]), col(i["ssm_norm"][0]), rows(i["dt_bias"][0]), rows(i["a_log"][0]),
         rows(i["d_skip"][0]), rows(i["b_router"][0]), rel], axis=1)
    params2 = np.stack([np.concatenate(
        [col(i["mix_pre_g_2"][l]), col(i["mix_post_g_2"][l]), col(i["ffn_pre_g_2"][l]), col(i["ffn_post_g_2"][l]),
         i["mlstm_conv_w_2"][l].reshape(5, 8, P).transpose(2, 1, 0).reshape(P, -1), col(i["mlstm_conv_b_2"][l]),
         col(i["mlstm_head_g_2"][l]), i["ffn_conv_w_2"][l].reshape(3, 2 * FC, P).transpose(2, 1, 0).reshape(P, -1),
         col(i["ffn_conv_b_2"][l]), rows(i["mlstm_gate_b_2"][l])], axis=1) for l in range(LAYERS)])
    return {
        "xT": np.ascontiguousarray(i["x"][0].reshape(L, KC, P).transpose(2, 1, 0)),
        "consts": constants(), "params": np.ascontiguousarray(params), "params2": np.ascontiguousarray(params2),
        "w_ada": i["w_ada"][0], "w_in": i["w_in"][0], "w_kv_up": i["w_kv_up"][0], "w_attn_o": i["w_attn_o"][0],
        "w_ssm_o": i["w_ssm_o"][0], "w_out": i["w_out"][0], "w_router": i["w_router"][0], "w_gu": i["w_gu"][0],
        "b_gu": i["b_gu"][0], "w_dn": i["w_dn"][0], "b_dn": i["b_dn"][0],
        "w_in_2": i["w_in_2"], "w_out_2": i["w_out_2"], "w_up_2": i["w_up_2"], "w_down_2": i["w_down_2"],
    }


INPUTS = ["xT", "consts", "params", "params2", "w_ada", "w_in", "w_kv_up", "w_attn_o", "w_ssm_o", "w_out", "w_router",
          "w_gu", "b_gu", "w_dn", "b_dn", "w_in_2", "w_out_2", "w_up_2", "w_down_2"]



class Arena:

    def __init__(self, ap, at=0):
        self.ap, self.at = ap, at

    def take(self, *dims):
        n = int(np.prod(dims))
        assert self.at + n <= self.ap.shape[1], (self.at, n, self.ap.shape)
        v = self.ap[:, self.at:self.at + n]
        self.at += n
        if len(dims) == 2:
            v = v.rearrange("p (a b) -> p a b", a=dims[0])
        if len(dims) == 3:
            v = v.rearrange("p (a b c) -> p a b c", a=dims[0], b=dims[1])
        return v


def matmul(pe, out, lhsT, rhs, first=True, last=True, **kw):
    return pe.matmul(out, lhsT, rhs, start=first, stop=last, **kw)


def rows(ap, n):
    return ap.unsqueeze(2).to_broadcast([ap.shape[0], ap.shape[1], n])


def across(ap, n):
    return ap.unsqueeze(1).to_broadcast([ap.shape[0], n, ap.shape[1]])


class Memory:

    def __init__(self, nc, ctx):
        sb = lambda name, n: ctx.enter_context(nc.sbuf_tensor(name, [P, n], F32))
        self.ring = sb("ring", SLOTS * SLOT)
        self.xT = sb("residual", KC * L)[:, :].rearrange("p (k t) -> p k t", k=KC)
        self.h = sb("normed", KC * L)[:, :].rearrange("p (k t) -> p k t", k=KC)
        self.consts, self.params = sb("consts_sb", CONSTS.n), sb("params_sb", PARAMS.n)
        self.mod, self.small, self.route = sb("mod_sb", 48), sb("small", 1024), sb("route", 512)
        self.flag = ctx.enter_context(nc.sbuf_tensor("flag", [P, 1], I32))
        self.work = sb("work", WORK)
        self.psum = ctx.enter_context(nc.psum_tensor("psum", [P, BANKS, 512], F32))

    def K(self, name, rows=P):
        return CONSTS.of(self.consts, name, rows)

    def prm(self, name, rows=P):
        return PARAMS.of(self.params, name, rows)

    def slot(self, i, *dims):
        n = int(np.prod(dims))
        v = self.ring[:, i * SLOT:i * SLOT + n]
        return v.rearrange("p (a b) -> p a b", a=dims[0])


WORK = 26800


PAIRS_OF_HEADS = (0, 1, 4, 5)


class Experts:

    def __init__(self, mem, sem, tag):
        self.picked = sem("picked" + tag)
        self.rows_ready = sem("rows_ready" + tag)
        self.clipped = sem("clipped" + tag)
        self.sig_ready = sem("sig_ready" + tag)
        self.act_ready = sem("act_ready" + tag)
        self.bias_in = sem("bgu_in" + tag)
        self.down_half = sem("down_half" + tag)
        self.zeroed = sem("zeroed" + tag)
        self.moved = sem("moved" + tag)
        self.step = sem("experts_step" + tag)
        self.mem = mem
        R = Arena(mem.route)
        self.lr, self.mask, self.tm, self.rank, self.ex = (R.take(NT, E) for _ in range(5))
        self.place, self.gate = R.take(NT, E + 2), R.take(NT, E + 2)
        self.flag = mem.flag[:, :]
        A = Arena(mem.work)
        self.h_tok = A.take(NT, D)
        self.y_sum = A.take(KC, L)
        self.hgT, self.actT = A.take(KC, P), A.take(KC, P)
        self.g, self.u = A.take(2, 512), A.take(2, 512)
        self.act, self.out = A.take(2, 512), A.take(2, 512)
        self.one_hot, self.weighted = A.take(NT, P), A.take(NT, P)
        self.wT = A.take(1, L)[:, 0]
        self.gateT = A.take(1, L)[:, 0]
        self.b_dn, self.b_gu = A.take(1, D)[:, 0], A.take(1, 2 * DE)[:, 0]

    def load_weights(self, sp, io, S, B, slot, p, it):
        before = lambda *name: (B.ready(*name, it=it)[0], B.ready(*name, it=it)[1] - B.per[B.no(name)])
        used = [(self.down_half, it + 1), before("dn", 1), B.ready("g", 0, it=it), B.ready("u", 0, it=it),
                B.ready("g", 1, it=it), B.ready("u", 1, it=it)]
        for i, name in enumerate(PAIR_SLOTS):
            kind, half, e = name
            if e == 0:
                sp.wait_ge(*used[i // 2])
            if kind == "wd":
                src = io["w_dn"][bass.ds(2 * p + e, 1), half * 512:half * 512 + 512, :]
                dst = slot(S.no(name), 4, 1024)
            else:
                c = half * 512 + (DE if kind == "wu" else 0)
                src = io["w_gu"][bass.ds(2 * p + e, 1), :, c:c + 512]
                dst = slot(S.no(name), KC, 512)
            sp.dma_start(dst, src.rearrange("a (k p) n -> p (a k) n", p=P)).then_inc(*S.fills(*name))

    def load_biases(self, pool, io, B, p, it):
        full, n = B.ready("u", 1, it=it)
        pool.wait_ge(full, n - B.per[B.no(("u", 1))])
        pool.dma_start(self.b_gu[0:2, :], io["b_gu"][bass.ds(2 * p, 2), :]).then_inc(self.bias_in, 16)

    def more_rounds(self, eng):
        return eng.value_load(self.flag[0:1, 0:1], min_val=0, max_val=1) > 0

    def pick(self, dve, e2, B=None, it=0):
        if B is not None:
            dve.wait_ge(*B.ready("sT", it=it))
        for t in range(NT):
            for e in range(2):
                c = slice(e * CAP, (e + 1) * CAP)
                one = lambda v: v[:, t, bass.ds(2 * e2 + e, 1)]
                dve.tensor_scalar(self.one_hot[:, t, c], self.mem.K("slot_no"), one(self.place), None, ALU.is_equal)
                ins = dve.tensor_scalar(self.weighted[:, t, c], self.mem.K("slot_no"), one(self.place), one(self.gate),
                                        ALU.is_equal, ALU.mult)
        ins.then_inc(self.picked, 1)

    def gather(self, pe, B, psum, it):
        pe.wait_ge(self.picked, it + 2)
        it = 0 if isinstance(it, int) and it < 0 else it
        for j in range(2):
            pe.wait_ge(*B.empty("hg", j, it=it))
            for i in range(4):
                k = 4 * j + i
                for t in range(NT):
                    ins = matmul(pe, psum[:, B.no(("hg", j)), i * P:(i + 1) * P], self.h_tok[:, t, k * P:(k + 1) * P],
                                 self.one_hot[:, t], t == 0, t == NT - 1)
            ins.then_inc(*B.fills("hg", j))

    def take_gathered(self, act, B, psum, it=0):
        for j in range(2):
            act.wait_ge(*B.ready("hg", j, it=it))
            act.activation(self.hgT[:, 4 * j:4 * j + 4], psum[:, B.no(("hg", j))].rearrange("p (a b) -> p a b", a=4), ACT.Copy)\
               .then_inc(*B.frees("hg", j))
            act.wait_ge(*B.released("hg", j, it=it))
        act.nop().then_inc(self.rows_ready, 1)

    def products(self, pe, mem, B, S, it):
        psum, K = mem.psum, mem.K
        pe.wait_ge(self.rows_ready, it + 1)
        pe.wait_ge(self.bias_in, it * 16 + 16)
        for half in range(2):
            for i, name in enumerate((("g", half), ("u", half))):
                b = psum[:, B.no(name)]
                pe.wait_ge(*B.empty(*name, it=it))
                pe.matmul(b, K("pair_row", 2), self.b_gu[0:2, i * DE + half * 512:i * DE + half * 512 + 512],
                          start=True, stop=False, skip_group_check=True)
                ws = []
                for e in range(2):
                    s = (("wg", "wu")[i], half, e)
                    pe.wait_ge(*S.ready(*s, it=it))
                    ws.append(mem.slot(S.no(s), KC, 512))
                for k in range(KC):
                    for e in range(2):
                        r = slice(e * CAP, (e + 1) * CAP)
                        ins = pe.matmul(b[r], self.hgT[:, k, r], ws[e][:, k], start=False, stop=k == KC - 1,
                                        skip_group_check=True)
                ins.then_inc(*B.fills(*name))
        pe.wait_ge(*B.empty("sT", it=it))
        for t in range(NT):
            ins = pe.transpose(psum[:, B.no(("sT",)), t * P:(t + 1) * P], self.weighted[:, t], K("ident"))
        ins.then_inc(*B.fills("sT"))
        for dh in range(2):
            pe.wait_ge(*B.empty("dn", dh, it=it))
        for half in range(2):
            pe.wait_ge(self.act_ready, it * 2 + half + 1)
            pe.wait_ge(*B.empty("aT", half, it=it))
            for i in range(4):
                ins = pe.transpose(psum[:, B.no(("aT", half)), i * P:(i + 1) * P], self.act[:, half, i * P:(i + 1) * P], K("ident"))
            ins.then_inc(*B.fills("aT", half))
            pe.wait_ge(*B.released("aT", half, it=it))
            ws = []
            for e in range(2):
                pe.wait_ge(*S.ready("wd", half, e, it=it))
                ws.append(mem.slot(S.no(("wd", half, e)), 4, 1024))
            for k in range(4):
                for dh in range(2):
                    for e in range(2):
                        r = slice(e * CAP, (e + 1) * CAP)
                        ins = pe.matmul(psum[r, B.no(("dn", dh))], self.actT[:, 4 * half + k, r], ws[e][:, k, dh * 512:dh * 512 + 512],
                                        start=half == 0 and k == 0, stop=half == 1 and k == 3, skip_group_check=True)
                    if half == 1 and k == 3:
                        ins.then_inc(*B.fills("dn", dh))
            if half == 0:
                ins.then_inc(self.down_half, 1)

    def act_part(self, act, B, psum, it):
        for half in range(2):
            act.wait_ge(self.clipped, it * 2 + half + 1)
            act.activation(self.u[:, half], self.g[:, half], ACT.Sigmoid, scale=ALPHA).then_inc(self.sig_ready, 1)
        act.wait_ge(*B.ready("sT", it=it))
        act.activation(self.wT, psum[:, B.no(("sT",)), 0:L], ACT.Copy).then_inc(*B.frees("sT"))
        for half in range(2):
            act.wait_ge(*B.ready("aT", half, it=it))
            act.activation(self.actT[:, 4 * half:4 * half + 4], psum[:, B.no(("aT", half))].rearrange("p (a b) -> p a b", a=4),
                           ACT.Copy).then_inc(*B.frees("aT", half))
        for dh in range(2):
            act.wait_ge(*B.ready("dn", dh, it=it))
            act.activation(self.out[:, dh], psum[:, B.no(("dn", dh))], ACT.Copy).then_inc(*B.frees("dn", dh))

    def combine(self, pe, B, psum, it):
        pe.wait_ge(*B.released("dn", 1, it=it))
        pe.wait_ge(*B.released("dn", 0, it=it))
        pe.wait_ge(*B.released("sT", it=it))
        for p in range(4):
            pe.wait_ge(*B.empty("y", p, it=it))
            for i in range(2):
                k = 2 * p + i
                ins = matmul(pe, psum[:, B.no(("y", p)), i * L:(i + 1) * L],
                             self.out[:, k // 4, (k % 4) * P:(k % 4 + 1) * P], self.wT)
            ins.then_inc(*B.fills("y", p))

    def glu(self, dve, B, psum, it):
        for half in range(2):
            g, u, act = self.g[:, half], self.u[:, half], self.act[:, half]
            dve.wait_ge(*B.ready("g", half, it=it))
            dve.tensor_scalar(g, psum[:, B.no(("g", half))], LIMIT, None, ALU.min).then_inc(*B.frees("g", half))
            dve.wait_ge(*B.released("g", half, it=it))
            dve.nop().then_inc(self.clipped, 1)
            dve.wait_ge(*B.ready("u", half, it=it))
            dve.tensor_scalar(act, psum[:, B.no(("u", half))], LIMIT, -LIMIT, ALU.min, ALU.max).then_inc(*B.frees("u", half))
            dve.wait_ge(self.sig_ready, it * 2 + half + 1)
            dve.tensor_tensor(g, g, u, ALU.mult).then_inc(self.step, 1)
            dve.wait_ge(*B.released("u", half, it=it))
            dve.wait_ge(self.step, it * 2 + half + 1)
            dve.scalar_tensor_tensor(out=act, in0=act, scalar=1.0, in1=g, op0=ALU.add, op1=ALU.mult)\
               .then_inc(self.act_ready, 1)

    def add_up(self, dve, B, psum, y_sum, it):
        for p in range(4):
            dve.wait_ge(*B.ready("y", p, it=it))
            v = y_sum[:, 2 * p:2 * p + 2]
            dve.tensor_tensor(v, v, psum[:, B.no(("y", p))].rearrange("p (a b) -> p a b", a=2), ALU.add)\
               .then_inc(*B.frees("y", p))
            if p == 3:
                dve.wait_ge(*B.released("y", p, it=it))


def first_block(nc, ctx, io, mem):
    sem = lambda n: ctx.enter_context(nc.semaphore(n))
    xT, h, psum, mod = mem.xT, mem.h, mem.psum, mem.mod
    K, prm, slot = mem.K, mem.prm, mem.slot
    line = nc.dram_tensor("bias_line", [HEADS, P, 384], F32, kind="Internal").ap()

    bank_full = [sem(f"bank_full{b}") for b in range(BANKS)]
    bank_free = [sem(f"bank_free{b}") for b in range(BANKS)]
    slot_full = [sem(f"slot_full{b}") for b in range(SLOTS)]
    B = Uses(bank_full, bank_free, front_banks())
    S = Uses(slot_full, slot_full, front_slots(), inc=16)
    BP = Uses(bank_full, bank_free, PAIR_BANKS, base=B.after())
    SP = Uses(slot_full, slot_full, PAIR_SLOTS, inc=16, base=S.after())

    small_in = sem("small_in")
    bdn_in = sem("bdn_in")
    act_step, dve_step, pool_step = sem("act_step"), sem("dve_step"), sem("pool_step")
    cond_ready = sem("cond_ready")
    ada_sum = sem("ada_sum")
    ada_sum_pool = sem("ada_sum_pool")
    mod_ready = sem("mod_ready")
    sq_ready = sem("sq_ready")
    var_ready = sem("var_ready")
    rstd_ready = sem("rstd_ready")
    scaled_ready = sem("scaled_ready")
    h_ready = sem("h_ready")
    tok_ready = sem("tok_ready")
    line_ready, line_out, bias_in = sem("line_ready"), sem("line_out"), sem("bias_in")
    relu_ready, relu_used = sem("relu_ready"), sem("relu_used")
    logits_ready, exp_ready, probs_ready = sem("logits_ready"), sem("exp_ready"), sem("probs_ready")
    conv_ready, silu_ready = sem("conv_ready"), sem("silu_ready")
    dt_abs, dt_log, dta_ready = sem("dt_abs"), sem("dt_log"), sem("dta_ready")
    acum_ready, decay_exp, xdt_ready = sem("acum_ready"), sem("decay_exp"), sem("xdt_ready")
    seg_ready, seg_exp, w_ready = sem("seg_ready"), sem("seg_exp"), sem("w_ready")
    y_ready = sem("y_ready")
    mixed_ready, x1_ready = sem("mixed_ready"), sem("x1_ready")
    route_ready, route_exp, mask_ready, gates_ready = (sem(n) for n in ("route_ready", "route_exp", "mask_ready", "gates_ready"))
    X = Experts(mem, sem, "")
    y_sum = X.y_sum

    A = Arena(mem.work)
    xbc = A.take(NX, L + 3)
    xc = A.take(NX, L)
    z = A.take(NT, SI)
    sig = A.take(2 * KC, L)
    attnT = A.take(4, L)
    acc = A.take(2, 512)
    w_dt = A.take(KC, SH)
    w_r = A.take(KC, E)
    pool_tmp = A.take(512)
    at = A.at
    qkt = A.take(2, NT, AW)
    bias = qkt.rearrange("p a t n -> p (a t n)").rearrange("p (h s) -> p h s", h=HEADS)
    q_tok, k_tok = qkt[:, 0], qkt[:, 1]
    v_tok = A.take(NT, AW)
    qT, kT, qiT = A.take(4, L), A.take(4, L), A.take(4, L)
    kiT = A.take(1, L)[:, 0]
    lg_at = A.at
    lg = A.take(HEADS, L)
    keep, score = A.take(NT, L), A.take(NT, L)
    pt_at = A.at
    pt = A.take(16, P)
    A2 = Arena(mem.work, lg_at)
    kvl, ki2, kvT, kw = A2.take(NT, 256), A2.take(NT, P), A2.take(2, L), A2.take(NT, 72)
    tmp = Arena(mem.work, pt_at).take(2, 512)
    relu = Arena(mem.work, pt_at).take(2, 2, L)
    top = Arena(mem.work, pt_at + 1024).take(4, L)
    A3 = Arena(mem.work, at)
    xs, xdt, seg = A3.take(NT, SI), A3.take(NT, SI), A3.take(SH, P)
    yT = A3.take(KC, L)
    Bt, cbT, state, xdec = A3.take(SG, P), A3.take(NT, SG, P), A3.take(SG, 512), A3.take(1, SI)[:, 0]
    y_tmp = xdec
    y_tok = Arena(mem.work).take(NT, SI)
    mixed = z.rearrange("p t n -> p (t n)").rearrange("p (k n) -> p k n", k=KC)
    line_sb = attnT.rearrange("p a b -> p (a b)")[0:HEADS, 0:384]
    SM = Arena(mem.small)
    cond, st, rs = SM.take(KC), SM.take(64), SM.take(64)
    a1, a2 = SM.take(KC), SM.take(KC)
    m8, cnt = SM.take(NT, 8), SM.take(8)
    wi = SM.take(NT, 8)
    mx, sm = SM.take(8), SM.take(8)
    ea = SM.take(SH)
    dtr, dtv, dt, dta, acum, nac, alast, dec, eac = (SM.take(NT, SH) for _ in range(9))
    rstd = SM.take(L)

    ident, ones = K("ident"), K("ones")[:, 0:P]

    def kpm(ap):
        return ap.rearrange("(k p) n -> p k n", p=P)

    block = ctx.enter_context(nc.Block())

    @block.sync
    def _(sp):
        for dst, src in ((mem.params[:, :], io["params"]), (xT, io["xT"]), (mem.consts[:, :], io["consts"]),
                         (w_dt, kpm(io["w_in"][:, C_DT:C_DT + SH])), (w_r, kpm(io["w_router"]))):
            sp.dma_start(dst, src).then_inc(small_in, 16)

        order = front_slots()

        def slot_used(name):
            kind, j = name[0], name[-1]
            if kind == "ada":
                return (ada_sum, j + 1) if j < 4 else (ada_sum_pool, j - 3)
            return B.ready(*{"win": WIN_LAST[j] if kind == "win" else None, "wkv": ("kv_up", 1, 1), "wo": ("ya", 3),
                             "gate": ("ga", 1 + 2 * j) if kind == "gate" else None,
                             "wso": ("ys", 1 + 2 * j) if kind == "wso" else None,
                             "wout": ("x1", 1 + 2 * j) if kind == "wout" else None}[kind])

        def load(src, *name):
            if order.index(name) >= SLOTS:
                sp.wait_ge(*slot_used(order[order.index(name) - SLOTS]))
            k, n = src.shape[0] // P, src.shape[1]
            sp.dma_start(slot(S.no(name), k, n), kpm(src)).then_inc(*S.fills(*name))

        win = [(C_Q, 512), (C_KV, 512), (C_QI + 256, 328)] + [(C_XBC + 512 * j, 512) for j in range(3)] + \
              [(C_Z + 512 * j, 512) for j in range(2)]
        for name in front_slots():
            kind, j = name[0], name[-1]
            if kind == "ada":
                load(io["w_ada"][:, 512 * j:512 * j + 512], *name)
            elif kind == "win":
                load(io["w_in"][:, win[j][0]:win[j][0] + win[j][1]], *name)
            elif kind == "wkv":
                load(io["w_kv_up"], *name)
            elif kind == "gate":
                load(io["w_in"][:, C_GATE + 512 * j:C_GATE + 512 * j + 512], *name)
            elif kind == "wo":
                load(io["w_attn_o"], *name)
            elif kind == "wso":
                load(io["w_ssm_o"][:, 512 * j:512 * j + 512], *name)
            elif kind == "wout":
                load(io["w_out"][:, 512 * j:512 * j + 512], *name)
        sp.wait_ge(*slot_used(("ada", 11)))
        sp.wait_ge(*slot_used(("wout", 1)))
        with sp.Fori(0, PAIRS) as p:
            X.load_weights(sp, io, SP, BP, slot, p, p)
        with sp.If(X.more_rounds(sp)):
            with sp.Fori(1, ROUNDS) as r:
                with sp.Fori(0, PAIRS) as p:
                    X.load_weights(sp, io, SP, BP, slot, p, r * PAIRS + p)

    @block.gpsimd
    def _(pool):
        step = Steps(pool, pool_step)
        pool.memset(xbc[:, :, 0:3], 0.0).then_inc(X.zeroed, 1)
        pool.wait_ge(line_ready, 1)
        pool.dma_start(line, line_sb.unsqueeze(1).to_broadcast([HEADS, P, 384])).then_inc(line_out, 16)
        pool.wait_ge(line_out, 16)
        pool.wait_ge(*B.ready("kT", 1))
        toeplitz = bass.AP(tensor=line.tensor, offset=P - 1, ap=[[383, P], [384 * P, HEADS], [1, L]])
        pool.dma_start(bias, toeplitz).then_inc(bias_in, 16)
        pool.wait_ge(cond_ready, 1)
        for j in range(4, 12):
            pool.wait_ge(*S.ready("ada", j))
            if j >= 6:
                pool.wait_ge(*B.ready("m", j - 2))
            w, a, t = slot(S.no(("ada", j)), KC, 512), acc[:, j % 2], pool_tmp
            step(pool.tensor_scalar(a, w[:, 0], cond[:, 0:1], None, ALU.mult))
            for k in range(1, KC):
                ins = pool.tensor_scalar(t, w[:, k], cond[:, k:k + 1], None, ALU.mult)
                step(ins)
                ins = pool.tensor_tensor(a, a, t, ALU.add)
                if k < KC - 1:
                    step(ins)
            ins.then_inc(ada_sum_pool, 1)
            pool.wait_ge(ada_sum_pool, j - 3)
        pool.wait_ge(gates_ready, 1)
        with pool.Fori(0, PAIRS) as p:
            X.load_biases(pool, io, BP, p, p)
        with pool.If(X.more_rounds(pool)):
            with pool.Fori(1, ROUNDS) as r:
                with pool.Fori(0, PAIRS) as p:
                    X.load_biases(pool, io, BP, p, r * PAIRS + p)

    @block.tensor
    def _(pe):
        pe.wait_ge(small_in, 80)

        def bank(*name):
            return psum[:, B.no(name)]

        def sum_mod(j):
            pe.wait_ge(*((ada_sum, j + 1) if j < 4 else (ada_sum_pool, j - 3)))
            pe.wait_ge(*B.empty("m", j))
            for i in range(4):
                ins = matmul(pe, bank("m", j)[:, i:i + 1], acc[:, j % 2, i * P:(i + 1) * P], ones[:, 0:1])
            ins.then_inc(*B.fills("m", j))

        def sum_squares(n, sq):
            pe.wait_ge(sq_ready, n)
            pe.wait_ge(*B.empty("ss", n))
            for k in range(KC):
                ins = matmul(pe, bank("ss", n)[:, 0:L], ones, sq[:, k], k == 0, k == KC - 1)
            ins.then_inc(*B.fills("ss", n))

        def by_token(name, w, c0, n, lhs=h, kc=KC):
            for t in range(NT):
                pe.wait_ge(*B.empty(*name, t))
                for k in range(kc):
                    ins = matmul(pe, bank(*name, t)[:, 0:n], lhs[:, k, t * P:(t + 1) * P], w[:, k, c0:c0 + n],
                                 k == 0, k == kc - 1)
                ins.then_inc(*B.fills(*name, t))
            return ins

        def by_feature(name, w, c0, rhs=h, kc=KC):
            pe.wait_ge(*B.empty(*name))
            for i in range(2):
                for k in range(kc):
                    ins = matmul(pe, bank(*name)[:, i * L:(i + 1) * L], w[:, k, c0 + i * P:c0 + (i + 1) * P], rhs[:, k],
                                 k == 0, k == kc - 1)
            ins.then_inc(*B.fills(*name))

        def wait_slot(*name):
            pe.wait_ge(*S.ready(*name))
            return slot(S.no(name), KC, 512)

        def transposes(name, blocks):
            pe.wait_ge(*B.empty(*name))
            for i, b in enumerate(blocks):
                ins = pe.transpose(bank(*name)[0:b.shape[1], i * P:(i + 1) * P], b, ident)
            ins.then_inc(*B.fills(*name))

        for j in range(4):
            sum_mod(j)
        sum_squares(1, sig[:, 0:KC])
        pe.wait_ge(h_ready, KC)
        by_token(("q",), wait_slot("win", 0), 0, 512)
        w = wait_slot("win", 1)
        by_token(("kv",), w, 0, 256)
        by_feature(("qi", 0), w, 256)
        pe.wait_ge(*S.ready("win", 2))
        w = slot(S.no(("win", 2)), KC, 328)
        by_feature(("qi", 1), w, 0)
        by_token(("kw",), w, 256, 72)
        for j in range(3):
            w = wait_slot("win", 3 + j)
            by_feature(("xbc", 2 * j), w, 0)
            by_feature(("xbc", 2 * j + 1), w, 256)
        pe.wait_ge(*B.empty("dt"))
        for t in range(NT):
            for k in range(KC):
                ins = matmul(pe, bank("dt")[:, t * SH:(t + 1) * SH], h[:, k, t * P:(t + 1) * P], w_dt[:, k], k == 0, k == KC - 1)
        ins.then_inc(*B.fills("dt"))
        pe.wait_ge(*B.empty("bvec"))
        matmul(pe, bank("bvec")[0:HEADS, 0:384], prm("rel_bias", BUCKETS), K("bucket", BUCKETS)).then_inc(*B.fills("bvec"))
        pe.wait_ge(tok_ready, 1)
        transposes(("kvT",), [kvl[:, t, c * P:(c + 1) * P] for c in range(2) for t in range(NT)])
        for t in range(NT):
            transposes(("qT", t), [q_tok[:, t, c * P:(c + 1) * P] for c in range(4)])
        transposes(("kiT",), [ki2[:, t] for t in range(NT)])
        for j in range(2):
            by_token(("z", j), wait_slot("win", 6 + j), 0, 512)
        pe.wait_ge(*S.ready("wkv"))
        w = slot(S.no(("wkv",)), 2, 1024)
        pe.wait_ge(*B.released("kvT"))
        for j in range(2):
            by_token(("kv_up", j), w, 512 * j, 512, kvT, 2)
        pe.wait_ge(*B.released("kiT"))
        pe.wait_ge(*B.released("qi", 1))
        for t in range(NT):
            for g, h0 in enumerate(PAIRS_OF_HEADS):
                pe.wait_ge(*B.empty("dots", t, g))
                for i in range(2):
                    hd = h0 + 2 * i
                    r = slice(64 * (hd % 2), 64 * (hd % 2) + 64)
                    ins = matmul(pe, bank("dots", t, g)[:, i * L:(i + 1) * L], qiT[r, hd // 2, t * P:(t + 1) * P], kiT[r, :])
                ins.then_inc(*B.fills("dots", t, g))
        pe.wait_ge(tok_ready, 2)
        for t in range(NT):
            transposes(("kT", t), [k_tok[:, t, c * P:(c + 1) * P] for c in range(4)])
        for j in range(2):
            w = wait_slot("gate", j)
            by_feature(("ga", 2 * j), w, 0)
            by_feature(("ga", 2 * j + 1), w, 256)
            sum_mod(4 + j)
        pe.wait_ge(*B.released("kT", 1))
        for t in range(NT):
            nk = (t + 1) * P
            for g, h0 in enumerate(PAIRS_OF_HEADS):
                pe.wait_ge(*B.empty("S", t, g))
                for i in range(2):
                    hd = h0 + 2 * i
                    r = slice(64 * (hd % 2), 64 * (hd % 2) + 64)
                    ins = matmul(pe, bank("S", t, g)[:, i * nk:(i + 1) * nk], qT[r, hd // 2, t * P:(t + 1) * P], kT[r, hd // 2, 0:nk])
                ins.then_inc(*B.fills("S", t, g))
            w = wait_slot("gate", 2 + t)
            by_feature(("ga", 4 + 2 * t), w, 0)
            by_feature(("ga", 5 + 2 * t), w, 256)
            sum_mod(6 + t)
            pe.wait_ge(probs_ready, t + 1)
            blocks = [(hd, s) for hd in range(HEADS) for s in range(t + 1)]
            for j in range(2 * (t + 1)):
                transposes(("PT", t, j), [lg[:, hd, s * P:(s + 1) * P] for hd, s in blocks[4 * j:4 * j + 4]])
            pe.wait_ge(*B.empty("O", t))
            pe.wait_ge(*B.released("PT", t, 2 * t + 1))
            for hd in range(HEADS):
                r = slice(64 * (hd % 2), 64 * (hd % 2) + 64)
                for s in range(t + 1):
                    ins = matmul(pe, bank("O", t)[r, (hd // 2) * P:(hd // 2 + 1) * P], v_tok[:, s, hd * HD:(hd + 1) * HD],
                                 pt[:, blocks.index((hd, s))], s == 0, s == t)
            ins.then_inc(*B.fills("O", t))
        sum_mod(8)
        for t in range(NT):
            for j in range(2):
                pe.wait_ge(silu_ready, 4 * j + 4)
                transposes(("xT", t, j), [xc[:, 4 * j + c, t * P:(t + 1) * P] for c in range(4)])
        pe.wait_ge(silu_ready, NX)
        transposes(("BT",), [xc[:, KC + g, 0:P] for g in range(SG)])
        pe.wait_ge(dta_ready, 1)
        pe.wait_ge(*B.empty("acum"))
        for c in range(NT):
            matmul(pe, bank("acum")[:, c * SH:(c + 1) * SH], K("tri_le"), dta[:, c])
            ins = matmul(pe, bank("acum")[:, (2 + c) * SH:(3 + c) * SH], ones, dta[:, c])
        ins.then_inc(*B.fills("acum"))
        sum_mod(9)
        for c in range(NT):
            pe.wait_ge(*B.empty("cb", c))
            for g in range(SG):
                ins = matmul(pe, bank("cb", c)[:, g * P:(g + 1) * P], xc[:, KC + g, c * P:(c + 1) * P],
                             xc[:, KC + SG + g, c * P:(c + 1) * P])
            ins.then_inc(*B.fills("cb", c))

        def cum_rows(c):
            for j in range(4):
                pe.wait_ge(*B.empty("row", c, j))
                for i in range(4):
                    hd = 4 * j + i
                    ins = matmul(pe, bank("row", c, j)[:, i * P:(i + 1) * P], acum[:, c, hd:hd + 1].to_broadcast([P, P]), ident)
                ins.then_inc(*B.fills("row", c, j))

        def intra(c):
            pe.wait_ge(w_ready, c + 1)
            for g in range(SG):
                pe.wait_ge(*B.empty("yi", c, g))
                for i in range(8):
                    hd = 8 * g + i
                    ins = matmul(pe, bank("yi", c, g)[:, i * 64:(i + 1) * 64], seg[:, hd], xdt[:, c, hd * 64:(hd + 1) * 64])
                ins.then_inc(*B.fills("yi", c, g))

        pe.wait_ge(acum_ready, 1)
        cum_rows(0)
        pe.wait_ge(xdt_ready, 1)
        pe.wait_ge(*B.released("BT"))
        for g in range(SG):
            pe.wait_ge(*B.empty("state", g))
            matmul(pe, bank("state", g), Bt[:, g], xdec[:, g * 512:(g + 1) * 512]).then_inc(*B.fills("state", g))
        intra(0)
        cum_rows(1)
        for g in range(SG):
            pe.wait_ge(*B.empty("yx", g))
            pe.wait_ge(*B.released("state", g))
            matmul(pe, bank("yx", g), xc[:, KC + SG + g, P:2 * P], state[:, g]).then_inc(*B.fills("yx", g))
        intra(1)
        for t in range(NT):
            pe.wait_ge(y_ready, t + 1)
            for j in range(2):
                transposes(("yT", t, j), [y_tok[:, t, (4 * j + c) * P:(4 * j + c + 1) * P] for c in range(4)])
        sum_mod(10)
        pe.wait_ge(*S.ready("wo"))
        pe.wait_ge(*B.released("O", 1))
        w = slot(S.no(("wo",)), 4, 1024)
        for p in range(4):
            by_feature(("ya", p), w, 256 * p, attnT, 4)
        pe.wait_ge(*B.released("yT", 1, 1))
        for j in range(2):
            w = wait_slot("wso", j)
            by_feature(("ys", 2 * j), w, 0, yT)
            by_feature(("ys", 2 * j + 1), w, 256, yT)
        sum_mod(11)
        pe.wait_ge(mixed_ready, 1)
        for j in range(2):
            w = wait_slot("wout", j)
            by_feature(("x1", 2 * j), w, 0, mixed)
            by_feature(("x1", 2 * j + 1), w, 256, mixed)
        sum_squares(2, sig[:, 0:KC])
        pe.wait_ge(h_ready, 2 * KC)
        for t in range(NT):
            for j in range(2):
                transposes(("tok", t, j), [h[:, 4 * j + c, t * P:(t + 1) * P] for c in range(4)])
        pe.wait_ge(*B.empty("rl"))
        for t in range(NT):
            for k in range(KC):
                ins = matmul(pe, bank("rl")[:, t * E:(t + 1) * E], h[:, k, t * P:(t + 1) * P], w_r[:, k], k == 0, k == KC - 1)
        ins.then_inc(*B.fills("rl"))
        pe.wait_ge(mask_ready, 1)
        pe.wait_ge(*B.empty("cum"))
        matmul(pe, bank("cum")[:, 0:E], K("tri_le"), X.mask[:, 0])
        matmul(pe, bank("cum")[:, E:2 * E], K("tri_le"), X.mask[:, 1], True, False)
        matmul(pe, bank("cum")[:, E:2 * E], ones, X.mask[:, 0], False, True)
        matmul(pe, bank("cum")[:, 2 * E:3 * E], ones, X.mask[:, 0], True, False)
        matmul(pe, bank("cum")[:, 2 * E:3 * E], ones, X.mask[:, 1], False, True).then_inc(*B.fills("cum"))
        pe.wait_ge(gates_ready, 1)
        transposes(("GT",), [X.gate[:, t, 0:E] for t in range(NT)])
        pe.wait_ge(*B.released("GT"))
        pe.wait_ge(bdn_in, 16)
        for p in range(4):
            pe.wait_ge(*B.empty("yb", p))
            for i in range(2):
                k = 2 * p + i
                ins = matmul(pe, bank("yb", p)[:, i * L:(i + 1) * L], X.b_dn[0:E, k * P:(k + 1) * P], X.gateT[0:E, :])
            ins.then_inc(*B.fills("yb", p))
        pe.wait_ge(*B.released("tok", 1, 1))
        X.gather(pe, B, psum, -1)
        pe.nop().then_inc(X.down_half, 1)
        with pe.Fori(0, PAIRS) as p:
            X.products(pe, mem, BP, SP, p)
            X.gather(pe, BP, psum, p)
            X.combine(pe, BP, psum, p)
        with pe.If(X.more_rounds(pe)):
            with pe.Fori(PAIRS, ROUNDS * PAIRS) as i:
                X.products(pe, mem, BP, SP, i)
                X.gather(pe, BP, psum, i)
                X.combine(pe, BP, psum, i)

    @block.scalar
    def _(act):
        step = Steps(act, act_step)
        act.wait_ge(small_in, 80)
        step(act.activation(ea, prm("a_log"), ACT.Exp))
        act.activation(cond, prm("c"), ACT.Silu).then_inc(cond_ready, 1)
        act.activation(sig[:, 0:KC], xT, ACT.Square).then_inc(sq_ready, 1)

        def take(out, in_, *name, func=ACT.Copy, **kw):
            act.wait_ge(*B.ready(*name))
            act.activation(out, in_, func, **kw).then_inc(*B.frees(*name))

        def bank(*name):
            return psum[:, B.no(name)]

        def two(v, n=2):
            return v.rearrange("p (a b) -> p a b", a=n)

        def root(n, out, in_):
            act.wait_ge(var_ready, n)
            act.activation(out, in_, ACT.Sqrt).then_inc(rstd_ready, 1)

        root(1, rstd, rstd)
        act.wait_ge(mod_ready, 1)
        for k in range(KC):
            act.wait_ge(scaled_ready, k + 1)
            act.activation(h[:, k], h[:, k], ACT.Identity, bias=mod[:, k:k + 1]).then_inc(h_ready, 1)
        for t in range(NT):
            take(q_tok[:, t], bank("q", t), "q", t)
        for t in range(NT):
            take(kvl[:, t], bank("kv", t)[:, 0:256], "kv", t)
        take(qiT[:, 0:2], two(bank("qi", 0)), "qi", 0)
        take(qiT[:, 2:4], two(bank("qi", 1)), "qi", 1)
        for t in range(NT):
            take(kw[:, t], bank("kw", t)[:, 0:72], "kw", t)
        act.wait_ge(X.zeroed, 1)
        for p in range(NX // 2):
            take(xbc[:, 2 * p:2 * p + 2, 3:], two(bank("xbc", p)), "xbc", p)
        take(dtr, two(bank("dt")[:, 0:2 * SH]), "dt")
        root(2, rs[:, 0:20], st[:, 0:20])
        for j in range(2):
            for t in range(NT):
                take(z[:, t, j * 512:(j + 1) * 512], bank("z", j, t), "z", j, t, func=ACT.Silu)
        for j, dst in enumerate((k_tok, v_tok)):
            for t in range(NT):
                take(dst[:, t], bank("kv_up", j, t), "kv_up", j, t)
        root(3, rs[:, 20:36], st[:, 20:36])
        for t in range(NT):
            for g in range(4):
                n = 4 * t + g
                act.wait_ge(*B.ready("dots", t, g))
                if n >= 2:
                    act.wait_ge(relu_used, n - 1)
                elif n == 0:
                    act.wait_ge(tok_ready, 2)
                act.activation(relu[:, n % 2], two(bank("dots", t, g)), ACT.Relu).then_inc(*B.frees("dots", t, g))
        act.wait_ge(dt_abs, 1)
        step(act.activation(dt, dt, ACT.Exp, scale=-1.0))
        act.activation(dt, dt, ACT.Ln, bias=1.0).then_inc(dt_log, 1)

        def gate(p):
            take(sig[:, 2 * p:2 * p + 2], two(bank("ga", p)), "ga", p, func=ACT.Sigmoid)

        for p in range(4):
            gate(p)
        for t in range(NT):
            nk = (t + 1) * P
            gate(4 + 2 * t)
            gate(5 + 2 * t)
            act.wait_ge(logits_ready, t + 1)
            act.activation(lg[:, :, 0:nk], lg[:, :, 0:nk], ACT.Exp).then_inc(exp_ready, 1)
            for j in range(2 * (t + 1)):
                take(pt[:, 4 * j:4 * j + 4], two(bank("PT", t, j), 4), "PT", t, j)
            take(attnT[:, :, t * P:(t + 1) * P], two(bank("O", t), 4), "O", t)
        for k in range(NX):
            act.wait_ge(conv_ready, k + 1)
            act.activation(xc[:, k], xc[:, k], ACT.Silu).then_inc(silu_ready, 1)
        for t in range(NT):
            for j in range(2):
                take(xs[:, t, j * 512:(j + 1) * 512], bank("xT", t, j), "xT", t, j)
        take(Bt, two(bank("BT")[:, 0:2 * P]), "BT")
        act.wait_ge(acum_ready, 1)
        step(act.activation(dec, dec, ACT.Exp))
        act.activation(eac, acum, ACT.Exp).then_inc(decay_exp, 1)
        for c in range(NT):
            take(cbT[:, c], two(bank("cb", c)[:, 0:2 * P]), "cb", c)
        act.wait_ge(seg_ready, 4)
        act.activation(seg, seg, ACT.Exp).then_inc(seg_exp, 1)
        for g in range(SG):
            take(state[:, g], bank("state", g), "state", g)
        act.wait_ge(seg_ready, 8)
        act.activation(seg, seg, ACT.Exp).then_inc(seg_exp, 1)
        root(4, rs[:, 0:2], st[:, 0:2])
        root(5, rs[:, 2:4], st[:, 2:4])
        for t in range(NT):
            for j in range(2):
                act.wait_ge(*B.ready("yT", t, j))
                for c in range(4):
                    k = 4 * j + c
                    ins = act.activation(yT[:, k, t * P:(t + 1) * P], bank("yT", t, j)[:, c * P:(c + 1) * P], ACT.Copy,
                                         scale=prm("ssm_norm")[:, k:k + 1])
                ins.then_inc(*B.frees("yT", t, j))
        act.wait_ge(x1_ready, 1)
        act.activation(sig[:, 0:KC], xT, ACT.Square).then_inc(sq_ready, 1)
        root(6, rstd, rstd)
        act.wait_ge(mod_ready, 2)
        for k in range(KC):
            act.wait_ge(scaled_ready, KC + k + 1)
            act.activation(h[:, k], h[:, k], ACT.Identity, bias=mod[:, 24 + k:25 + k]).then_inc(h_ready, 1)
        act.dma_start(X.b_dn[0:E, :], io["b_dn"]).then_inc(bdn_in, 16)
        for t in range(NT):
            for j in range(2):
                take(X.h_tok[:, t, j * 512:(j + 1) * 512], bank("tok", t, j), "tok", t, j)
        act.wait_ge(route_ready, 1)
        act.activation(X.ex, X.ex, ACT.Exp).then_inc(route_exp, 1)
        act.wait_ge(*B.ready("GT"))
        act.activation(X.gateT[0:E, :], bank("GT")[0:E, 0:L], ACT.Copy).then_inc(*B.frees("GT"))
        for p in range(4):
            take(y_sum[:, 2 * p:2 * p + 2], two(bank("yb", p)), "yb", p)
        X.take_gathered(act, B, psum)
        with act.Fori(0, PAIRS) as p:
            X.act_part(act, BP, psum, p)
            X.take_gathered(act, BP, psum, p)
        with act.If(X.more_rounds(act)):
            with act.Fori(PAIRS, ROUNDS * PAIRS) as i:
                X.act_part(act, BP, psum, i)
                X.take_gathered(act, BP, psum, i)

    @block.vector
    def _(dve):
        step = Steps(dve, dve_step)
        TS, TT, STT = dve.tensor_scalar, dve.tensor_tensor, dve.scalar_tensor_tensor

        def bank(*name):
            return psum[:, B.no(name)]

        def two(v, n=2):
            return v.rearrange("p (a b) -> p a b", a=n)

        def take(ins, *name):
            ins.then_inc(*B.frees(*name))
            dve.wait_ge(*B.released(*name))

        def signal(ins, sem, n):
            ins.then_inc(sem, 1)
            dve.wait_ge(sem, n)

        def take_mod(j):
            dve.wait_ge(*B.ready("m", j))
            take(TT(mod[:, 4 * j:4 * j + 4], bank("m", j)[:, 0:4], prm("b_ada")[:, 4 * j:4 * j + 4], ALU.add), "m", j)

        def inverse(ap, count):
            step(TS(ap, ap, 1.0 / count, EPS, ALU.mult, ALU.add))

        dve.wait_ge(small_in, 80)
        dve.wait_ge(cond_ready, 1)
        for j in range(4):
            dve.wait_ge(*S.ready("ada", j))
            if j >= 2:
                dve.wait_ge(*B.ready("m", j - 2))
            w, a = slot(S.no(("ada", j)), KC, 512), acc[:, j % 2]
            step(TS(a, w[:, 0], cond[:, 0:1], None, ALU.mult))
            for k in range(1, KC):
                ins = STT(out=a, in0=w[:, k], scalar=cond[:, k:k + 1], in1=a, op0=ALU.mult, op1=ALU.add)
                if k < KC - 1:
                    step(ins)
            signal(ins, ada_sum, j + 1)
            if j >= 1:
                take_mod(j - 1)
        take_mod(3)

        def scale_columns(a, norm, base):
            step(TS(a, mod[:, base:base + KC], 1.0, None, ALU.add))
            step(TT(a, a, norm, ALU.mult))

        def norm_input(n, a, first):
            dve.wait_ge(*B.ready("ss", n))
            take(TS(rstd, bank("ss", n)[:, 0:L], 1.0 / D, EPS, ALU.mult, ALU.add), "ss", n)
            signal(dve.reciprocal(rstd, rstd), var_ready, 1 if n == 1 else 6)
            dve.wait_ge(rstd_ready, 1 if n == 1 else 6)
            for k in range(KC):
                STT(out=h[:, k], in0=xT[:, k], scalar=a[:, k:k + 1], in1=rstd, op0=ALU.mult, op1=ALU.mult)\
                    .then_inc(scaled_ready, 1)

        scale_columns(a1, prm("norm_mix"), 8)
        dve.nop().then_inc(mod_ready, 1)
        norm_input(1, a1, 0)

        for t in range(NT):
            dve.wait_ge(*B.released("q", t))
            step(TT(tmp[:, 0], q_tok[:, t], q_tok[:, t], ALU.mult))
            step(dve.tensor_reduce(st[:, 8 * t:8 * t + 8], two(tmp[:, 0], 8), AX.X, ALU.add))
        for t in range(NT):
            dve.wait_ge(*B.released("kv", t))
            step(TT(tmp[:, 0, 0:256], kvl[:, t], kvl[:, t], ALU.mult))
            step(dve.tensor_reduce(st[:, 16 + t:17 + t], tmp[:, 0, 0:256], AX.X, ALU.add))
        for t in range(NT):
            dve.wait_ge(*B.released("kw", t))
            step(dve.tensor_reduce(cnt[:, t:t + 1], kw[:, t, 0:64], AX.X, ALU.add))
            step(TS(cnt[:, t:t + 1], cnt[:, t:t + 1], -1.0 / 64, None, ALU.mult))
            step(TS(ki2[:, t, 0:64], kw[:, t, 0:64], cnt[:, t:t + 1], None, ALU.add))
            step(TT(tmp[:, 0, 0:64], ki2[:, t, 0:64], ki2[:, t, 0:64], ALU.mult))
            step(dve.tensor_reduce(st[:, 18 + t:19 + t], tmp[:, 0, 0:64], AX.X, ALU.add))
            step(TS(wi[:, t], kw[:, t, 64:72], HEADS ** -0.5 * HD ** -0.5, None, ALU.mult))
        inverse(st[:, 0:16], HD)
        inverse(st[:, 16:18], 256)
        inverse(st[:, 18:20], 64)
        signal(dve.reciprocal(st[:, 0:20], st[:, 0:20]), var_ready, 2)
        dve.wait_ge(rstd_ready, 2)
        for t in range(NT):
            step(TT(two(q_tok[:, t], 8), two(q_tok[:, t], 8), rows(rs[:, 8 * t:8 * t + 8], HD), ALU.mult))
            step(TS(kvl[:, t], kvl[:, t], rs[:, 16 + t:17 + t], None, ALU.mult))
            step(TS(ki2[:, t, 64:], ki2[:, t, 0:64], rs[:, 18 + t:19 + t], None, ALU.mult))
            step(TS(ki2[:, t, 0:64], ki2[:, t, 0:64], rs[:, 18 + t:19 + t], None, ALU.mult))
        dve.nop().then_inc(tok_ready, 1)
        dve.wait_ge(*B.ready("bvec"))
        dve.tensor_copy(line_sb, bank("bvec")[0:HEADS, 0:384]).then_inc(*B.frees("bvec"))
        dve.wait_ge(*B.released("bvec"))
        dve.nop().then_inc(line_ready, 1)
        dve.wait_ge(*B.ready("kvT"))
        step(TS(kvT[:, 0], bank("kvT")[:, 0:L], prm("kv_norm")[:, 0:1], None, ALU.mult))
        take(TS(kvT[:, 1], bank("kvT")[:, L:2 * L], prm("kv_norm")[:, 1:2], None, ALU.mult), "kvT")
        for t in range(NT):
            dve.wait_ge(*B.ready("qT", t))
            take(TS(qT[:, :, t * P:(t + 1) * P], two(bank("qT", t), 4), prm("q_norm"), None, ALU.mult), "qT", t)
        dve.wait_ge(*B.ready("kiT"))
        take(TS(kiT, bank("kiT")[:, 0:L], prm("ln_w"), prm("ln_b"), ALU.mult, ALU.add), "kiT")
        dve.wait_ge(*B.released("dt"))
        step(TT(dtv, dtr, across(prm("dt_bias"), NT), ALU.add))
        signal(STT(out=dt, in0=dtv, scalar=-1.0, in1=dtv, op0=ALU.mult, op1=ALU.max), dt_abs, 1)
        for t in range(NT):
            dve.wait_ge(*B.released("kv_up", 0, t))
            step(TT(tmp[:, 1], k_tok[:, t], k_tok[:, t], ALU.mult))
            step(dve.tensor_reduce(st[:, 20 + 8 * t:28 + 8 * t], two(tmp[:, 1], 8), AX.X, ALU.add))
        inverse(st[:, 20:36], HD)
        signal(dve.reciprocal(st[:, 20:36], st[:, 20:36]), var_ready, 3)
        dve.wait_ge(rstd_ready, 3)
        for t in range(NT):
            step(TT(two(k_tok[:, t], 8), two(k_tok[:, t], 8), rows(rs[:, 20 + 8 * t:28 + 8 * t], HD), ALU.mult))
        dve.nop().then_inc(tok_ready, 1)

        def pick_top(scores, n, want, m8, gt, eq, rank, cnt):
            thr = m8[:, (want - 1) % 8:(want - 1) % 8 + 1]
            step(TS(gt, scores, thr, None, ALU.is_gt))
            step(TS(eq, scores, thr, None, ALU.is_equal))
            step(dve.tensor_reduce(cnt, gt, AX.X, ALU.add))
            step(TS(cnt, cnt, -1.0, float(want), ALU.mult, ALU.add))
            step(dve.tensor_tensor_scan(rank, K("ones")[:, 0:n], eq, 0.0, ALU.mult, ALU.add))
            step(STT(out=eq, in0=rank, scalar=cnt, in1=eq, op0=ALU.is_le, op1=ALU.mult))
            step(TT(gt, gt, eq, ALU.add))

        for t in range(NT):
            for g, h0 in enumerate(PAIRS_OF_HEADS):
                n = 4 * t + g
                dve.wait_ge(*B.released("dots", t, g))
                for i in range(2):
                    hd = h0 + 2 * i
                    if g == 0 and i == 0:
                        ins = TS(score[:, t], relu[:, n % 2, i], wi[:, t, hd:hd + 1], None, ALU.mult)
                    else:
                        ins = STT(out=score[:, t], in0=relu[:, n % 2, i], scalar=wi[:, t, hd:hd + 1], in1=score[:, t],
                                  op0=ALU.mult, op1=ALU.add)
                    if i == 0:
                        step(ins)
                    else:
                        signal(ins, relu_used, n + 1)
            causal = two(K("causal"))[:, t]
            step(TT(score[:, t], score[:, t], causal, ALU.add))
            step(dve.tensor_copy(top[:, 0], score[:, t]))
            for r in range(TOPK // 8):
                step(dve.max(m8[:, t], top[:, 0]))
                if r < TOPK // 8 - 1:
                    step(dve.match_replace(top[:, 0], m8[:, t], top[:, 0], 1.1 * FAR))
            pick_top(score[:, t], L, TOPK, m8[:, t], top[:, 1], top[:, 2], top[:, 3], cnt[:, t:t + 1])
            step(TS(keep[:, t], top[:, 1], -1.0, -NEG, ALU.add, ALU.mult))
            step(TT(keep[:, t], keep[:, t], causal, ALU.add))
        for t in range(NT):
            dve.wait_ge(*B.ready("kT", t))
            take(TS(kT[:, :, t * P:(t + 1) * P], two(bank("kT", t), 4), prm("k_norm"), None, ALU.mult), "kT", t)
        dve.wait_ge(dt_log, 1)
        step(TS(dtv, dtv, 0.0, None, ALU.max))
        step(TT(dt, dt, dtv, ALU.add))
        signal(STT(out=dta, in0=dt, scalar=-1.0, in1=across(ea, NT), op0=ALU.mult, op1=ALU.mult), dta_ready, 1)
        take_mod(4)
        take_mod(5)
        dve.wait_ge(bias_in, 16)
        for t in range(NT):
            nk = (t + 1) * P
            for g, h0 in enumerate(PAIRS_OF_HEADS):
                dve.wait_ge(*B.ready("S", t, g))
                take(STT(out=lg[:, h0:h0 + 3:2, 0:nk], in0=two(bank("S", t, g)[:, 0:2 * nk]), scalar=HD ** -0.5,
                         in1=bias[:, h0:h0 + 3:2, L - nk:], op0=ALU.mult, op1=ALU.add), "S", t, g)
            v = lg[:, :, 0:nk]
            step(TT(v, v, across(keep[:, t, 0:nk], HEADS), ALU.add))
            step(dve.tensor_reduce(mx, v, AX.X, ALU.max))
            signal(TT(v, v, rows(mx, nk), ALU.subtract), logits_ready, t + 1)
            take_mod(6 + t)
            dve.wait_ge(exp_ready, t + 1)
            step(dve.tensor_reduce(sm, v, AX.X, ALU.add))
            step(dve.reciprocal(sm, sm))
            signal(TT(v, v, rows(sm, nk), ALU.mult), probs_ready, t + 1)
            for k in range(6 * t, 6 * t + 6):
                cw = prm("conv_w")[:, 4 * k:4 * k + 4]
                dve.wait_ge(*B.released("xbc", k // 2))
                step(TS(xc[:, k], xbc[:, k, 0:L], cw[:, 0:1], prm("conv_b")[:, k:k + 1], ALU.mult, ALU.add))
                for j in range(1, 4):
                    ins = STT(out=xc[:, k], in0=xbc[:, k, j:j + L], scalar=cw[:, j:j + 1], in1=xc[:, k],
                              op0=ALU.mult, op1=ALU.add)
                    if j < 3:
                        step(ins)
                signal(ins, conv_ready, k + 1)
        take_mod(8)
        dve.wait_ge(*B.ready("acum"))
        step(dve.tensor_copy(acum, two(bank("acum")[:, 0:2 * SH])))
        take(dve.tensor_copy(alast, two(bank("acum")[:, 2 * SH:4 * SH])), "acum")
        step(TS(nac, acum, -1.0, None, ALU.mult))
        signal(TT(dec, alast, acum, ALU.subtract), acum_ready, 1)
        take_mod(9)

        def heads(v):
            return v.rearrange("p (h n) -> p h n", n=64)

        for t in range(NT):
            dve.wait_ge(*B.released("xT", t, 1))
            step(TT(heads(xdt[:, t]), heads(xs[:, t]), rows(dt[:, t], 64), ALU.mult))
        dve.wait_ge(decay_exp, 1)
        step(TT(dec, dec, dt, ALU.mult))
        signal(TT(heads(xdec), heads(xs[:, 0]), rows(dec[:, 0], 64), ALU.mult), xdt_ready, 1)
        for c in range(NT):
            for j in range(4):
                dve.wait_ge(*B.ready("row", c, j))
                if c == 1 and j == 0:
                    dve.wait_ge(*B.ready("yi", 0, 1))
                for i in range(4):
                    hd = 4 * j + i
                    ins = STT(out=seg[:, hd], in0=bank("row", c, j)[:, i * P:(i + 1) * P], scalar=nac[:, c, hd:hd + 1],
                              in1=K("ssd_mask"), op0=ALU.add, op1=ALU.add)
                    if i < 3:
                        step(ins)
                take(ins, "row", c, j)
                dve.nop().then_inc(seg_ready, 1)
            step(TT(heads(y_tok[:, c]), heads(xs[:, c]), rows(prm("d_skip"), 64), ALU.mult))
            dve.wait_ge(seg_exp, c + 1)
            dve.wait_ge(*B.released("cb", c))
            step(TT(seg[:, 0:8], seg[:, 0:8], across(cbT[:, c, 0], 8), ALU.mult))
            signal(TT(seg[:, 8:16], seg[:, 8:16], across(cbT[:, c, 1], 8), ALU.mult), w_ready, c + 1)
            if c == 1:
                for g in range(SG):
                    half = y_tmp[:, g * 512:(g + 1) * 512]
                    dve.wait_ge(*B.ready("yx", g))
                    take(TT(heads(half), heads(bank("yx", g)), rows(eac[:, 1, 8 * g:8 * g + 8], 64), ALU.mult), "yx", g)
                step(TT(y_tok[:, 1], y_tok[:, 1], y_tmp, ALU.add))
            for g in range(SG):
                half = y_tok[:, c, g * 512:(g + 1) * 512]
                dve.wait_ge(*B.ready("yi", c, g))
                take(TT(half, bank("yi", c, g), half, ALU.add), "yi", c, g)
            step(TT(y_tok[:, c], y_tok[:, c], z[:, c], ALU.mult))
            step(TT(y_tmp, y_tok[:, c], y_tok[:, c], ALU.mult))
            v = st[:, 2 * c:2 * c + 2]
            step(dve.tensor_reduce(v, two(y_tmp), AX.X, ALU.add))
            inverse(v, 512)
            signal(dve.reciprocal(v, v), var_ready, 4 + c)
        for c in range(NT):
            dve.wait_ge(rstd_ready, 4 + c)
            signal(TT(two(y_tok[:, c]), two(y_tok[:, c]), rows(rs[:, 2 * c:2 * c + 2], 512), ALU.mult), y_ready, c + 1)
        take_mod(10)
        for p in range(4):
            dve.wait_ge(*B.ready("ya", p))
            take(TT(mixed[:, 2 * p:2 * p + 2], two(bank("ya", p)), sig[:, 2 * p:2 * p + 2], ALU.mult), "ya", p)
        for p in range(4):
            dve.wait_ge(*B.ready("ys", p))
            v = seg[:, 4 * p:4 * p + 4].rearrange("p a b -> p (a b)")
            take(TT(two(v), two(bank("ys", p)), sig[:, KC + 2 * p:KC + 2 * p + 2], ALU.mult), "ys", p)
            m = mixed[:, 2 * p:2 * p + 2]
            step(TT(m, m, two(v), ALU.add))
        dve.nop().then_inc(mixed_ready, 1)
        take_mod(11)
        scale_columns(a2, prm("norm_ffn"), 32)
        dve.nop().then_inc(mod_ready, 1)
        for p in range(4):
            dve.wait_ge(*B.ready("x1", p))
            for i in range(2):
                k = 2 * p + i
                ins = STT(out=xT[:, k], in0=bank("x1", p)[:, i * L:(i + 1) * L], scalar=mod[:, 16 + k:17 + k], in1=xT[:, k],
                          op0=ALU.mult, op1=ALU.add)
                if i == 0:
                    step(ins)
            take(ins, "x1", p)
        dve.nop().then_inc(x1_ready, 1)
        norm_input(2, a2, 24)
        dve.wait_ge(*B.ready("rl"))
        take(TT(X.lr, two(bank("rl")[:, 0:2 * E]), across(prm("b_router"), NT), ALU.add), "rl")
        for t in range(NT):
            step(dve.max(m8[:, t], X.lr[:, t]))
            pick_top(X.lr[:, t], E, TOP_K, m8[:, t], X.mask[:, t], X.tm[:, t], X.rank[:, t], cnt[:, t:t + 1])
            step(TS(X.ex[:, t], X.lr[:, t], m8[:, t, 0:1], None, ALU.subtract))
        dve.nop().then_inc(mask_ready, 1)
        dve.nop().then_inc(route_ready, 1)
        dve.wait_ge(route_exp, 1)
        step(TT(X.ex, X.ex, X.mask, ALU.mult))
        step(dve.tensor_reduce(cnt[:, 2:4], X.ex, AX.X, ALU.add))
        step(dve.reciprocal(cnt[:, 2:4], cnt[:, 2:4]))
        signal(TT(X.gate[:, :, 0:E], X.ex, rows(cnt[:, 2:4], E), ALU.mult), gates_ready, 1)
        dve.wait_ge(*B.ready("cum"))
        step(TT(X.tm, two(bank("cum")[:, 0:2 * E]), X.mask, ALU.mult))
        step(TS(X.place[:, :, 0:E], X.tm, -1.0, None, ALU.add))
        take(dve.tensor_reduce(cnt[:, 4:5], bank("cum")[:, 2 * E:3 * E], AX.X, ALU.max), "cum")
        step(TS(X.flag, cnt[:, 4:5], float(CAP), None, ALU.is_gt))
        step(TS(X.place[:, :, E:], X.place[:, :, 0:2], float(-CAP), None, ALU.add))
        step(dve.tensor_copy(X.gate[:, :, E:], X.gate[:, :, 0:2]))
        X.pick(dve, 0)
        dve.wait_ge(*B.released("yb", 3))
        with dve.Fori(0, PAIRS) as p:
            X.glu(dve, BP, psum, p)
            X.pick(dve, p + 1, BP, p)
            X.add_up(dve, BP, psum, y_sum, p)
        with dve.If(X.more_rounds(dve)):
            with dve.Fori(1, ROUNDS) as r:
                dve.wait_ge(X.picked, r * PAIRS + 1)
                TS(X.place, X.place, float(-CAP), None, ALU.add).then_inc(X.moved, 1)
                with dve.Fori(0, PAIRS) as p:
                    X.glu(dve, BP, psum, r * PAIRS + p)
                    dve.wait_ge(X.moved, r)
                    X.pick(dve, p + 1, BP, r * PAIRS + p)
                    X.add_up(dve, BP, psum, y_sum, r * PAIRS + p)
    return X


def chunk_of(d, s):
    return s if d == 0 else 1 - s


def second_block(nc, ctx, io, mem, out, first_sum):
    sem = lambda n: ctx.enter_context(nc.semaphore(n))
    xT, h, psum = mem.xT, mem.h, mem.psum
    K, slot = mem.K, mem.slot

    bank_full = [sem(f"bank_full_2_{b}") for b in range(BANKS)]
    bank_free = [sem(f"bank_free_2_{b}") for b in range(BANKS)]
    slot_full = [sem(f"slot_full_2_{b}") for b in range(SLOTS)]
    B = Uses(bank_full, bank_free, layer_banks(), credit=1)
    S = Uses(slot_full, slot_full, LAYER_SLOTS, inc=16, twice=[("up", j) for j in range(11)])

    act_step, dve_step, pool_step = sem("act_step_2"), sem("dve_step_2"), sem("pool_step_2")
    x_ready = sem("x_ready")
    params_in = sem("params_in")
    pads_ready = sem("pads_ready")
    down_used = [sem("down_used_first"), sem("down_used_second")]
    sq_ready, var_ready, rstd_ready = sem("sq_ready_2"), sem("var_ready_2"), sem("rstd_ready_2")
    h_ready = sem("h_ready_2")
    rope_ready = sem("rope_ready")
    gate_abs, gate_log, lf_ready = sem("gate_abs"), sem("gate_log"), sem("lf_ready")
    r_ready = sem("r_ready")
    logits_ready, exp_ready, probs_ready = sem("logits_ready_2"), sem("exp_ready_2"), sem("probs_ready_2")
    conv_ready, silu_ready = sem("conv_ready_2"), sem("silu_ready_2")
    dlog_ready, dexp_ready, sc_ready = sem("dlog_ready"), sem("dexp_ready"), sem("sc_ready")
    kw_ready, total_ready = sem("kw_ready"), sem("total_ready")
    hm_ready, cat_ready = sem("hm_ready"), sem("cat_ready")
    tap_ready, tap_used, conv2_ready, gelu_ready, hid_ready = (
        sem(n) for n in ("tap_ready", "tap_used", "conv2_ready", "gelu_ready", "hid_ready"))
    out_done = sem("out_done")

    prm = lambda name: PARAMS2.of(mem.route, name)
    ident, ones = K("ident"), K("ones")[:, 0:P]
    A = Arena(mem.work)
    mqk_pad = A.take(8, L + 4)
    v_aug = A.take(NT, MH, P + 1)
    mixed_at = A.at
    aqk = A.take(2, NT, AW)
    mixed = Arena(mem.work, mixed_at).take(KC, L)
    w_g = A.take(KC, 16)
    rstd = A.take(1, L)[:, 0]
    cat = A.take(KC, L)
    hid_at = A.at
    av = A.take(NT, AW)
    qT, kT = A.take(4, L), A.take(4, L)
    lg_at = A.at
    lg = A.take(HEADS, L)
    pt = A.take(16, P)
    mqk = A.take(8, L)
    mo = A.take(MH, L)
    k_tok = A.take(NT, MH, P)
    qk = A.take(NT, MH, P)
    dl = A.take(8, P)
    scT = A.take(8, P)
    kw = A.take(8, P)
    st, tot = A.take(8, P + 1), A.take(8, P + 1)
    hm = A.take(NT, MH, P)
    rope_tmp = Arena(mem.work, lg_at).take(4, 8, 32)
    sq = Arena(mem.work, lg_at).take(KC, L)
    hid = Arena(mem.work, hid_at).take(FC, L)
    F = Arena(mem.work, hid_at + FC * L + 600)
    taps = F.take(3, 2, L)
    SM = Arena(mem.small)
    li, lf, lfx = SM.take(2, 8), SM.take(2, 8), SM.take(2, 8)
    bcum, btot, r = SM.take(2, 8), SM.take(2, 8), SM.take(2, 8)
    mxr, md, inter, mt, mst, mnew, den, gn = (SM.take(8) for _ in range(8))
    ex3 = SM.take(3, 8)
    mx, sm = SM.take(8), SM.take(8)
    hs = SM.take(8)

    block = ctx.enter_context(nc.Block())

    @block.sync
    def _(sp):
        with sp.Fori(0, LAYERS) as l:
            def used(name, j):
                kind = name[0]
                if kind == "win":
                    last = (("aq", 1), ("ak", 1), ("av", 1), ("mqk", 1), ("mqk", 3), ("mv", 1), ("mo", 1))[name[1]]
                    return B.ready(*last, it=l)
                if kind == "wout":
                    return B.ready("mix", 2 * name[1] + 1, it=l)
                if kind == "up":
                    return B.ready("up", 2 * name[1] + 1, it=l)
                return down_used[name[2]], l * 4 + 4 + name[1] + 1

            for i, name in enumerate(LAYER_SLOTS):
                kind, j = name[0], name[1]
                if i < SLOTS:
                    sp.wait_ge(down_used[i % 2], l * 4 + 2 + i // 2 + 1)
                else:
                    sp.wait_ge(*used(LAYER_SLOTS[i - SLOTS], i))
                lay = bass.ds(l, 1)
                if kind == "up":
                    dst = slot(S.no(name), KC, 512)
                    for part in range(2):
                        src = io["w_up_2"][lay, :, part * FF + 256 * j:part * FF + 256 * j + 256]
                        sp.dma_start(dst[:, :, part * 256:part * 256 + 256], src.rearrange("a (k p) n -> p (a k) n", p=P))\
                          .then_inc(*S.fills(*name))
                    continue
                if kind == "down":
                    half = name[2]
                    src = io["w_down_2"][lay, half * FF // 2:(half + 1) * FF // 2, 256 * j:256 * j + 256]
                    dst = slot(S.no(name), FC // 2, 256)
                else:
                    w = io["w_in_2"] if kind == "win" else io["w_out_2"]
                    src, dst = w[lay, :, 512 * j:512 * j + 512], slot(S.no(name), KC, 512)
                sp.dma_start(dst, src.rearrange("a (k p) n -> p (a k) n", p=P)).then_inc(*S.fills(*name))
        sp.wait_ge(x_ready, 1 + 2 * LAYERS)
        sp.dma_start(out, xT).then_inc(out_done, 16)
        sp.wait_ge(out_done, 16)

    @block.gpsimd
    def _(pool):
        step = Steps(pool, pool_step)
        pool.wait_ge(x_ready, 1)
        pool.memset(mqk_pad[:, :, 0:2], 0.0).then_inc(pads_ready, 1)
        pool.memset(mqk_pad[:, :, L + 2:], 0.0).then_inc(pads_ready, 1)
        pool.memset(v_aug[:, :, :, P:], 1.0).then_inc(pads_ready, 1)
        with pool.Fori(0, LAYERS) as l:
            pool.wait_ge(x_ready, l * 2 + 1)
            lay = bass.ds(l, 1)
            pool.dma_start(mem.route[:, 0:PARAMS2.n], io["params2"][lay].rearrange("a p n -> p (a n)")).then_inc(params_in, 16)
            pool.dma_start(w_g, io["w_in_2"][lay, :, 3584:3600].rearrange("a (k p) n -> p (a k) n", p=P)).then_inc(params_in, 16)
            for i in range(2):
                for t in range(NT):
                    pool.wait_ge(*B.released(("aq", "ak")[i], t, it=l))
                    v = aqk[:, i, t].rearrange("p (h c n) -> p h c n", h=HEADS, c=2)
                    cos = across(K("cos")[:, 32 * t:32 * t + 32], HEADS)
                    sin = across(K("sin")[:, 32 * t:32 * t + 32], HEADS)
                    step(pool.tensor_tensor(rope_tmp[:, 0], v[:, :, 0], cos, ALU.mult))
                    step(pool.tensor_tensor(rope_tmp[:, 1], v[:, :, 1], sin, ALU.mult))
                    step(pool.tensor_tensor(rope_tmp[:, 2], v[:, :, 1], cos, ALU.mult))
                    step(pool.tensor_tensor(rope_tmp[:, 3], v[:, :, 0], sin, ALU.mult))
                    step(pool.tensor_tensor(v[:, :, 0], rope_tmp[:, 0], rope_tmp[:, 1], ALU.subtract))
                    step(pool.tensor_tensor(v[:, :, 1], rope_tmp[:, 2], rope_tmp[:, 3], ALU.add))
                    pool.nop().then_inc(rope_ready, 1)
            step.restart()

    @block.tensor
    def _(pe):
        pe.nop().then_inc(down_used[0], 4)
        for free in bank_free:
            pe.nop().then_inc(free, 1)
        with pe.Fori(0, LAYERS) as l:
            def bank(*name):
                return psum[:, B.no(name)]

            def empty(*name):
                pe.wait_ge(*B.empty(*name, it=l))

            def ready(*name):
                pe.wait_ge(*S.ready(*name, it=l))
                return slot(S.no(name), KC, 512)

            def evicted(*name):
                pe.wait_ge(*B.released(*name, it=l))

            def sum_squares(n):
                pe.wait_ge(sq_ready, l * 4 + n + 1)
                empty("ss", n)
                for k in range(KC):
                    ins = matmul(pe, bank("ss", n)[:, 0:L], ones, sq[:, k], k == 0, k == KC - 1)
                ins.then_inc(*B.fills("ss", n))

            def by_token(name, w, n=512):
                for t in range(NT):
                    empty(name, t)
                    for k in range(KC):
                        ins = matmul(pe, bank(name, t)[:, 0:n], h[:, k, t * P:(t + 1) * P], w[:, k, 0:n], k == 0, k == KC - 1)
                    ins.then_inc(*B.fills(name, t))

            def by_feature(name, w, c0, rhs=h):
                empty(*name)
                for i in range(2):
                    for k in range(KC):
                        ins = matmul(pe, bank(*name)[:, i * L:(i + 1) * L], w[:, k, c0 + i * P:c0 + (i + 1) * P], rhs[:, k],
                                     k == 0, k == KC - 1)
                ins.then_inc(*B.fills(*name))

            def transposes(name, blocks):
                empty(*name)
                for i, b in enumerate(blocks):
                    ins = pe.transpose(bank(*name)[:, i * P:(i + 1) * P], b, ident)
                ins.then_inc(*B.fills(*name))

            sum_squares(0)
            pe.wait_ge(h_ready, l * 2 + 1)
            for j, name in enumerate(("aq", "ak", "av")):
                by_token(name, ready("win", j))
            for j in range(2):
                w = ready("win", 3 + j)
                by_feature(("mqk", 2 * j), w, 0)
                by_feature(("mqk", 2 * j + 1), w, 256)
            pe.wait_ge(params_in, l * 32 + 32)
            empty("gates")
            for t in range(NT):
                for k in range(KC):
                    ins = matmul(pe, bank("gates")[:, t * 16:t * 16 + 16], h[:, k, t * P:(t + 1) * P], w_g[:, k], k == 0, k == KC - 1)
            ins.then_inc(*B.fills("gates"))
            by_token("mv", ready("win", 5))
            w = ready("win", 6)
            for p in range(2):
                by_feature(("mo", p), w, 256 * p)
            pe.wait_ge(lf_ready, l + 1)
            empty("bc")
            for s in range(2):
                for d in range(2):
                    c = 8 * s + 4 * d
                    matmul(pe, bank("bc")[:, c:c + 4], K("tri_le") if d == 0 else K("tri_ge"), lf[:, s, 4 * d:4 * d + 4])
                ins = matmul(pe, bank("bc")[:, 16 + 8 * s:24 + 8 * s], ones, lf[:, s])
            ins.then_inc(*B.fills("bc"))
            for t in range(NT):
                for i, name in enumerate(("qT", "kT")):
                    if t == 0 and i == 0:
                        pe.wait_ge(rope_ready, l * 4 + 4)
                    transposes((name, t), [aqk[:, i, t, c * P:(c + 1) * P] for c in range(4)])

            def logits(t):
                evicted("kT", 1)
                for g, h0 in enumerate(PAIRS_OF_HEADS):
                    empty("S", t, g)
                    for i in range(2):
                        hd = h0 + 2 * i
                        r_ = slice(64 * (hd % 2), 64 * (hd % 2) + 64)
                        ins = matmul(pe, bank("S", t, g)[:, i * L:(i + 1) * L], qT[r_, hd // 2, t * P:(t + 1) * P], kT[r_, hd // 2])
                    ins.then_inc(*B.fills("S", t, g))

            def attend(t):
                pe.wait_ge(probs_ready, l * 2 + t + 1)
                for j in range(4):
                    transposes(("PT", t, j), [lg[:, 2 * j + i, s * P:(s + 1) * P] for i in range(2) for s in range(2)])
                empty("O", t)
                evicted("PT", t, 3)
                for hd in range(HEADS):
                    r_ = slice(64 * (hd % 2), 64 * (hd % 2) + 64)
                    for s in range(2):
                        ins = matmul(pe, bank("O", t)[r_, (hd // 2) * P:(hd // 2 + 1) * P], av[:, s, hd * HD:(hd + 1) * HD],
                                     pt[:, 2 * hd + s], s == 0, s == 1)
                ins.then_inc(*B.fills("O", t))

            def r_rows(s):
                for d in range(2):
                    empty("r", s, d)
                    for i in range(MH):
                        ins = matmul(pe, bank("r", s, d)[:, i * P:(i + 1) * P],
                                     r[:, s, 4 * d + i:4 * d + i + 1].to_broadcast([P, P]), ident)
                    ins.then_inc(*B.fills("r", s, d))

            def numerators(s):
                pe.wait_ge(sc_ready, l * 2 + s + 1)
                for d in range(2):
                    transposes(("cT", s, d), [dl[:, 4 * d + i] for i in range(MH)])
                evicted("cT", s, 1)
                for j in range(4):
                    empty("num", s, j)
                    for i in range(2):
                        c = 2 * j + i
                        ins = matmul(pe, bank("num", s, j)[:, i * 129:(i + 1) * 129], scT[:, c], v_aug[:, chunk_of(c // 4, s), c % 4])
                    ins.then_inc(*B.fills("num", s, j))

            logits(0)
            pe.wait_ge(silu_ready, l + 1)
            for c in range(NT):
                empty("qk", c)
                for i in range(MH):
                    ins = matmul(pe, bank("qk", c)[:, i * P:(i + 1) * P], mqk[:, i, c * P:(c + 1) * P], mqk[:, MH + i, c * P:(c + 1) * P])
                ins.then_inc(*B.fills("qk", c))
            for t in range(NT):
                transposes(("kt", t), [mqk[:, MH + i, t * P:(t + 1) * P] for i in range(MH)])
            attend(0)
            logits(1)
            pe.wait_ge(r_ready, l + 1)
            r_rows(0)
            attend(1)
            numerators(0)
            pe.wait_ge(kw_ready, l + 1)
            for j in range(4):
                empty("st", j)
                for i in range(2):
                    c = 2 * j + i
                    ins = matmul(pe, bank("st", j)[:, i * 129:(i + 1) * 129], kw[:, c], v_aug[:, chunk_of(c // 4, 0), c % 4])
                ins.then_inc(*B.fills("st", j))
            r_rows(1)
            numerators(1)
            evicted("st", 3)
            for j in range(4):
                empty("ix", j)
                for i in range(2):
                    c = 2 * j + i
                    t = chunk_of(c // 4, 1)
                    ins = matmul(pe, bank("ix", j)[:, i * 129:(i + 1) * 129], mqk[:, c % 4, t * P:(t + 1) * P], st[:, c])
                ins.then_inc(*B.fills("ix", j))
            pe.wait_ge(hm_ready, l + 1)
            for t in range(NT):
                transposes(("hT", t), [hm[:, t, i] for i in range(MH)])
            evicted("hT", 1)
            evicted("O", 1)
            for p in range(4):
                if p % 2 == 0:
                    w = ready("wout", p // 2)
                by_feature(("mix", p), w, 256 * (p % 2), cat)
            sum_squares(1)
            sum_squares(2)
            pe.wait_ge(h_ready, l * 2 + 2)
            for c in range(FC):
                if c % 2 == 0:
                    w = ready("up", c // 2)
                empty("up", c)
                for part in range(2):
                    for k in range(KC):
                        c0 = 256 * part + P * (c % 2)
                        ins = matmul(pe, bank("up", c)[:, part * L:(part + 1) * L], w[:, k, c0:c0 + P], h[:, k], k == 0, k == KC - 1)
                ins.then_inc(*B.fills("up", c))
            pe.wait_ge(hid_ready, l * FC + FC)
            for j in range(4):
                empty("down", 2 * j)
                empty("down", 2 * j + 1)
                for half in range(2):
                    pe.wait_ge(*S.ready("down", j, half, it=l))
                    w = slot(S.no(("down", j, half)), FC // 2, 256)
                    for i in range(2):
                        for k in range(FC // 2):
                            ins = matmul(pe, bank("down", 2 * j + i)[:, 0:L], w[:, k, i * P:(i + 1) * P], hid[:, half * (FC // 2) + k],
                                         half == 0 and k == 0, half == 1 and k == FC // 2 - 1)
                        if half == 1:
                            ins.then_inc(*B.fills("down", 2 * j + i))
                    if half == 0:
                        ins.then_inc(down_used[0], 1)
            sum_squares(3)

    @block.scalar
    def _(act):
        step = Steps(act, act_step)
        act.nop().then_inc(down_used[1], 4)
        act.wait_ge(x_ready, 1)
        with act.Fori(0, LAYERS) as l:
            def bank(*name):
                return psum[:, B.no(name)]

            def take(out_, in_, *name, func=ACT.Copy, **kw_):
                act.wait_ge(*B.ready(*name, it=l))
                act.activation(out_, in_, func, **kw_).then_inc(*B.frees(*name))

            def cut(v, n):
                return v.rearrange("p (a b) -> p a b", a=n)

            def squares(v, n):
                act.activation(sq, v, ACT.Square).then_inc(sq_ready, 1)

            def root(out_, in_, n):
                act.wait_ge(var_ready, l * 5 + n)
                act.activation(out_, in_, ACT.Sqrt).then_inc(rstd_ready, 1)

            act.wait_ge(x_ready, l * 2 + 1)
            squares(xT, 0)
            root(rstd, rstd, 1)
            for i, name in enumerate(("aq", "ak")):
                for t in range(NT):
                    take(aqk[:, i, t], bank(name, t), name, t)
            for t in range(NT):
                take(av[:, t], bank("av", t), "av", t)
            act.wait_ge(pads_ready, 3)
            for p in range(4):
                take(mqk_pad[:, 2 * p:2 * p + 2, 2:L + 2], cut(bank("mqk", p), 2), "mqk", p)
            for t in range(NT):
                take(v_aug[:, t, :, 0:P], cut(bank("mv", t), MH), "mv", t)
            for p in range(2):
                take(mo[:, 2 * p:2 * p + 2], cut(bank("mo", p), 2), "mo", p, func=ACT.Sigmoid)
            act.wait_ge(gate_abs, l + 1)
            step(act.activation(lf, lf, ACT.Exp, scale=-1.0))
            act.activation(lf, lf, ACT.Ln, bias=1.0).then_inc(gate_log, 1)
            act.wait_ge(conv_ready, l + 1)
            act.activation(mqk, mqk, ACT.Silu).then_inc(silu_ready, 1)
            act.wait_ge(logits_ready, l * 2 + 1)
            act.activation(lg, lg, ACT.Exp).then_inc(exp_ready, 1)
            for c in range(NT):
                take(qk[:, c], cut(bank("qk", c), MH), "qk", c, scale=P ** -0.5)
            for t in range(NT):
                take(k_tok[:, t], cut(bank("kt", t), MH), "kt", t, scale=P ** -0.5)

            def attended(t):
                for j in range(4):
                    take(pt[:, 4 * j:4 * j + 4], cut(bank("PT", t, j), 4), "PT", t, j)
                take(cat[:, 0:4, t * P:(t + 1) * P], cut(bank("O", t), 4), "O", t)

            attended(0)
            act.wait_ge(logits_ready, l * 2 + 2)
            act.activation(lg, lg, ACT.Exp).then_inc(exp_ready, 1)
            attended(1)
            for s in range(2):
                act.wait_ge(dlog_ready, l * 2 + s + 1)
                step(act.activation(ex3, ex3, ACT.Exp))
                act.activation(dl, dl, ACT.Exp).then_inc(dexp_ready, 1)
                for d in range(2):
                    take(scT[:, 4 * d:4 * d + 4], cut(bank("cT", s, d), MH), "cT", s, d)
                if s == 1:
                    act.wait_ge(total_ready, l + 1)
                for j in range(4):
                    take(tot[:, 2 * j:2 * j + 2], cut(bank("num", s, j)[:, 0:258], 2), "num", s, j)
                if s == 0:
                    for j in range(4):
                        take(st[:, 2 * j:2 * j + 2], cut(bank("st", j)[:, 0:258], 2), "st", j)
            root(hs, hs, 2)
            for p in range(4):
                take(mixed[:, 2 * p:2 * p + 2], cut(bank("mix", p), 2), "mix", p)
            act.wait_ge(*B.released("mix", 3, it=l))
            squares(mixed, 1)
            root(rstd, rstd, 3)
            act.wait_ge(x_ready, l * 2 + 2)
            squares(xT, 2)
            root(rstd, rstd, 4)

            def tap(c):
                act.wait_ge(*B.ready("up", c, it=l))
                if c >= 3:
                    act.wait_ge(hid_ready, l * FC + (c - 2))
                for part in range(2):
                    f = c + FC * part
                    ins = act.activation(taps[:, c % 3, part], bank("up", c)[:, part * L:(part + 1) * L], ACT.Identity,
                                         scale=prm("ffn_w")[:, 3 * f + 1:3 * f + 2], bias=prm("ffn_b")[:, f:f + 1])
                ins.then_inc(tap_ready, 1)

            def gelu(c):
                act.wait_ge(conv2_ready, l * FC + (c + 1))
                act.activation(taps[:, c % 3, 0], taps[:, c % 3, 0], ACT.Gelu_apprx_tanh).then_inc(gelu_ready, 1)

            for c in range(FC):
                tap(c)
                if c >= 1:
                    gelu(c - 1)
            gelu(FC - 1)
            for c in range(KC):
                take(mixed[:, c], bank("down", c)[:, 0:L], "down", c)
                if c % 2 == 1:
                    act.wait_ge(*B.released("down", c, it=l))
                    act.nop().then_inc(down_used[1], 1)
            squares(mixed, 3)
            root(rstd, rstd, 5)
            step.restart()

    @block.vector
    def _(dve):
        step = Steps(dve, dve_step)
        TS, TT, STT = dve.tensor_scalar, dve.tensor_tensor, dve.scalar_tensor_tensor
        for k in range(KC):
            step(STT(out=xT[:, k], in0=first_sum[:, k], scalar=mem.mod[:, 40 + k:41 + k], in1=xT[:, k],
                     op0=ALU.mult, op1=ALU.add))
        dve.nop().then_inc(x_ready, 1)
        step.restart()
        with dve.Fori(0, LAYERS) as l:
            def bank(*name):
                return psum[:, B.no(name)]

            def filled(*name):
                dve.wait_ge(*B.ready(*name, it=l))

            def take(ins, *name):
                ins.then_inc(*B.frees(*name))
                dve.wait_ge(*B.released(*name, it=l))

            def signal(ins, sem_, n):
                ins.then_inc(sem_, 1)
                dve.wait_ge(sem_, n)

            def cut(v, n):
                return v.rearrange("p (a b) -> p a b", a=n)

            def inverse_root(n, which):
                filled("ss", n)
                take(TS(rstd, bank("ss", n)[:, 0:L], 1.0 / D, EPS, ALU.mult, ALU.add), "ss", n)
                signal(dve.reciprocal(rstd, rstd), var_ready, l * 5 + which)
                dve.wait_ge(rstd_ready, l * 5 + which)

            def norm_input(g, n):
                for k in range(KC):
                    ins = STT(out=h[:, k], in0=xT[:, k], scalar=g[:, k:k + 1], in1=rstd, op0=ALU.mult, op1=ALU.mult)
                signal(ins, h_ready, l * 2 + n)

            def add_normed(g, n, last=False):
                for k in range(KC):
                    ins = STT(out=mixed[:, k], in0=mixed[:, k], scalar=g[:, k:k + 1], in1=rstd, op0=ALU.mult, op1=ALU.mult)
                step(ins)
                if last:
                    step.restart()
                signal(TT(xT, xT, mixed, ALU.add), x_ready, l * 2 + n)

            inverse_root(0, 1)
            dve.wait_ge(params_in, l * 32 + 32)
            norm_input(prm("mix_pre"), 1)
            filled("gates")
            for s in range(2):
                for d in range(2):
                    t = chunk_of(d, s)
                    c = slice(4 * d, 4 * d + 4)
                    a = 8 * d
                    step(TT(li[:, s, c], bank("gates")[:, 16 * t + a:16 * t + a + 4], prm("gate_b")[:, a:a + 4], ALU.add))
                    ins = TT(lfx[:, s, c], bank("gates")[:, 16 * t + a + 4:16 * t + a + 8], prm("gate_b")[:, a + 4:a + 8], ALU.add)
                    if (s, d) != (1, 1):
                        step(ins)
            take(ins, "gates")
            signal(STT(out=lf, in0=lfx, scalar=-1.0, in1=lfx, op0=ALU.mult, op1=ALU.max), gate_abs, l + 1)
            for k in range(8):
                if k % 2 == 0:
                    dve.wait_ge(*B.released("mqk", k // 2, it=l))
                cw = prm("conv_w")[:, 5 * k:5 * k + 5]
                step(TS(mqk[:, k], mqk_pad[:, k, 0:L], cw[:, 0:1], prm("conv_b")[:, k:k + 1], ALU.mult, ALU.add))
                for j in range(1, 5):
                    ins = STT(out=mqk[:, k], in0=mqk_pad[:, k, j:j + L], scalar=cw[:, j:j + 1], in1=mqk[:, k],
                              op0=ALU.mult, op1=ALU.add)
                    if (k, j) != (7, 4):
                        step(ins)
            signal(ins, conv_ready, l + 1)
            dve.wait_ge(gate_log, l + 1)
            step(TS(lfx, lfx, 0.0, None, ALU.min))
            signal(TT(lf, lfx, lf, ALU.subtract), lf_ready, l + 1)
            filled("bc")
            step(dve.tensor_copy(bcum, cut(bank("bc")[:, 0:16], 2)))
            take(dve.tensor_copy(btot, cut(bank("bc")[:, 16:32], 2)), "bc")
            signal(TT(r, li, bcum, ALU.subtract), r_ready, l + 1)
            for t in range(NT):
                for dst, name in ((qT, "qT"), (kT, "kT")):
                    filled(name, t)
                    take(dve.tensor_copy(dst[:, :, t * P:(t + 1) * P], cut(bank(name, t), 4)), name, t)

            def soften(t):
                for g, h0 in enumerate(PAIRS_OF_HEADS):
                    filled("S", t, g)
                    take(STT(out=lg[:, h0:h0 + 3:2], in0=cut(bank("S", t, g), 2), scalar=HD ** -0.5,
                             in1=across(K("log_count")[:, L * t:L * t + L], 2), op0=ALU.mult, op1=ALU.add), "S", t, g)
                step(dve.tensor_reduce(mx, lg, AX.X, ALU.max))
                signal(TT(lg, lg, rows(mx, L), ALU.subtract), logits_ready, l * 2 + t + 1)
                dve.wait_ge(exp_ready, l * 2 + t + 1)
                step(dve.tensor_reduce(sm, lg, AX.X, ALU.add))
                step(dve.reciprocal(sm, sm))
                signal(TT(lg, lg, rows(sm, L), ALU.mult), probs_ready, l * 2 + t + 1)

            def weigh(s):
                if s == 0:
                    step(dve.memset(mst, 0.0))
                for d in range(2):
                    filled("r", s, d)
                    step(dve.tensor_reduce(mxr[:, 4 * d:4 * d + 4], cut(bank("r", s, d), MH), AX.X, ALU.max))
                    for i in range(MH):
                        c = 4 * d + i
                        ins = STT(out=dl[:, c], in0=bank("r", s, d)[:, i * P:(i + 1) * P], scalar=bcum[:, s, c:c + 1],
                                  in1=K("mask_fwd") if d == 0 else K("mask_bwd"), op0=ALU.add, op1=ALU.add)
                        if i < MH - 1:
                            step(ins)
                    take(ins, "r", s, d)
                step(dve.tensor_reduce(md, dl, AX.X, ALU.max))
                step(TT(inter, bcum[:, s], mst, ALU.add))
                step(TT(mt, inter, md, ALU.max))
                step(TT(mnew, btot[:, s], mst, ALU.add))
                step(TT(mxr, mxr, btot[:, s], ALU.add))
                step(TT(mnew, mnew, mxr, ALU.max))
                step(TT(ex3[:, 0], inter, mt, ALU.subtract))
                step(TS(ex3[:, 1], mt, -1.0, None, ALU.mult))
                step(TT(ex3[:, 2], r[:, s], btot[:, s], ALU.add))
                step(TT(ex3[:, 2], ex3[:, 2], mnew, ALU.subtract))
                step(dve.tensor_copy(mst, mnew))
                signal(TT(dl, dl, rows(mt, P), ALU.subtract), dlog_ready, l * 2 + s + 1)
                dve.wait_ge(dexp_ready, l * 2 + s + 1)
                dve.wait_ge(*B.released("qk", 1, it=l))
                for d in range(2):
                    v = dl[:, 4 * d:4 * d + 4]
                    ins = TT(v, v, qk[:, chunk_of(d, s)], ALU.mult)
                    if d == 0:
                        step(ins)
                signal(ins, sc_ready, l * 2 + s + 1)
                if s == 0:
                    dve.wait_ge(*B.released("kt", 1, it=l))
                    for d in range(2):
                        ins = TT(kw[:, 4 * d:4 * d + 4], k_tok[:, chunk_of(d, 0)], rows(ex3[:, 2, 4 * d:4 * d + 4], P), ALU.mult)
                        if d == 0:
                            step(ins)
                    signal(ins, kw_ready, l + 1)

            def divide(s):
                dve.wait_ge(*B.released("num", s, 3, it=l))
                if s == 1:
                    for j in range(4):
                        filled("ix", j)
                        for i in range(2):
                            c = 2 * j + i
                            ins = STT(out=tot[:, c], in0=bank("ix", j)[:, i * 129:(i + 1) * 129], scalar=ex3[:, 0, c:c + 1],
                                      in1=tot[:, c], op0=ALU.mult, op1=ALU.add)
                            if i == 0:
                                step(ins)
                        take(ins, "ix", j)
                d_ = tot[:, :, P:].rearrange("p a b -> p (a b)")
                step(STT(out=den, in0=d_, scalar=-1.0, in1=d_, op0=ALU.mult, op1=ALU.max))
                step(TT(den, den, ex3[:, 1], ALU.max))
                step(dve.reciprocal(den, den))
                for d in range(2):
                    v, rd = tot[:, 4 * d:4 * d + 4, 0:P], rows(den[:, 4 * d:4 * d + 4], P)
                    if s == 0:
                        step(TT(hm[:, chunk_of(d, 0)], v, rd, ALU.mult))
                    else:
                        step(TT(v, v, rd, ALU.mult))
                        step(TT(hm[:, chunk_of(d, 1)], hm[:, chunk_of(d, 1)], v, ALU.add))
                if s == 0:
                    dve.nop().then_inc(total_ready, 1)

            soften(0)
            soften(1)
            weigh(0)
            divide(0)
            weigh(1)
            divide(1)
            hm8 = hm.rearrange("p t h n -> p (t h) n")
            step(TT(kw, hm8, hm8, ALU.mult))
            step(dve.tensor_reduce(hs, kw, AX.X, ALU.add))
            step(TS(hs, hs, 1.0 / P, EPS, ALU.mult, ALU.add))
            signal(dve.reciprocal(hs, hs), var_ready, l * 5 + 2)
            dve.wait_ge(rstd_ready, l * 5 + 2)
            signal(TT(hm8, hm8, rows(hs, P), ALU.mult), hm_ready, l + 1)
            for t in range(NT):
                filled("hT", t)
                for i in range(MH):
                    ins = STT(out=cat[:, 4 + i, t * P:(t + 1) * P], in0=bank("hT", t)[:, i * P:(i + 1) * P],
                              scalar=prm("head_g")[:, i:i + 1], in1=mo[:, i, t * P:(t + 1) * P], op0=ALU.mult, op1=ALU.mult)
                    if i < MH - 1:
                        step(ins)
                take(ins, "hT", t)
            inverse_root(1, 3)
            add_normed(prm("mix_post"), 2)
            inverse_root(2, 4)
            norm_input(prm("ffn_pre"), 2)

            def outer_taps(c):
                dve.wait_ge(tap_ready, l * FC + (c + 1))
                for part in range(2):
                    f = c + FC * part
                    u, v = bank("up", c)[:, part * L:(part + 1) * L], taps[:, c % 3, part]
                    fw = prm("ffn_w")[:, 3 * f:3 * f + 3]
                    step(STT(out=v[:, 1:], in0=u[:, 0:L - 1], scalar=fw[:, 0:1], in1=v[:, 1:], op0=ALU.mult, op1=ALU.add))
                    ins = STT(out=v[:, 0:L - 1], in0=u[:, 1:], scalar=fw[:, 2:3], in1=v[:, 0:L - 1], op0=ALU.mult, op1=ALU.add)
                    if part == 0:
                        step(ins)
                take(ins, "up", c)
                dve.nop().then_inc(conv2_ready, 1)

            def hidden(c):
                dve.wait_ge(gelu_ready, l * FC + (c + 1))
                signal(TT(hid[:, c], taps[:, c % 3, 0], taps[:, c % 3, 1], ALU.mult), hid_ready, l * FC + (c + 1))

            for c in range(FC):
                outer_taps(c)
                if c >= 1:
                    hidden(c - 1)
            hidden(FC - 1)
            inverse_root(3, 5)
            add_normed(prm("ffn_post"), 3, last=True)


def program(nc, shapes):
    io = {name: nc.dram_tensor(name, shapes[name], F32, kind="ExternalInput").ap() for name in INPUTS}
    out = nc.dram_tensor("out", [P, KC, L], F32, kind="ExternalOutput").ap()
    with ExitStack() as ctx:
        mem = Memory(nc, ctx)
        with ExitStack() as c1:
            X = first_block(nc, c1, io, mem)
        second_block(nc, ctx, io, mem, out, X.y_sum)


def kernel(**inputs):
    import concourse.bacc as _bacc
    from concourse.bass_utils import run_bass_kernel_spmd as _run

    arrays = {name: np.ascontiguousarray(v) for name, v in lay_out(inputs).items()}
    nc = _bacc.Bacc("TRN2", target_bir_lowering=False, num_devices=1)
    program(nc, {name: v.shape for name, v in arrays.items()})
    r = _run(nc, [arrays], core_ids=[0])
    return r.results[0]["out"].transpose(2, 1, 0).reshape(1, L, D)
```

```python
from contextlib import ExitStack
import math

import numpy as np

import concourse.bass as bass
from concourse import mybir

F32 = mybir.dt.float32
I32 = mybir.dt.int32
ACT = mybir.ActivationFunctionType
ALU = mybir.AluOpType
AX = mybir.AxisListType

P = 128
D = 1024
L = 256
KC = D // P
NT = L // P
HEADS, HD = 8, 64
AW = HEADS * HD
TOPK = min(256, L // 4)
BUCKETS, MAX_DIST = 32, 128
SH, SG, SN = 16, 2, 128
SI = SH * 64
CONV_CH = SI + 2 * SG * SN
NX = CONV_CH // P
E, TOP_K, DE = 32, 4, 1024
PAIRS = E // 2
CAP = 64
ROUNDS = L // CAP
LIMIT, ALPHA = 7.0, 1.702
EPS = 1e-6
LAYERS = 2
MH = 4
FF = ((8 * D // 3 + 255) // 256) * 256
FC = FF // P
SLOT = 4096
SLOTS = 4
MOE_SLOTS = 6
BANKS = 8
FAR = -3.0e38
NEG = -1.0e30

C_Q, C_KV, C_QI, C_KI = 0, 512, 768, 1280
C_Z, C_XBC, C_DT, C_GATE = 1352, 2376, 3912, 3928
D_IN = C_GATE + 2 * D


class Layout:

    def __init__(self, parts):
        self.at, self.n = {}, 0
        for name, n in parts:
            self.at[name] = (self.n, n)
            self.n += n

    def of(self, ap, name, rows=P):
        a, n = self.at[name]
        return ap[0:rows, a:a + n]


CONSTS = Layout([("ident", P), ("tri_le", P), ("tri_ge", P), ("ones", 2 * P), ("ssd_mask", P), ("causal", NT * L),
                 ("mask_fwd", P), ("mask_bwd", P), ("log_count", NT * L), ("cos", NT * 32), ("sin", NT * 32),
                 ("bucket", 384), ("slot_no", CAP), ("pair_row", P)])
PARAMS = Layout([("c", KC), ("norm_mix", KC), ("norm_ffn", KC), ("b_ada", 48), ("conv_w", NX * 4), ("conv_b", NX),
                 ("kv_norm", 2), ("q_norm", 1), ("k_norm", 1), ("ln_w", 1), ("ln_b", 1), ("ssm_norm", KC),
                 ("dt_bias", SH), ("a_log", SH), ("d_skip", SH), ("b_router", E), ("rel_bias", HEADS)])
PARAMS2 = Layout([("mix_pre", KC), ("mix_post", KC), ("ffn_pre", KC), ("ffn_post", KC), ("conv_w", 8 * 5),
                  ("conv_b", 8), ("head_g", MH), ("ffn_w", 2 * FC * 3), ("ffn_b", 2 * FC), ("gate_b", 16)])


def constants():
    out = np.zeros((P, CONSTS.n), np.float32)

    def put(name, v):
        a, n = CONSTS.at[name]
        v = np.asarray(v, np.float32)
        out[:v.shape[0], a:a + n] = v.reshape(v.shape[0], n)

    i, j = np.arange(P)[:, None], np.arange(P)[None, :]
    put("ident", i == j)
    put("tri_le", i <= j)
    put("tri_ge", i >= j)
    put("ones", np.ones((P, 2 * P)))
    put("ssd_mask", np.where(i <= j, 0.0, NEG))
    q = np.arange(L).reshape(NT, P).T[:, :, None]
    k = np.arange(L)[None, None, :]
    put("causal", np.where(k <= q, 0.0, FAR))
    put("mask_fwd", np.where(j <= i, 0.0, NEG))
    put("mask_bwd", np.where(j >= i, 0.0, NEG))
    off = np.abs(q - k)
    count = (off <= 64) * 1 + (off % 4 == 0) * (off // 4 <= 64) + (off % 16 == 0) * (off // 16 <= 64)
    put("log_count", np.where(count > 0, np.log(np.maximum(count, 1)), NEG))
    inv = (10000.0 ** (-np.arange(0, 64, 2, dtype=np.float32) / np.float32(64))).astype(np.float32)
    ang = (np.arange(L, dtype=np.float32)[:, None] * inv[None, :]).astype(np.float32).reshape(NT, P, 32)
    put("cos", np.cos(ang).transpose(1, 0, 2))
    put("sin", np.sin(ang).transpose(1, 0, 2))
    n = np.maximum(L - 1 - np.arange(384), 0)
    exact = BUCKETS // 2
    large = exact + (np.log(np.maximum(n, 1).astype(np.float32) / exact)
                     / math.log(MAX_DIST / exact) * (BUCKETS - exact)).astype(np.int32)
    bucket = np.where(n < exact, n, np.minimum(large, BUCKETS - 1))
    put("bucket", np.arange(BUCKETS)[:, None] == bucket[None, :])
    put("slot_no", np.broadcast_to(np.arange(CAP), (P, CAP)))
    put("pair_row", np.arange(2)[:, None] == (np.arange(P)[None, :] // CAP))
    return out


class Uses:

    def __init__(self, full, free, names, inc=1, base=None, twice=(), credit=0):
        n = len(full)
        self.credit = credit
        self.full, self.free, self.inc = full, free, inc
        self.base = list(base or [0] * n)
        self.at = {}
        self.per, self.fills_per, self.filled = [0] * n, [0] * n, {}
        for i, name in enumerate(names):
            assert name not in self.at, name
            self.at[name] = (i % n, self.per[i % n])
            self.per[i % n] += 1
            self.fills_per[i % n] += 2 if name in twice else 1
            self.filled[name] = self.fills_per[i % n]

    def no(self, name):
        return self.at[name][0]

    def _value(self, name, it):
        b, u = self.at[name]
        return it * self.per[b] + (self.base[b] + u + self.credit)

    def empty(self, *name, it=0):
        return self.free[self.at[name][0]], self._value(name, it)

    def ready(self, *name, it=0):
        b = self.at[name][0]
        return self.full[b], it * (self.fills_per[b] * self.inc) + (self.base[b] + self.filled[name]) * self.inc

    def released(self, *name, it=0):
        return self.free[self.at[name][0]], self._value(name, it) + 1

    def fills(self, *name):
        return self.full[self.at[name][0]], self.inc

    def frees(self, *name):
        return self.free[self.at[name][0]], 1

    def after(self, passes=1):
        return [b + passes * p for b, p in zip(self.base, self.per)]


class Steps:

    def __init__(self, eng, sem):
        self.eng, self.sem, self.n = eng, sem, 0

    def __call__(self, ins):
        self.n += 1
        ins.then_inc(self.sem, 1)
        self.eng.wait_ge(self.sem, self.n)

    def restart(self):
        self.eng.sem_clear(self.sem)
        self.n = 0


def front_banks():
    u = [("m", 0), ("ss", 1)] + [("m", j) for j in range(1, 4)]
    u += [("q", t) for t in range(NT)] + [("kv", t) for t in range(NT)]
    u += [("qi", p) for p in range(2)] + [("kw", t) for t in range(NT)] + [("bvec",), ("m", 4)]
    u += [("xbc", 0), ("xbc", 1), ("m", 5), ("kvT",), ("qT", 0), ("qT", 1), ("kiT",)]
    u += [("kv_up", s, t) for s in range(2) for t in range(NT)]
    u += [("dots", 0, g) for g in range(4)] + [("xbc", 2), ("xbc", 3), ("m", 6)]
    u += [("dots", 1, g) for g in range(4)] + [("kT", t) for t in range(NT)]
    u += [("xbc", 4), ("xbc", 5), ("dt",), ("m", 7)]
    for t in range(NT):
        u += [("S", t, g) for g in range(4)] + [("z", t, 0), ("z", t, 1), ("m", 8 + t)]
        u += [("PT", t, j) for j in range(2 * (t + 1))] + [("O", t)]
    u += [("ga", 0), ("ga", 1), ("m", 10), ("ga", 2), ("ga", 3), ("m", 11)]
    u += [("xT", t, j) for t in range(NT) for j in range(2)] + [("BT",), ("acum",)]
    u += [("cb", c) for c in range(2)] + [("row", 0, j) for j in range(4)] + [("ga", 4)]
    u += [("state", g) for g in range(SG)]
    u += [("yi", 0, g) for g in range(SG)] + [("row", 1, j) for j in range(4)] + [("ga", 5)]
    u += [("yx", g) for g in range(SG)] + [("yi", 1, g) for g in range(SG)] + [("ga", 6), ("ga", 7)]
    u += [("ya", p) for p in range(4)]
    u += [("yT", t, j) for t in range(NT) for j in range(2)]
    u += [("ys", p) for p in range(4)]
    u += [("x1", p) for p in range(4)] + [("ss", 2)]
    u += [("tok", t, j) for t in range(NT) for j in range(2)]
    u += [("rl",), ("cum",), ("GT",)] + [("hg", j) for j in range(2)] + [("yb", p) for p in range(4)]
    return u


def front_slots():
    s = [("ada", j) for j in range(4)]
    s += [("win", 0), ("win", 1), ("ada", 4), ("win", 2), ("ada", 5), ("win", 3), ("ada", 6), ("wkv",), ("win", 4)]
    s += [("ada", 7), ("win", 5), ("win", 6), ("ada", 8), ("win", 7), ("ada", 9), ("gate", 0), ("ada", 10)]
    s += [("gate", 1), ("ada", 11), ("gate", 2), ("gate", 3), ("wo",), ("wso", 0), ("wso", 1)]
    s += [("wout", 0), ("wout", 1)]
    return s


WIN_LAST = [("q", 1), ("qi", 0), ("kw", 1), ("xbc", 1), ("xbc", 3), ("xbc", 5), ("z", 0, 1), ("z", 1, 1)]
PAIR_BANKS = [("g", 0), ("u", 0), ("g", 1), ("u", 1), ("sT",), ("aT", 0), ("dn", 0), ("dn", 1), ("aT", 1),
              ("hg", 0), ("hg", 1)] + [("y", p) for p in range(4)]
PAIR_SLOTS = [(w, half, e) for half in range(2) for w in ("wg", "wu") for e in range(2)] + \
             [("wd", kh, e) for kh in range(2) for e in range(2)]


def layer_banks():
    u = [("ss", 0)]
    u += [("gates",)] + [("mqk", p) for p in range(4)] + [("aq", t) for t in range(NT)] + [("bc",)]
    u += [("ak", t) for t in range(NT)] + [("r", 0, d) for d in range(2)]
    u += [("qk", c) for c in range(2)] + [("kt", t) for t in range(NT)] + [("mv", t) for t in range(NT)]
    u += [(n, t) for t in range(NT) for n in ("qT", "kT")] + [("S", 0, g) for g in range(4)]
    u += [("cT", 0, d) for d in range(2)] + [("num", 0, j) for j in range(4)] + [("st", j) for j in range(4)]
    u += [("r", 1, d) for d in range(2)] + [("av", t) for t in range(NT)] + [("PT", 0, j) for j in range(4)]
    u += [("O", 0)] + [("S", 1, g) for g in range(4)]
    u += [("cT", 1, d) for d in range(2)] + [("num", 1, j) for j in range(4)] + [("ix", j) for j in range(4)]
    u += [("mo", p) for p in range(2)] + [("PT", 1, j) for j in range(4)] + [("O", 1)]
    u += [("hT", t) for t in range(NT)]
    u += [("mix", p) for p in range(4)] + [("ss", 1), ("ss", 2)]
    u += [("up", c) for c in range(FC)]
    u += [("down", c) for c in range(KC)] + [("ss", 3)]
    return u


LAYER_SLOTS = [("win", j) for j in (3, 4, 0, 1, 5, 2, 6)] + [("wout", j) for j in range(2)] + \
              [("up", j) for j in range(11)] + [("down", c, h) for c in range(4) for h in range(2)]
assert len(PAIR_SLOTS) % MOE_SLOTS == 0 and len(LAYER_SLOTS) % SLOTS == 0


def col(v):
    v = np.asarray(v)
    return np.moveaxis(v.reshape(*v.shape[:-1], -1, P), -1, 0).reshape(P, -1)


def lay_out(i):
    i = {k: np.asarray(v) for k, v in i.items()}
    rows = lambda v: np.broadcast_to(v.reshape(1, -1), (P, v.size))
    two = lambda v: np.concatenate([v, v]).reshape(P, 1)
    rel = np.zeros((P, HEADS), np.float32)
    rel[:BUCKETS] = i["rel_bias"]
    params = np.concatenate(
        [col(i["c"][0]), col(i["norm_mix"][0]), col(i["norm_ffn"][0]), col(i["b_ada"][0]),
         i["conv_w"][0].reshape(4, NX, P).transpose(2, 1, 0).reshape(P, -1), col(i["conv_b"][0]),
         col(i["kv_norm"][0]), two(i["q_norm"][0]), two(i["k_norm"][0]), two(i["idx_k_ln_w"][0]),
         two(i["idx_k_ln_b"][0]), col(i["ssm_norm"][0]), rows(i["dt_bias"][0]), rows(i["a_log"][0]),
         rows(i["d_skip"][0]), rows(i["b_router"][0]), rel], axis=1)
    params2 = np.stack([np.concatenate(
        [col(i["mix_pre_g_2"][l]), col(i["mix_post_g_2"][l]), col(i["ffn_pre_g_2"][l]), col(i["ffn_post_g_2"][l]),
         i["mlstm_conv_w_2"][l].reshape(5, 8, P).transpose(2, 1, 0).reshape(P, -1), col(i["mlstm_conv_b_2"][l]),
         col(i["mlstm_head_g_2"][l]), i["ffn_conv_w_2"][l].reshape(3, 2 * FC, P).transpose(2, 1, 0).reshape(P, -1),
         col(i["ffn_conv_b_2"][l]), rows(i["mlstm_gate_b_2"][l])], axis=1) for l in range(LAYERS)])
    return {
        "xT": np.ascontiguousarray(i["x"][0].reshape(L, KC, P).transpose(2, 1, 0)),
        "consts": constants(), "params": np.ascontiguousarray(params), "params2": np.ascontiguousarray(params2),
        "w_ada": i["w_ada"][0], "w_in": i["w_in"][0], "w_kv_up": i["w_kv_up"][0], "w_attn_o": i["w_attn_o"][0],
        "w_ssm_o": i["w_ssm_o"][0], "w_out": i["w_out"][0], "w_router": i["w_router"][0], "w_gu": i["w_gu"][0],
        "b_gu": i["b_gu"][0], "w_dn": i["w_dn"][0], "b_dn": i["b_dn"][0],
        "w_in_2": i["w_in_2"], "w_out_2": i["w_out_2"], "w_up_2": i["w_up_2"], "w_down_2": i["w_down_2"],
    }


INPUTS = ["xT", "consts", "params", "params2", "w_ada", "w_in", "w_kv_up", "w_attn_o", "w_ssm_o", "w_out", "w_router",
          "w_gu", "b_gu", "w_dn", "b_dn", "w_in_2", "w_out_2", "w_up_2", "w_down_2"]



class Arena:

    def __init__(self, ap, at=0):
        self.ap, self.at = ap, at

    def take(self, *dims):
        n = int(np.prod(dims))
        assert self.at + n <= self.ap.shape[1], (self.at, n, self.ap.shape)
        v = self.ap[:, self.at:self.at + n]
        self.at += n
        if len(dims) == 2:
            v = v.rearrange("p (a b) -> p a b", a=dims[0])
        if len(dims) == 3:
            v = v.rearrange("p (a b c) -> p a b c", a=dims[0], b=dims[1])
        return v


def matmul(pe, out, lhsT, rhs, first=True, last=True, **kw):
    return pe.matmul(out, lhsT, rhs, start=first, stop=last, **kw)


def rows(ap, n):
    return ap.unsqueeze(2).to_broadcast([ap.shape[0], ap.shape[1], n])


def across(ap, n):
    return ap.unsqueeze(1).to_broadcast([ap.shape[0], n, ap.shape[1]])


class Memory:

    def __init__(self, nc, ctx):
        sb = lambda name, n: ctx.enter_context(nc.sbuf_tensor(name, [P, n], F32))
        self.ring = sb("ring", SLOTS * SLOT)
        self.xT = sb("residual", KC * L)[:, :].rearrange("p (k t) -> p k t", k=KC)
        self.h = sb("normed", KC * L)[:, :].rearrange("p (k t) -> p k t", k=KC)
        self.consts, self.params = sb("consts_sb", CONSTS.n), sb("params_sb", PARAMS.n)
        self.mod, self.small, self.route = sb("mod_sb", 48), sb("small", 1024), sb("route", 512)
        self.flag = ctx.enter_context(nc.sbuf_tensor("flag", [P, 1], I32))
        self.work = sb("work", WORK)
        assert LAYERS * PARAMS2.n <= P + NT * L and LAYERS * KC * 16 <= 384
        self.staged = self.consts[:, CONSTS.at["ssd_mask"][0]:][:, 0:LAYERS * PARAMS2.n]
        self.staged_gates = self.consts[:, CONSTS.at["bucket"][0]:][:, 0:LAYERS * KC * 16]
        self.staged_in = ctx.enter_context(nc.semaphore("staged_in"))
        self.psum = ctx.enter_context(nc.psum_tensor("psum", [P, BANKS, 512], F32))

    def K(self, name, rows=P):
        return CONSTS.of(self.consts, name, rows)

    def prm(self, name, rows=P):
        return PARAMS.of(self.params, name, rows)

    def slot(self, i, *dims):
        n = int(np.prod(dims))
        ring, at = (self.ring, i * SLOT) if i < SLOTS else (self.work, WORK - (MOE_SLOTS - i) * SLOT)
        v = ring[:, at:at + n]
        return v.rearrange("p (a b) -> p a b", a=dims[0])


WORK = 26800


PAIRS_OF_HEADS = (0, 1, 4, 5)


class Experts:

    def __init__(self, mem, sem, tag):
        self.picked = sem("picked" + tag)
        self.rows_ready = sem("rows_ready" + tag)
        self.clipped = sem("clipped" + tag)
        self.sig_ready = sem("sig_ready" + tag)
        self.act_ready = sem("act_ready" + tag)
        self.bias_in = sem("bgu_in" + tag)
        self.down_half = sem("down_half" + tag)
        self.zeroed = sem("zeroed" + tag)
        self.moved = sem("moved" + tag)
        self.step = sem("experts_step" + tag)
        self.mem = mem
        R = Arena(mem.route)
        self.lr, self.mask, self.tm, self.rank, self.ex = (R.take(NT, E) for _ in range(5))
        self.place, self.gate = R.take(NT, E + 2), R.take(NT, E + 2)
        self.flag = mem.flag[:, :]
        A = Arena(mem.work)
        self.h_tok = A.take(NT, D)
        self.y_sum = A.take(KC, L)
        self.hgT, self.actT = A.take(KC, P), A.take(KC, P)
        self.g, self.u = A.take(2, 512), A.take(2, 512)
        self.act, self.out = A.take(2, 512), A.take(2, 512)
        self.one_hot, self.weighted = A.take(NT, P), A.take(NT, P)
        self.wT = A.take(1, L)[:, 0]
        self.gateT = A.take(1, L)[:, 0]
        self.b_gu = A.take(1, 2 * DE)[:, 0]
        self.b_dn = Arena(mem.work, WORK - (MOE_SLOTS - SLOTS) * SLOT - D).take(1, D)[:, 0]

    def load_weights(self, sp, io, S, B, slot, p, it=None):
        first = it is None
        it = 0 if first else it
        before = lambda *name: (B.ready(*name, it=it)[0], B.ready(*name, it=it)[1] - B.per[B.no(name)])
        used = [before("u", 1), (self.down_half, it), before("dn", 1), B.ready("g", 0, it=it), B.ready("u", 0, it=it),
                B.ready("g", 1, it=it)]
        for i, name in enumerate(PAIR_SLOTS):
            kind, half, e = name
            if e == 0 and not (first and i < MOE_SLOTS):
                sp.wait_ge(*used[i // 2])
            if kind == "wd":
                src = io["w_dn"][bass.ds(2 * p + e, 1), half * 512:half * 512 + 512, :]
                dst = slot(S.no(name), 4, 1024)
            else:
                c = half * 512 + (DE if kind == "wu" else 0)
                src = io["w_gu"][bass.ds(2 * p + e, 1), :, c:c + 512]
                dst = slot(S.no(name), KC, 512)
            sp.dma_start(dst, src.rearrange("a (k p) n -> p (a k) n", p=P)).then_inc(*S.fills(*name))

    def load_biases(self, pool, io, B, p, it):
        full, n = B.ready("u", 1, it=it)
        pool.wait_ge(full, n - B.per[B.no(("u", 1))])
        pool.dma_start(self.b_gu[0:2, :], io["b_gu"][bass.ds(2 * p, 2), :]).then_inc(self.bias_in, 16)

    def more_rounds(self, eng):
        return eng.value_load(self.flag[0:1, 0:1], min_val=0, max_val=1) > 0

    def pick(self, dve, e2, B=None, it=0):
        if B is not None:
            dve.wait_ge(*B.ready("sT", it=it))
        for t in range(NT):
            for e in range(2):
                c = slice(e * CAP, (e + 1) * CAP)
                one = lambda v: v[:, t, bass.ds(2 * e2 + e, 1)]
                dve.tensor_scalar(self.one_hot[:, t, c], self.mem.K("slot_no"), one(self.place), None, ALU.is_equal)
                ins = dve.tensor_scalar(self.weighted[:, t, c], self.mem.K("slot_no"), one(self.place), one(self.gate),
                                        ALU.is_equal, ALU.mult)
        ins.then_inc(self.picked, 1)

    def gather(self, pe, B, psum, it):
        pe.wait_ge(self.picked, it + 2)
        it = 0 if isinstance(it, int) and it < 0 else it
        for j in range(2):
            pe.wait_ge(*B.empty("hg", j, it=it))
            for i in range(4):
                k = 4 * j + i
                for t in range(NT):
                    ins = matmul(pe, psum[:, B.no(("hg", j)), i * P:(i + 1) * P], self.h_tok[:, t, k * P:(k + 1) * P],
                                 self.one_hot[:, t], t == 0, t == NT - 1)
            ins.then_inc(*B.fills("hg", j))

    def take_gathered(self, act, B, psum, it=0):
        for j in range(2):
            act.wait_ge(*B.ready("hg", j, it=it))
            act.activation(self.hgT[:, 4 * j:4 * j + 4], psum[:, B.no(("hg", j))].rearrange("p (a b) -> p a b", a=4), ACT.Copy)\
               .then_inc(*B.frees("hg", j))
            act.wait_ge(*B.released("hg", j, it=it))
        act.nop().then_inc(self.rows_ready, 1)

    def products(self, pe, mem, B, S, it):
        psum, K = mem.psum, mem.K
        pe.wait_ge(self.rows_ready, it + 1)
        pe.wait_ge(self.bias_in, it * 16 + 16)
        for half in range(2):
            for i, name in enumerate((("g", half), ("u", half))):
                b = psum[:, B.no(name)]
                pe.wait_ge(*B.empty(*name, it=it))
                pe.matmul(b, K("pair_row", 2), self.b_gu[0:2, i * DE + half * 512:i * DE + half * 512 + 512],
                          start=True, stop=False, skip_group_check=True)
                ws = []
                for e in range(2):
                    s = (("wg", "wu")[i], half, e)
                    pe.wait_ge(*S.ready(*s, it=it))
                    ws.append(mem.slot(S.no(s), KC, 512))
                for k in range(KC):
                    for e in range(2):
                        r = slice(e * CAP, (e + 1) * CAP)
                        ins = pe.matmul(b[r], self.hgT[:, k, r], ws[e][:, k], start=False, stop=k == KC - 1,
                                        skip_group_check=True)
                ins.then_inc(*B.fills(*name))
        pe.wait_ge(*B.empty("sT", it=it))
        for t in range(NT):
            ins = pe.transpose(psum[:, B.no(("sT",)), t * P:(t + 1) * P], self.weighted[:, t], K("ident"))
        ins.then_inc(*B.fills("sT"))
        for dh in range(2):
            pe.wait_ge(*B.empty("dn", dh, it=it))
        for half in range(2):
            pe.wait_ge(self.act_ready, it * 2 + half + 1)
            pe.wait_ge(*B.empty("aT", half, it=it))
            for i in range(4):
                ins = pe.transpose(psum[:, B.no(("aT", half)), i * P:(i + 1) * P], self.act[:, half, i * P:(i + 1) * P], K("ident"))
            ins.then_inc(*B.fills("aT", half))
            pe.wait_ge(*B.released("aT", half, it=it))
            ws = []
            for e in range(2):
                pe.wait_ge(*S.ready("wd", half, e, it=it))
                ws.append(mem.slot(S.no(("wd", half, e)), 4, 1024))
            for k in range(4):
                for dh in range(2):
                    for e in range(2):
                        r = slice(e * CAP, (e + 1) * CAP)
                        ins = pe.matmul(psum[r, B.no(("dn", dh))], self.actT[:, 4 * half + k, r], ws[e][:, k, dh * 512:dh * 512 + 512],
                                        start=half == 0 and k == 0, stop=half == 1 and k == 3, skip_group_check=True)
                    if half == 1 and k == 3:
                        ins.then_inc(*B.fills("dn", dh))
            if half == 0:
                ins.then_inc(self.down_half, 1)

    def act_part(self, act, B, psum, it):
        for half in range(2):
            act.wait_ge(self.clipped, it * 2 + half + 1)
            act.activation(self.u[:, half], self.g[:, half], ACT.Sigmoid, scale=ALPHA).then_inc(self.sig_ready, 1)
        act.wait_ge(*B.ready("sT", it=it))
        act.activation(self.wT, psum[:, B.no(("sT",)), 0:L], ACT.Copy).then_inc(*B.frees("sT"))
        for half in range(2):
            act.wait_ge(*B.ready("aT", half, it=it))
            act.activation(self.actT[:, 4 * half:4 * half + 4], psum[:, B.no(("aT", half))].rearrange("p (a b) -> p a b", a=4),
                           ACT.Copy).then_inc(*B.frees("aT", half))
        for dh in range(2):
            act.wait_ge(*B.ready("dn", dh, it=it))
            act.activation(self.out[:, dh], psum[:, B.no(("dn", dh))], ACT.Copy).then_inc(*B.frees("dn", dh))

    def combine(self, pe, B, psum, it):
        pe.wait_ge(*B.released("dn", 1, it=it))
        pe.wait_ge(*B.released("dn", 0, it=it))
        pe.wait_ge(*B.released("sT", it=it))
        for p in range(4):
            pe.wait_ge(*B.empty("y", p, it=it))
            for i in range(2):
                k = 2 * p + i
                ins = matmul(pe, psum[:, B.no(("y", p)), i * L:(i + 1) * L],
                             self.out[:, k // 4, (k % 4) * P:(k % 4 + 1) * P], self.wT)
            ins.then_inc(*B.fills("y", p))

    def glu(self, dve, B, psum, it):
        for half in range(2):
            g, u, act = self.g[:, half], self.u[:, half], self.act[:, half]
            dve.wait_ge(*B.ready("g", half, it=it))
            dve.tensor_scalar(g, psum[:, B.no(("g", half))], LIMIT, None, ALU.min).then_inc(*B.frees("g", half))
            dve.wait_ge(*B.released("g", half, it=it))
            dve.nop().then_inc(self.clipped, 1)
            dve.wait_ge(*B.ready("u", half, it=it))
            dve.tensor_scalar(act, psum[:, B.no(("u", half))], LIMIT, -LIMIT, ALU.min, ALU.max).then_inc(*B.frees("u", half))
            dve.wait_ge(self.sig_ready, it * 2 + half + 1)
            dve.tensor_tensor(g, g, u, ALU.mult).then_inc(self.step, 1)
            dve.wait_ge(*B.released("u", half, it=it))
            dve.wait_ge(self.step, it * 2 + half + 1)
            dve.scalar_tensor_tensor(out=act, in0=act, scalar=1.0, in1=g, op0=ALU.add, op1=ALU.mult)\
               .then_inc(self.act_ready, 1)

    def add_up(self, dve, B, psum, y_sum, it):
        for p in range(4):
            dve.wait_ge(*B.ready("y", p, it=it))
            v = y_sum[:, 2 * p:2 * p + 2]
            dve.tensor_tensor(v, v, psum[:, B.no(("y", p))].rearrange("p (a b) -> p a b", a=2), ALU.add)\
               .then_inc(*B.frees("y", p))
            if p == 3:
                dve.wait_ge(*B.released("y", p, it=it))


def first_block(nc, ctx, io, mem):
    sem = lambda n: ctx.enter_context(nc.semaphore(n))
    xT, h, psum, mod = mem.xT, mem.h, mem.psum, mem.mod
    K, prm, slot = mem.K, mem.prm, mem.slot
    line = nc.dram_tensor("bias_line", [HEADS, P, 384], F32, kind="Internal").ap()

    bank_full = [sem(f"bank_full{b}") for b in range(BANKS)]
    bank_free = [sem(f"bank_free{b}") for b in range(BANKS)]
    slot_full = [sem(f"slot_full{b}") for b in range(MOE_SLOTS)]
    B = Uses(bank_full, bank_free, front_banks())
    S = Uses(slot_full[0:SLOTS], slot_full[0:SLOTS], front_slots(), inc=16)
    BP = Uses(bank_full, bank_free, PAIR_BANKS, base=B.after())
    SP = Uses(slot_full, slot_full, PAIR_SLOTS, inc=16, base=S.after() + [0] * (MOE_SLOTS - SLOTS))

    params_in = sem("params_in_1")
    small_in = sem("small_in")
    tables_in = sem("tables_in")
    narrow_in = sem("narrow_in")
    bdn_in = sem("bdn_in")
    act_step, dve_step = sem("act_step"), sem("dve_step")
    cond_ready = sem("cond_ready")
    ada_sum = sem("ada_sum")
    mod_ready = sem("mod_ready")
    sq_ready = sem("sq_ready")
    var_ready = sem("var_ready")
    rstd_ready = sem("rstd_ready")
    scaled_ready = sem("scaled_ready")
    h_ready = sem("h_ready")
    tok_ready = sem("tok_ready")
    line_ready, line_out, bias_in = sem("line_ready"), sem("line_out"), sem("bias_in")
    relu_used = sem("relu_used")
    logits_ready, exp_ready, probs_ready = sem("logits_ready"), sem("exp_ready"), sem("probs_ready")
    conv_ready, silu_ready = sem("conv_ready"), sem("silu_ready")
    dt_abs, dt_log, dta_ready = sem("dt_abs"), sem("dt_log"), sem("dta_ready")
    acum_ready, decay_exp, xdt_ready = sem("acum_ready"), sem("decay_exp"), sem("xdt_ready")
    seg_ready, seg_exp, w_ready = sem("seg_ready"), sem("seg_exp"), sem("w_ready")
    y_ready = sem("y_ready")
    mixed_ready, x1_ready = sem("mixed_ready"), sem("x1_ready")
    route_ready, route_exp, mask_ready, gates_ready = (sem(n) for n in ("route_ready", "route_exp", "mask_ready", "gates_ready"))
    X = Experts(mem, sem, "")
    y_sum = X.y_sum

    A = Arena(mem.work)
    xbc = A.take(NX, L + 3)
    xc = A.take(NX, L)
    z = A.take(NT, SI)
    sig = A.take(2 * KC, L)
    attnT = A.take(4, L)
    acc = A.take(3, 512)
    w_dt = A.take(KC, SH)
    w_r = A.take(KC, E)
    at = A.at
    qkt = A.take(2, NT, AW)
    bias = qkt.rearrange("p a t n -> p (a t n)").rearrange("p (h s) -> p h s", h=HEADS)
    q_tok, k_tok = qkt[:, 0], qkt[:, 1]
    v_tok = A.take(NT, AW)
    qT, kT, qiT = A.take(4, L), A.take(4, L), A.take(4, L)
    kiT = A.take(1, L)[:, 0]
    lg_at = A.at
    lg = A.take(HEADS, L)
    keep, score = A.take(NT, L), A.take(NT, L)
    pt_at = A.at
    pt = A.take(16, P)
    A2 = Arena(mem.work, lg_at)
    kvl, ki2, kvT, kw = A2.take(NT, 256), A2.take(NT, P), A2.take(2, L), A2.take(NT, 72)
    tmp = Arena(mem.work, pt_at).take(2, 512)
    relu = Arena(mem.work, pt_at).take(2, 2, L)
    top = Arena(mem.work, pt_at + 1024).take(4, L)
    A3 = Arena(mem.work, at)
    xs, xdt, seg = A3.take(NT, SI), A3.take(NT, SI), A3.take(SH, P)
    yT = A3.take(KC, L)
    Bt, cbT, state, xdec = A3.take(SG, P), A3.take(NT, SG, P), A3.take(SG, 512), A3.take(1, SI)[:, 0]
    y_tmp = xdec
    y_tok = Arena(mem.work).take(NT, SI)
    mixed = z.rearrange("p t n -> p (t n)").rearrange("p (k n) -> p k n", k=KC)
    line_sb = attnT.rearrange("p a b -> p (a b)")[0:HEADS, 0:384]
    SM = Arena(mem.small)
    cond, st, rs = SM.take(KC), SM.take(64), SM.take(64)
    a1, a2 = SM.take(KC), SM.take(KC)
    m8, cnt = SM.take(NT, 8), SM.take(8)
    wi = SM.take(NT, 8)
    mx, sm = SM.take(8), SM.take(8)
    ea = SM.take(SH)
    dtr, dtv, dt, dta, acum, nac, alast, dec, eac = (SM.take(NT, SH) for _ in range(9))
    rstd = SM.take(L)

    ident, ones = K("ident"), K("ones")[:, 0:P]

    def kpm(ap):
        return ap.rearrange("(k p) n -> p k n", p=P)

    block = ctx.enter_context(nc.Block())

    @block.sync
    def _(sp):
        sp.dma_start(mem.params[:, :], io["params"]).then_inc(params_in, 16)
        early = CONSTS.at["ssd_mask"][0]

        order = front_slots()

        def slot_used(name):
            kind, j = name[0], name[-1]
            if kind == "ada":
                return ada_sum, j + 1
            return B.ready(*{"win": WIN_LAST[j] if kind == "win" else None, "wkv": ("kv_up", 1, 1), "wo": ("ya", 3),
                             "gate": ("ga", 1 + 2 * j) if kind == "gate" else None,
                             "wso": ("ys", 1 + 2 * j) if kind == "wso" else None,
                             "wout": ("x1", 1 + 2 * j) if kind == "wout" else None}[kind])

        def load(src, *name):
            if order.index(name) >= SLOTS:
                sp.wait_ge(*slot_used(order[order.index(name) - SLOTS]))
            k, n = src.shape[0] // P, src.shape[1]
            sp.dma_start(slot(S.no(name), k, n), kpm(src)).then_inc(*S.fills(*name))

        win = [(C_Q, 512), (C_KV, 512), (C_QI + 256, 328)] + [(C_XBC + 512 * j, 512) for j in range(3)] + \
              [(C_Z + 512 * j, 512) for j in range(2)]
        for name in front_slots():
            kind, j = name[0], name[-1]
            if kind == "ada":
                load(io["w_ada"][:, 512 * j:512 * j + 512], *name)
                if j == 0:
                    sp.dma_start(xT, io["xT"]).then_inc(small_in, 16)
                    sp.dma_start(mem.consts[:, 0:early], io["consts"][:, 0:early]).then_inc(small_in, 16)
                if j == 3:
                    sp.dma_start(mem.consts[:, early:], io["consts"][:, early:]).then_inc(tables_in, 16)
                    sp.dma_start(w_dt, kpm(io["w_in"][:, C_DT:C_DT + SH])).then_inc(narrow_in, 16)
                    sp.dma_start(w_r, kpm(io["w_router"])).then_inc(narrow_in, 16)
            elif kind == "win":
                load(io["w_in"][:, win[j][0]:win[j][0] + win[j][1]], *name)
            elif kind == "wkv":
                load(io["w_kv_up"], *name)
            elif kind == "gate":
                load(io["w_in"][:, C_GATE + 512 * j:C_GATE + 512 * j + 512], *name)
            elif kind == "wo":
                load(io["w_attn_o"], *name)
            elif kind == "wso":
                load(io["w_ssm_o"][:, 512 * j:512 * j + 512], *name)
            elif kind == "wout":
                load(io["w_out"][:, 512 * j:512 * j + 512], *name)
        sp.wait_ge(*slot_used(("wout", 1)))
        sp.wait_ge(mixed_ready, 1)
        X.load_weights(sp, io, SP, BP, slot, 0)
        with sp.Fori(1, PAIRS) as p:
            X.load_weights(sp, io, SP, BP, slot, p, p)
        with sp.If(X.more_rounds(sp)):
            with sp.Fori(1, ROUNDS) as r:
                with sp.Fori(0, PAIRS) as p:
                    X.load_weights(sp, io, SP, BP, slot, p, r * PAIRS + p)

    @block.gpsimd
    def _(pool):
        pool.memset(xbc[:, :, 0:3], 0.0).then_inc(X.zeroed, 1)
        pool.wait_ge(line_ready, 1)
        pool.dma_start(line, line_sb.unsqueeze(1).to_broadcast([HEADS, P, 384])).then_inc(line_out, 16)
        pool.wait_ge(line_out, 16)
        pool.wait_ge(*B.ready("kT", 1))
        toeplitz = bass.AP(tensor=line.tensor, offset=P - 1, ap=[[383, P], [384 * P, HEADS], [1, L]])
        pool.dma_start(bias, toeplitz).then_inc(bias_in, 16)
        pool.wait_ge(gates_ready, 1)
        for l in range(LAYERS):
            n = KC * 16
            pool.dma_start(mem.staged[:, l * PARAMS2.n:(l + 1) * PARAMS2.n], io["params2"][l]).then_inc(mem.staged_in, 16)
            pool.dma_start(mem.staged_gates[:, l * n:(l + 1) * n].rearrange("p (k n) -> p k n", k=KC),
                           kpm(io["w_in_2"][l, :, 3584:3600])).then_inc(mem.staged_in, 16)
        with pool.Fori(0, PAIRS) as p:
            X.load_biases(pool, io, BP, p, p)
        with pool.If(X.more_rounds(pool)):
            with pool.Fori(1, ROUNDS) as r:
                with pool.Fori(0, PAIRS) as p:
                    X.load_biases(pool, io, BP, p, r * PAIRS + p)

    @block.tensor
    def _(pe):
        pe.wait_ge(params_in, 16)
        pe.wait_ge(small_in, 32)

        def bank(*name):
            return psum[:, B.no(name)]

        def sum_mod(j):
            pe.wait_ge(ada_sum, j + 1)
            pe.wait_ge(*B.empty("m", j))
            for i in range(4):
                ins = matmul(pe, bank("m", j)[:, i:i + 1], acc[:, j % 3, i * P:(i + 1) * P], ones[:, 0:1])
            ins.then_inc(*B.fills("m", j))

        def sum_squares(n, sq):
            pe.wait_ge(*B.empty("ss", n))
            for k in range(KC):
                if k % 2 == 0:
                    pe.wait_ge(sq_ready, 4 * (n - 1) + k // 2 + 1)
                ins = matmul(pe, bank("ss", n)[:, 0:L], ones, sq[:, k], k == 0, k == KC - 1)
            ins.then_inc(*B.fills("ss", n))

        def by_token(name, w, c0, n, lhs=h, kc=KC):
            for t in range(NT):
                pe.wait_ge(*B.empty(*name, t))
                for k in range(kc):
                    if name == ("q",) and t == 0:
                        pe.wait_ge(h_ready, k + 1)
                    ins = matmul(pe, bank(*name, t)[:, 0:n], lhs[:, k, t * P:(t + 1) * P], w[:, k, c0:c0 + n],
                                 k == 0, k == kc - 1)
                ins.then_inc(*B.fills(*name, t))
            return ins

        def by_feature(name, w, c0, rhs=h, kc=KC):
            pe.wait_ge(*B.empty(*name))
            for i in range(2):
                for k in range(kc):
                    ins = matmul(pe, bank(*name)[:, i * L:(i + 1) * L], w[:, k, c0 + i * P:c0 + (i + 1) * P], rhs[:, k],
                                 k == 0, k == kc - 1)
            ins.then_inc(*B.fills(*name))

        def wait_slot(*name):
            pe.wait_ge(*S.ready(*name))
            return slot(S.no(name), KC, 512)

        def transposes(name, blocks):
            pe.wait_ge(*B.empty(*name))
            for i, b in enumerate(blocks):
                ins = pe.transpose(bank(*name)[0:b.shape[1], i * P:(i + 1) * P], b, ident)
            ins.then_inc(*B.fills(*name))

        sum_mod(0)
        sum_squares(1, sig[:, 0:KC])
        for j in range(1, 4):
            sum_mod(j)
        by_token(("q",), wait_slot("win", 0), 0, 512)
        w = wait_slot("win", 1)
        by_token(("kv",), w, 0, 256)
        by_feature(("qi", 0), w, 256)
        pe.wait_ge(*S.ready("win", 2))
        w = slot(S.no(("win", 2)), KC, 328)
        by_feature(("qi", 1), w, 0)
        by_token(("kw",), w, 256, 72)
        pe.wait_ge(*B.empty("bvec"))
        pe.wait_ge(tables_in, 16)
        matmul(pe, bank("bvec")[0:HEADS, 0:384], prm("rel_bias", BUCKETS), K("bucket", BUCKETS)).then_inc(*B.fills("bvec"))
        sum_mod(4)

        def conv_inputs(j):
            w = wait_slot("win", 3 + j)
            by_feature(("xbc", 2 * j), w, 0)
            by_feature(("xbc", 2 * j + 1), w, 256)

        def pair_of_heads(t, name, q, keys, n):
            for g, h0 in enumerate(PAIRS_OF_HEADS):
                pe.wait_ge(*B.empty(name, t, g))
                for i in range(2):
                    hd = h0 + 2 * i
                    rr = slice(64 * (hd % 2), 64 * (hd % 2) + 64)
                    ins = matmul(pe, bank(name, t, g)[:, i * n:(i + 1) * n], q[rr, hd // 2, t * P:(t + 1) * P], keys(rr, hd))
                ins.then_inc(*B.fills(name, t, g))

        conv_inputs(0)
        sum_mod(5)
        pe.wait_ge(tok_ready, 1)
        transposes(("kvT",), [kvl[:, t, c * P:(c + 1) * P] for c in range(2) for t in range(NT)])
        for t in range(NT):
            transposes(("qT", t), [q_tok[:, t, c * P:(c + 1) * P] for c in range(4)])
        transposes(("kiT",), [ki2[:, t] for t in range(NT)])
        pe.wait_ge(*S.ready("wkv"))
        w = slot(S.no(("wkv",)), 2, 1024)
        pe.wait_ge(*B.released("kvT"))
        for j in range(2):
            by_token(("kv_up", j), w, 512 * j, 512, kvT, 2)
        pe.wait_ge(*B.released("kiT"))
        pe.wait_ge(*B.released("qi", 1))
        pair_of_heads(0, "dots", qiT, lambda rr, hd: kiT[rr, :], L)
        conv_inputs(1)
        sum_mod(6)
        pair_of_heads(1, "dots", qiT, lambda rr, hd: kiT[rr, :], L)
        pe.wait_ge(tok_ready, 2)
        for t in range(NT):
            transposes(("kT", t), [k_tok[:, t, c * P:(c + 1) * P] for c in range(4)])
        conv_inputs(2)
        pe.wait_ge(*B.empty("dt"))
        pe.wait_ge(narrow_in, 32)
        for t in range(NT):
            for k in range(KC):
                ins = matmul(pe, bank("dt")[:, t * SH:(t + 1) * SH], h[:, k, t * P:(t + 1) * P], w_dt[:, k], k == 0, k == KC - 1)
        ins.then_inc(*B.fills("dt"))
        sum_mod(7)
        pe.wait_ge(*B.released("kT", 1))
        for t in range(NT):
            nk = (t + 1) * P
            pair_of_heads(t, "S", qT, lambda rr, hd, nk=nk: kT[rr, hd // 2, 0:nk], nk)
            by_token(("z", t), wait_slot("win", 6 + t), 0, 512)
            sum_mod(8 + t)
            pe.wait_ge(probs_ready, t + 1)
            blocks = [(hd, s) for hd in range(HEADS) for s in range(t + 1)]
            for j in range(2 * (t + 1)):
                transposes(("PT", t, j), [lg[:, hd, s * P:(s + 1) * P] for hd, s in blocks[4 * j:4 * j + 4]])
            pe.wait_ge(*B.empty("O", t))
            pe.wait_ge(*B.released("PT", t, 2 * t + 1))
            for hd in range(HEADS):
                r = slice(64 * (hd % 2), 64 * (hd % 2) + 64)
                for s in range(t + 1):
                    ins = matmul(pe, bank("O", t)[r, (hd // 2) * P:(hd // 2 + 1) * P], v_tok[:, s, hd * HD:(hd + 1) * HD],
                                 pt[:, blocks.index((hd, s))], s == 0, s == t)
            ins.then_inc(*B.fills("O", t))
        for j in range(2):
            w = wait_slot("gate", j)
            by_feature(("ga", 2 * j), w, 0)
            by_feature(("ga", 2 * j + 1), w, 256)
            sum_mod(10 + j)
        for t in range(NT):
            for j in range(2):
                pe.wait_ge(silu_ready, 4 * j + 4)
                transposes(("xT", t, j), [xc[:, 4 * j + c, t * P:(t + 1) * P] for c in range(4)])
        pe.wait_ge(silu_ready, NX)
        transposes(("BT",), [xc[:, KC + g, 0:P] for g in range(SG)])
        pe.wait_ge(dta_ready, 1)
        pe.wait_ge(*B.empty("acum"))
        for c in range(NT):
            matmul(pe, bank("acum")[:, c * SH:(c + 1) * SH], K("tri_le"), dta[:, c])
            ins = matmul(pe, bank("acum")[:, (2 + c) * SH:(3 + c) * SH], ones, dta[:, c])
        ins.then_inc(*B.fills("acum"))
        for c in range(NT):
            pe.wait_ge(*B.empty("cb", c))
            for g in range(SG):
                ins = matmul(pe, bank("cb", c)[:, g * P:(g + 1) * P], xc[:, KC + g, c * P:(c + 1) * P],
                             xc[:, KC + SG + g, c * P:(c + 1) * P])
            ins.then_inc(*B.fills("cb", c))

        def cum_rows(c):
            for j in range(4):
                pe.wait_ge(*B.empty("row", c, j))
                for i in range(4):
                    hd = 4 * j + i
                    ins = matmul(pe, bank("row", c, j)[:, i * P:(i + 1) * P], acum[:, c, hd:hd + 1].to_broadcast([P, P]), ident)
                ins.then_inc(*B.fills("row", c, j))

        def intra(c):
            pe.wait_ge(w_ready, c + 1)
            for g in range(SG):
                pe.wait_ge(*B.empty("yi", c, g))
                for i in range(8):
                    hd = 8 * g + i
                    ins = matmul(pe, bank("yi", c, g)[:, i * 64:(i + 1) * 64], seg[:, hd], xdt[:, c, hd * 64:(hd + 1) * 64])
                ins.then_inc(*B.fills("yi", c, g))

        pe.wait_ge(acum_ready, 1)
        cum_rows(0)
        w_gate = wait_slot("gate", 2)
        by_feature(("ga", 4), w_gate, 0)
        pe.wait_ge(xdt_ready, 1)
        pe.wait_ge(*B.released("BT"))
        for g in range(SG):
            pe.wait_ge(*B.empty("state", g))
            matmul(pe, bank("state", g), Bt[:, g], xdec[:, g * 512:(g + 1) * 512]).then_inc(*B.fills("state", g))
        intra(0)
        cum_rows(1)
        by_feature(("ga", 5), w_gate, 256)
        for g in range(SG):
            pe.wait_ge(*B.empty("yx", g))
            pe.wait_ge(*B.released("state", g))
            matmul(pe, bank("yx", g), xc[:, KC + SG + g, P:2 * P], state[:, g]).then_inc(*B.fills("yx", g))
        intra(1)
        w = wait_slot("gate", 3)
        by_feature(("ga", 6), w, 0)
        by_feature(("ga", 7), w, 256)
        pe.wait_ge(*S.ready("wo"))
        pe.wait_ge(*B.released("O", 1))
        w = slot(S.no(("wo",)), 4, 1024)
        for p in range(4):
            by_feature(("ya", p), w, 256 * p, attnT, 4)
        for t in range(NT):
            pe.wait_ge(y_ready, t + 1)
            for j in range(2):
                transposes(("yT", t, j), [y_tok[:, t, (4 * j + c) * P:(4 * j + c + 1) * P] for c in range(4)])
        pe.wait_ge(*B.released("yT", 1, 1))
        for j in range(2):
            w = wait_slot("wso", j)
            by_feature(("ys", 2 * j), w, 0, yT)
            by_feature(("ys", 2 * j + 1), w, 256, yT)
        pe.wait_ge(mixed_ready, 1)
        for j in range(2):
            w = wait_slot("wout", j)
            by_feature(("x1", 2 * j), w, 0, mixed)
            by_feature(("x1", 2 * j + 1), w, 256, mixed)
        sum_squares(2, sig[:, 0:KC])
        for t in range(NT):
            for j in range(2):
                pe.wait_ge(h_ready, KC + 4 * j + 4)
                transposes(("tok", t, j), [h[:, 4 * j + c, t * P:(t + 1) * P] for c in range(4)])
        pe.wait_ge(*B.empty("rl"))
        for t in range(NT):
            for k in range(KC):
                ins = matmul(pe, bank("rl")[:, t * E:(t + 1) * E], h[:, k, t * P:(t + 1) * P], w_r[:, k], k == 0, k == KC - 1)
        ins.then_inc(*B.fills("rl"))
        pe.wait_ge(mask_ready, 1)
        pe.wait_ge(*B.empty("cum"))
        matmul(pe, bank("cum")[:, 0:E], K("tri_le"), X.mask[:, 0])
        matmul(pe, bank("cum")[:, E:2 * E], K("tri_le"), X.mask[:, 1], True, False)
        matmul(pe, bank("cum")[:, E:2 * E], ones, X.mask[:, 0], False, True)
        matmul(pe, bank("cum")[:, 2 * E:3 * E], ones, X.mask[:, 0], True, False)
        matmul(pe, bank("cum")[:, 2 * E:3 * E], ones, X.mask[:, 1], False, True).then_inc(*B.fills("cum"))
        pe.wait_ge(gates_ready, 1)
        transposes(("GT",), [X.gate[:, t, 0:E] for t in range(NT)])
        pe.wait_ge(*B.released("tok", 1, 1))
        X.gather(pe, B, psum, -1)
        pe.wait_ge(*B.released("GT"))
        pe.wait_ge(bdn_in, 16)
        for p in range(4):
            pe.wait_ge(*B.empty("yb", p))
            for i in range(2):
                k = 2 * p + i
                ins = matmul(pe, bank("yb", p)[:, i * L:(i + 1) * L], X.b_dn[0:E, k * P:(k + 1) * P], X.gateT[0:E, :])
            ins.then_inc(*B.fills("yb", p))
        with pe.Fori(0, PAIRS) as p:
            X.products(pe, mem, BP, SP, p)
            X.gather(pe, BP, psum, p)
            X.combine(pe, BP, psum, p)
        with pe.If(X.more_rounds(pe)):
            with pe.Fori(PAIRS, ROUNDS * PAIRS) as i:
                X.products(pe, mem, BP, SP, i)
                X.gather(pe, BP, psum, i)
                X.combine(pe, BP, psum, i)

    @block.scalar
    def _(act):
        step = Steps(act, act_step)
        act.wait_ge(params_in, 16)
        step(act.activation(ea, prm("a_log"), ACT.Exp))
        act.activation(cond, prm("c"), ACT.Silu).then_inc(cond_ready, 1)
        act.wait_ge(small_in, 32)
        for p in range(4):
            act.activation(sig[:, 2 * p:2 * p + 2], xT[:, 2 * p:2 * p + 2], ACT.Square).then_inc(sq_ready, 1)

        def take(out, in_, *name, func=ACT.Copy, **kw):
            act.wait_ge(*B.ready(*name))
            act.activation(out, in_, func, **kw).then_inc(*B.frees(*name))

        def bank(*name):
            return psum[:, B.no(name)]

        def two(v, n=2):
            return v.rearrange("p (a b) -> p a b", a=n)

        def root(n, out, in_):
            act.wait_ge(var_ready, n)
            act.activation(out, in_, ACT.Sqrt).then_inc(rstd_ready, 1)

        root(1, rstd, rstd)
        act.wait_ge(mod_ready, 1)
        for k in range(KC):
            act.wait_ge(scaled_ready, k + 1)
            act.activation(h[:, k], h[:, k], ACT.Identity, bias=mod[:, k:k + 1]).then_inc(h_ready, 1)
        for t in range(NT):
            take(q_tok[:, t], bank("q", t), "q", t)
        for t in range(NT):
            take(kvl[:, t], bank("kv", t)[:, 0:256], "kv", t)
        take(qiT[:, 0:2], two(bank("qi", 0)), "qi", 0)
        take(qiT[:, 2:4], two(bank("qi", 1)), "qi", 1)
        for t in range(NT):
            take(kw[:, t], bank("kw", t)[:, 0:72], "kw", t)
        act.wait_ge(X.zeroed, 1)

        def conv_inputs(j):
            for p in (2 * j, 2 * j + 1):
                take(xbc[:, 2 * p:2 * p + 2, 3:], two(bank("xbc", p)), "xbc", p)

        def index_relu(t):
            for g in range(4):
                n = 4 * t + g
                act.wait_ge(*B.ready("dots", t, g))
                if n >= 2:
                    act.wait_ge(relu_used, n - 1)
                elif n == 0:
                    act.wait_ge(tok_ready, 2)
                act.activation(relu[:, n % 2], two(bank("dots", t, g)), ACT.Relu).then_inc(*B.frees("dots", t, g))

        root(2, rs[:, 0:20], st[:, 0:20])
        conv_inputs(0)
        for j, dst in enumerate((k_tok, v_tok)):
            for t in range(NT):
                take(dst[:, t], bank("kv_up", j, t), "kv_up", j, t)
        root(3, rs[:, 20:36], st[:, 20:36])
        index_relu(0)
        conv_inputs(1)
        index_relu(1)
        conv_inputs(2)
        take(dtr, two(bank("dt")[:, 0:2 * SH]), "dt")
        act.wait_ge(dt_abs, 1)
        step(act.activation(dt, dt, ACT.Exp, scale=-1.0))
        act.activation(dt, dt, ACT.Ln, bias=1.0).then_inc(dt_log, 1)

        def gate(p):
            take(sig[:, 2 * p:2 * p + 2], two(bank("ga", p)), "ga", p, func=ACT.Sigmoid)

        for t in range(NT):
            nk = (t + 1) * P
            act.wait_ge(logits_ready, t + 1)
            act.activation(lg[:, :, 0:nk], lg[:, :, 0:nk], ACT.Exp).then_inc(exp_ready, 1)
            for i in range(NT):
                take(z[:, i, t * 512:(t + 1) * 512], bank("z", t, i), "z", t, i, func=ACT.Silu)
            for j in range(2 * (t + 1)):
                take(pt[:, 4 * j:4 * j + 4], two(bank("PT", t, j), 4), "PT", t, j)
            take(attnT[:, :, t * P:(t + 1) * P], two(bank("O", t), 4), "O", t)
        for p in range(4):
            gate(p)
        for k in range(NX):
            act.wait_ge(conv_ready, k + 1)
            act.activation(xc[:, k], xc[:, k], ACT.Silu).then_inc(silu_ready, 1)
        for t in range(NT):
            for j in range(2):
                take(xs[:, t, j * 512:(j + 1) * 512], bank("xT", t, j), "xT", t, j)
        take(Bt, two(bank("BT")[:, 0:2 * P]), "BT")
        act.wait_ge(acum_ready, 1)
        step(act.activation(dec, dec, ACT.Exp))
        act.activation(eac, acum, ACT.Exp).then_inc(decay_exp, 1)
        for c in range(NT):
            take(cbT[:, c], two(bank("cb", c)[:, 0:2 * P]), "cb", c)
        act.wait_ge(seg_ready, 4)
        act.activation(seg, seg, ACT.Exp).then_inc(seg_exp, 1)
        gate(4)
        for g in range(SG):
            take(state[:, g], bank("state", g), "state", g)
        act.wait_ge(seg_ready, 8)
        act.activation(seg, seg, ACT.Exp).then_inc(seg_exp, 1)
        gate(5)
        root(4, rs[:, 0:2], st[:, 0:2])
        root(5, rs[:, 2:4], st[:, 2:4])
        gate(6)
        gate(7)
        for t in range(NT):
            for j in range(2):
                act.wait_ge(*B.ready("yT", t, j))
                for c in range(4):
                    k = 4 * j + c
                    ins = act.activation(yT[:, k, t * P:(t + 1) * P], bank("yT", t, j)[:, c * P:(c + 1) * P], ACT.Copy,
                                         scale=prm("ssm_norm")[:, k:k + 1])
                ins.then_inc(*B.frees("yT", t, j))
        act.dma_start(X.b_dn[0:E, :], io["b_dn"]).then_inc(bdn_in, 16)
        for p in range(4):
            act.wait_ge(x1_ready, p + 1)
            act.activation(sig[:, 2 * p:2 * p + 2], xT[:, 2 * p:2 * p + 2], ACT.Square).then_inc(sq_ready, 1)
        root(6, rstd, rstd)
        act.wait_ge(mod_ready, 2)
        for k in range(KC):
            act.wait_ge(scaled_ready, KC + k + 1)
            act.activation(h[:, k], h[:, k], ACT.Identity, bias=mod[:, 24 + k:25 + k]).then_inc(h_ready, 1)
        for t in range(NT):
            for j in range(2):
                take(X.h_tok[:, t, j * 512:(j + 1) * 512], bank("tok", t, j), "tok", t, j)
        act.wait_ge(route_ready, 1)
        act.activation(X.ex, X.ex, ACT.Exp).then_inc(route_exp, 1)
        act.wait_ge(*B.ready("GT"))
        act.activation(X.gateT[0:E, :], bank("GT")[0:E, 0:L], ACT.Copy).then_inc(*B.frees("GT"))
        X.take_gathered(act, B, psum)
        for p in range(4):
            take(y_sum[:, 2 * p:2 * p + 2], two(bank("yb", p)), "yb", p)
        with act.Fori(0, PAIRS) as p:
            X.act_part(act, BP, psum, p)
            X.take_gathered(act, BP, psum, p)
        with act.If(X.more_rounds(act)):
            with act.Fori(PAIRS, ROUNDS * PAIRS) as i:
                X.act_part(act, BP, psum, i)
                X.take_gathered(act, BP, psum, i)

    @block.vector
    def _(dve):
        step = Steps(dve, dve_step)
        TS, TT, STT = dve.tensor_scalar, dve.tensor_tensor, dve.scalar_tensor_tensor

        def bank(*name):
            return psum[:, B.no(name)]

        def two(v, n=2):
            return v.rearrange("p (a b) -> p a b", a=n)

        def take(ins, *name):
            ins.then_inc(*B.frees(*name))
            dve.wait_ge(*B.released(*name))

        def signal(ins, sem, n):
            ins.then_inc(sem, 1)
            dve.wait_ge(sem, n)

        def take_mod(j):
            dve.wait_ge(*B.ready("m", j))
            take(TT(mod[:, 4 * j:4 * j + 4], bank("m", j)[:, 0:4], prm("b_ada")[:, 4 * j:4 * j + 4], ALU.add), "m", j)

        def inverse(ap, count):
            step(TS(ap, ap, 1.0 / count, EPS, ALU.mult, ALU.add))

        def product(j):
            dve.wait_ge(*S.ready("ada", j))
            if j >= 3:
                dve.wait_ge(*B.ready("m", j - 3))
            w, a = slot(S.no(("ada", j)), KC, 512), acc[:, j % 3]
            step(TS(a, w[:, 0], cond[:, 0:1], None, ALU.mult))
            for k in range(1, KC):
                ins = STT(out=a, in0=w[:, k], scalar=cond[:, k:k + 1], in1=a, op0=ALU.mult, op1=ALU.add)
                if k < KC - 1:
                    step(ins)
            signal(ins, ada_sum, j + 1)

        def inverse_root(n):
            dve.wait_ge(*B.ready("ss", n))
            take(TS(rstd, bank("ss", n)[:, 0:L], 1.0 / D, EPS, ALU.mult, ALU.add), "ss", n)
            signal(dve.reciprocal(rstd, rstd), var_ready, 1 if n == 1 else 6)
            dve.wait_ge(rstd_ready, 1 if n == 1 else 6)

        dve.wait_ge(params_in, 16)
        dve.wait_ge(cond_ready, 1)
        for j in range(4):
            product(j)
            if j == 1:
                dve.wait_ge(small_in, 32)
                inverse_root(1)
            if j >= 1:
                take_mod(j - 1)
        take_mod(3)

        def scale_columns(a, norm, base):
            step(TS(a, mod[:, base:base + KC], 1.0, None, ALU.add))
            step(TT(a, a, norm, ALU.mult))

        def norm_input(a):
            for k in range(KC):
                STT(out=h[:, k], in0=xT[:, k], scalar=a[:, k:k + 1], in1=rstd, op0=ALU.mult, op1=ALU.mult)\
                    .then_inc(scaled_ready, 1)

        scale_columns(a1, prm("norm_mix"), 8)
        dve.nop().then_inc(mod_ready, 1)
        norm_input(a1)
        product(4)

        for t in range(NT):
            dve.wait_ge(*B.released("q", t))
            step(TT(tmp[:, 0], q_tok[:, t], q_tok[:, t], ALU.mult))
            step(dve.tensor_reduce(st[:, 8 * t:8 * t + 8], two(tmp[:, 0], 8), AX.X, ALU.add))
        for t in range(NT):
            dve.wait_ge(*B.released("kv", t))
            step(TT(tmp[:, 0, 0:256], kvl[:, t], kvl[:, t], ALU.mult))
            step(dve.tensor_reduce(st[:, 16 + t:17 + t], tmp[:, 0, 0:256], AX.X, ALU.add))
        product(5)
        for t in range(NT):
            dve.wait_ge(*B.released("kw", t))
            step(dve.tensor_reduce(cnt[:, t:t + 1], kw[:, t, 0:64], AX.X, ALU.add))
            step(TS(cnt[:, t:t + 1], cnt[:, t:t + 1], -1.0 / 64, None, ALU.mult))
            step(TS(ki2[:, t, 0:64], kw[:, t, 0:64], cnt[:, t:t + 1], None, ALU.add))
            step(TT(tmp[:, 0, 0:64], ki2[:, t, 0:64], ki2[:, t, 0:64], ALU.mult))
            step(dve.tensor_reduce(st[:, 18 + t:19 + t], tmp[:, 0, 0:64], AX.X, ALU.add))
            step(TS(wi[:, t], kw[:, t, 64:72], HEADS ** -0.5 * HD ** -0.5, None, ALU.mult))
        inverse(st[:, 0:16], HD)
        inverse(st[:, 16:18], 256)
        inverse(st[:, 18:20], 64)
        signal(dve.reciprocal(st[:, 0:20], st[:, 0:20]), var_ready, 2)
        dve.wait_ge(*B.ready("bvec"))
        dve.tensor_copy(line_sb, bank("bvec")[0:HEADS, 0:384]).then_inc(*B.frees("bvec"))
        dve.wait_ge(*B.released("bvec"))
        dve.nop().then_inc(line_ready, 1)
        take_mod(4)
        dve.wait_ge(rstd_ready, 2)
        for t in range(NT):
            step(TT(two(q_tok[:, t], 8), two(q_tok[:, t], 8), rows(rs[:, 8 * t:8 * t + 8], HD), ALU.mult))
            step(TS(kvl[:, t], kvl[:, t], rs[:, 16 + t:17 + t], None, ALU.mult))
            step(TS(ki2[:, t, 64:], ki2[:, t, 0:64], rs[:, 18 + t:19 + t], None, ALU.mult))
            step(TS(ki2[:, t, 0:64], ki2[:, t, 0:64], rs[:, 18 + t:19 + t], None, ALU.mult))
        dve.nop().then_inc(tok_ready, 1)
        take_mod(5)
        dve.wait_ge(*B.ready("kvT"))
        step(TS(kvT[:, 0], bank("kvT")[:, 0:L], prm("kv_norm")[:, 0:1], None, ALU.mult))
        take(TS(kvT[:, 1], bank("kvT")[:, L:2 * L], prm("kv_norm")[:, 1:2], None, ALU.mult), "kvT")
        for t in range(NT):
            dve.wait_ge(*B.ready("qT", t))
            take(TS(qT[:, :, t * P:(t + 1) * P], two(bank("qT", t), 4), prm("q_norm"), None, ALU.mult), "qT", t)
        dve.wait_ge(*B.ready("kiT"))
        take(TS(kiT, bank("kiT")[:, 0:L], prm("ln_w"), prm("ln_b"), ALU.mult, ALU.add), "kiT")
        product(6)
        for t in range(NT):
            dve.wait_ge(*B.released("kv_up", 0, t))
            step(TT(tmp[:, 1], k_tok[:, t], k_tok[:, t], ALU.mult))
            step(dve.tensor_reduce(st[:, 20 + 8 * t:28 + 8 * t], two(tmp[:, 1], 8), AX.X, ALU.add))
        inverse(st[:, 20:36], HD)
        signal(dve.reciprocal(st[:, 20:36], st[:, 20:36]), var_ready, 3)
        dve.wait_ge(rstd_ready, 3)
        for t in range(NT):
            step(TT(two(k_tok[:, t], 8), two(k_tok[:, t], 8), rows(rs[:, 20 + 8 * t:28 + 8 * t], HD), ALU.mult))
        dve.nop().then_inc(tok_ready, 1)

        def pick_top(scores, n, want, m8, gt, eq, rank, cnt):
            thr = m8[:, (want - 1) % 8:(want - 1) % 8 + 1]
            step(TS(gt, scores, thr, None, ALU.is_gt))
            step(TS(eq, scores, thr, None, ALU.is_equal))
            step(dve.tensor_reduce(cnt, gt, AX.X, ALU.add))
            step(TS(cnt, cnt, -1.0, float(want), ALU.mult, ALU.add))
            step(dve.tensor_tensor_scan(rank, K("ones")[:, 0:n], eq, 0.0, ALU.mult, ALU.add))
            step(STT(out=eq, in0=rank, scalar=cnt, in1=eq, op0=ALU.is_le, op1=ALU.mult))
            step(TT(gt, gt, eq, ALU.add))

        dve.wait_ge(tables_in, 16)
        for t in range(NT):
            for g, h0 in enumerate(PAIRS_OF_HEADS):
                n = 4 * t + g
                dve.wait_ge(*B.released("dots", t, g))
                for i in range(2):
                    hd = h0 + 2 * i
                    if g == 0 and i == 0:
                        ins = TS(score[:, t], relu[:, n % 2, i], wi[:, t, hd:hd + 1], None, ALU.mult)
                    else:
                        ins = STT(out=score[:, t], in0=relu[:, n % 2, i], scalar=wi[:, t, hd:hd + 1], in1=score[:, t],
                                  op0=ALU.mult, op1=ALU.add)
                    if i == 0:
                        step(ins)
                    else:
                        signal(ins, relu_used, n + 1)
            causal = two(K("causal"))[:, t]
            step(TT(score[:, t], score[:, t], causal, ALU.add))
            step(dve.tensor_copy(top[:, 0], score[:, t]))
            for r in range(TOPK // 8):
                step(dve.max(m8[:, t], top[:, 0]))
                if r < TOPK // 8 - 1:
                    step(dve.match_replace(top[:, 0], m8[:, t], top[:, 0], 1.1 * FAR))
            pick_top(score[:, t], L, TOPK, m8[:, t], top[:, 1], top[:, 2], top[:, 3], cnt[:, t:t + 1])
            step(TS(keep[:, t], top[:, 1], -1.0, -NEG, ALU.add, ALU.mult))
            step(TT(keep[:, t], keep[:, t], causal, ALU.add))
            if t == 0:
                take_mod(6)
                product(7)
        for t in range(NT):
            dve.wait_ge(*B.ready("kT", t))
            take(TS(kT[:, :, t * P:(t + 1) * P], two(bank("kT", t), 4), prm("k_norm"), None, ALU.mult), "kT", t)
        dve.wait_ge(*B.released("dt"))
        step(TT(dtv, dtr, across(prm("dt_bias"), NT), ALU.add))
        signal(STT(out=dt, in0=dtv, scalar=-1.0, in1=dtv, op0=ALU.mult, op1=ALU.max), dt_abs, 1)
        take_mod(7)
        product(8)
        dve.wait_ge(bias_in, 16)
        for t in range(NT):
            nk = (t + 1) * P
            for g, h0 in enumerate(PAIRS_OF_HEADS):
                dve.wait_ge(*B.ready("S", t, g))
                take(STT(out=lg[:, h0:h0 + 3:2, 0:nk], in0=two(bank("S", t, g)[:, 0:2 * nk]), scalar=HD ** -0.5,
                         in1=bias[:, h0:h0 + 3:2, L - nk:], op0=ALU.mult, op1=ALU.add), "S", t, g)
            v = lg[:, :, 0:nk]
            step(TT(v, v, across(keep[:, t, 0:nk], HEADS), ALU.add))
            step(dve.tensor_reduce(mx, v, AX.X, ALU.max))
            signal(TT(v, v, rows(mx, nk), ALU.subtract), logits_ready, t + 1)
            if t == 0:
                dve.wait_ge(dt_log, 1)
                step(TS(dtv, dtv, 0.0, None, ALU.max))
                step(TT(dt, dt, dtv, ALU.add))
                signal(STT(out=dta, in0=dt, scalar=-1.0, in1=across(ea, NT), op0=ALU.mult, op1=ALU.mult), dta_ready, 1)
            dve.wait_ge(exp_ready, t + 1)
            step(dve.tensor_reduce(sm, v, AX.X, ALU.add))
            step(dve.reciprocal(sm, sm))
            signal(TT(v, v, rows(sm, nk), ALU.mult), probs_ready, t + 1)
            for k in range(6 * t, 6 * t + 6):
                cw = prm("conv_w")[:, 4 * k:4 * k + 4]
                dve.wait_ge(*B.released("xbc", k // 2))
                step(TS(xc[:, k], xbc[:, k, 0:L], cw[:, 0:1], prm("conv_b")[:, k:k + 1], ALU.mult, ALU.add))
                for j in range(1, 4):
                    ins = STT(out=xc[:, k], in0=xbc[:, k, j:j + L], scalar=cw[:, j:j + 1], in1=xc[:, k],
                              op0=ALU.mult, op1=ALU.add)
                    if j < 3:
                        step(ins)
                signal(ins, conv_ready, k + 1)
            take_mod(8 + t)
            product(9 + t)
        product(11)
        take_mod(10)
        take_mod(11)
        dve.wait_ge(*B.ready("acum"))
        step(dve.tensor_copy(acum, two(bank("acum")[:, 0:2 * SH])))
        take(dve.tensor_copy(alast, two(bank("acum")[:, 2 * SH:4 * SH])), "acum")
        step(TS(nac, acum, -1.0, None, ALU.mult))
        signal(TT(dec, alast, acum, ALU.subtract), acum_ready, 1)

        def heads(v):
            return v.rearrange("p (h n) -> p h n", n=64)

        for t in range(NT):
            dve.wait_ge(*B.released("xT", t, 1))
            step(TT(heads(xdt[:, t]), heads(xs[:, t]), rows(dt[:, t], 64), ALU.mult))
        dve.wait_ge(decay_exp, 1)
        step(TT(dec, dec, dt, ALU.mult))
        signal(TT(heads(xdec), heads(xs[:, 0]), rows(dec[:, 0], 64), ALU.mult), xdt_ready, 1)
        for c in range(NT):
            for j in range(4):
                dve.wait_ge(*B.ready("row", c, j))
                if c == 1 and j == 0:
                    dve.wait_ge(*B.ready("yi", 0, 1))
                for i in range(4):
                    hd = 4 * j + i
                    ins = STT(out=seg[:, hd], in0=bank("row", c, j)[:, i * P:(i + 1) * P], scalar=nac[:, c, hd:hd + 1],
                              in1=K("ssd_mask"), op0=ALU.add, op1=ALU.add)
                    if i < 3:
                        step(ins)
                take(ins, "row", c, j)
                dve.nop().then_inc(seg_ready, 1)
            step(TT(heads(y_tok[:, c]), heads(xs[:, c]), rows(prm("d_skip"), 64), ALU.mult))
            dve.wait_ge(seg_exp, c + 1)
            dve.wait_ge(*B.released("cb", c))
            step(TT(seg[:, 0:8], seg[:, 0:8], across(cbT[:, c, 0], 8), ALU.mult))
            signal(TT(seg[:, 8:16], seg[:, 8:16], across(cbT[:, c, 1], 8), ALU.mult), w_ready, c + 1)
            if c == 1:
                for g in range(SG):
                    half = y_tmp[:, g * 512:(g + 1) * 512]
                    dve.wait_ge(*B.ready("yx", g))
                    take(TT(heads(half), heads(bank("yx", g)), rows(eac[:, 1, 8 * g:8 * g + 8], 64), ALU.mult), "yx", g)
                step(TT(y_tok[:, 1], y_tok[:, 1], y_tmp, ALU.add))
            for g in range(SG):
                half = y_tok[:, c, g * 512:(g + 1) * 512]
                dve.wait_ge(*B.ready("yi", c, g))
                take(TT(half, bank("yi", c, g), half, ALU.add), "yi", c, g)
            step(TT(y_tok[:, c], y_tok[:, c], z[:, c], ALU.mult))
            step(TT(y_tmp, y_tok[:, c], y_tok[:, c], ALU.mult))
            v = st[:, 2 * c:2 * c + 2]
            step(dve.tensor_reduce(v, two(y_tmp), AX.X, ALU.add))
            inverse(v, 512)
            signal(dve.reciprocal(v, v), var_ready, 4 + c)
        for c in range(NT):
            dve.wait_ge(rstd_ready, 4 + c)
            signal(TT(two(y_tok[:, c]), two(y_tok[:, c]), rows(rs[:, 2 * c:2 * c + 2], 512), ALU.mult), y_ready, c + 1)
        for p in range(4):
            dve.wait_ge(*B.ready("ya", p))
            take(TT(mixed[:, 2 * p:2 * p + 2], two(bank("ya", p)), sig[:, 2 * p:2 * p + 2], ALU.mult), "ya", p)
        for p in range(4):
            dve.wait_ge(*B.ready("ys", p))
            v = seg[:, 4 * p:4 * p + 4].rearrange("p a b -> p (a b)")
            take(TT(two(v), two(bank("ys", p)), sig[:, KC + 2 * p:KC + 2 * p + 2], ALU.mult), "ys", p)
            m = mixed[:, 2 * p:2 * p + 2]
            step(TT(m, m, two(v), ALU.add))
        dve.nop().then_inc(mixed_ready, 1)
        scale_columns(a2, prm("norm_ffn"), 32)
        dve.nop().then_inc(mod_ready, 1)
        for p in range(4):
            dve.wait_ge(*B.ready("x1", p))
            for i in range(2):
                k = 2 * p + i
                ins = STT(out=xT[:, k], in0=bank("x1", p)[:, i * L:(i + 1) * L], scalar=mod[:, 16 + k:17 + k], in1=xT[:, k],
                          op0=ALU.mult, op1=ALU.add)
                if i == 0:
                    step(ins)
            take(ins, "x1", p)
            dve.nop().then_inc(x1_ready, 1)
        inverse_root(2)
        norm_input(a2)
        dve.wait_ge(*B.ready("rl"))
        take(TT(X.lr, two(bank("rl")[:, 0:2 * E]), across(prm("b_router"), NT), ALU.add), "rl")
        for t in range(NT):
            step(dve.max(m8[:, t], X.lr[:, t]))
            pick_top(X.lr[:, t], E, TOP_K, m8[:, t], X.mask[:, t], X.tm[:, t], X.rank[:, t], cnt[:, t:t + 1])
            step(TS(X.ex[:, t], X.lr[:, t], m8[:, t, 0:1], None, ALU.subtract))
        dve.nop().then_inc(mask_ready, 1)
        dve.nop().then_inc(route_ready, 1)
        dve.wait_ge(route_exp, 1)
        step(TT(X.ex, X.ex, X.mask, ALU.mult))
        step(dve.tensor_reduce(cnt[:, 2:4], X.ex, AX.X, ALU.add))
        step(dve.reciprocal(cnt[:, 2:4], cnt[:, 2:4]))
        signal(TT(X.gate[:, :, 0:E], X.ex, rows(cnt[:, 2:4], E), ALU.mult), gates_ready, 1)
        dve.wait_ge(*B.ready("cum"))
        step(TT(X.tm, two(bank("cum")[:, 0:2 * E]), X.mask, ALU.mult))
        step(TS(X.place[:, :, 0:E], X.tm, -1.0, None, ALU.add))
        take(dve.tensor_reduce(cnt[:, 4:5], bank("cum")[:, 2 * E:3 * E], AX.X, ALU.max), "cum")
        step(TS(X.flag, cnt[:, 4:5], float(CAP), None, ALU.is_gt))
        step(TS(X.place[:, :, E:], X.place[:, :, 0:2], float(-CAP), None, ALU.add))
        step(dve.tensor_copy(X.gate[:, :, E:], X.gate[:, :, 0:2]))
        X.pick(dve, 0)
        dve.wait_ge(*B.released("yb", 3))
        with dve.Fori(0, PAIRS) as p:
            X.glu(dve, BP, psum, p)
            X.pick(dve, p + 1, BP, p)
            X.add_up(dve, BP, psum, y_sum, p)
        with dve.If(X.more_rounds(dve)):
            with dve.Fori(1, ROUNDS) as r:
                dve.wait_ge(X.picked, r * PAIRS + 1)
                TS(X.place, X.place, float(-CAP), None, ALU.add).then_inc(X.moved, 1)
                with dve.Fori(0, PAIRS) as p:
                    X.glu(dve, BP, psum, r * PAIRS + p)
                    dve.wait_ge(X.moved, r)
                    X.pick(dve, p + 1, BP, r * PAIRS + p)
                    X.add_up(dve, BP, psum, y_sum, r * PAIRS + p)
    return X


def chunk_of(d, s):
    return s if d == 0 else 1 - s


def second_block(nc, ctx, io, mem, out, first_sum):
    sem = lambda n: ctx.enter_context(nc.semaphore(n))
    xT, h, psum = mem.xT, mem.h, mem.psum
    K, slot = mem.K, mem.slot

    bank_full = [sem(f"bank_full_2_{b}") for b in range(BANKS)]
    bank_free = [sem(f"bank_free_2_{b}") for b in range(BANKS)]
    slot_full = [sem(f"slot_full_2_{b}") for b in range(SLOTS)]
    B = Uses(bank_full, bank_free, layer_banks(), credit=1)
    S = Uses(slot_full, slot_full, LAYER_SLOTS, inc=16, twice=[("up", j) for j in range(11)])

    act_step, dve_step, pool_step = sem("act_step_2"), sem("dve_step_2"), sem("pool_step_2")
    x_ready = sem("x_ready")
    params_in = sem("params_in")
    pads_ready = sem("pads_ready")
    down_used = [sem("down_used_first"), sem("down_used_second")]
    sq_ready = sem("sq_ready_2")
    var_ready, rstd_ready = sem("var_ready_2"), sem("rstd_ready_2")
    h_ready = sem("h_ready_2")
    rope_ready = sem("rope_ready")
    gate_abs, gate_log, lf_ready = sem("gate_abs"), sem("gate_log"), sem("lf_ready")
    r_ready = sem("r_ready")
    logits_ready, exp_ready, probs_ready = sem("logits_ready_2"), sem("exp_ready_2"), sem("probs_ready_2")
    conv_ready, silu_ready = sem("conv_ready_2"), sem("silu_ready_2")
    dlog_ready, dexp_ready, sc_ready = sem("dlog_ready"), sem("dexp_ready"), sem("sc_ready")
    kw_ready = sem("kw_ready")
    total_ready = sem("total_ready")
    hm_ready = sem("hm_ready")
    tap_ready, conv2_ready, gelu_ready, hid_ready = (
        sem(n) for n in ("tap_ready", "conv2_ready", "gelu_ready", "hid_ready"))
    out_done = sem("out_done")

    prm = lambda name: PARAMS2.of(mem.route, name)
    ident, ones = K("ident"), K("ones")[:, 0:P]
    A = Arena(mem.work)
    mqk_pad = A.take(8, L + 4)
    v_aug = A.take(NT, MH, P + 1)
    mixed_at = A.at
    aqk = A.take(2, NT, AW)
    mixed = Arena(mem.work, mixed_at).take(KC, L)
    w_g = A.take(KC, 16)
    rstd = A.take(1, L)[:, 0]
    cat = A.take(KC, L)
    hid_at = A.at
    av = A.take(NT, AW)
    qT, kT = A.take(4, L), A.take(4, L)
    lg_at = A.at
    lg = A.take(HEADS, L)
    pt = A.take(16, P)
    mqk = A.take(8, L)
    mo = A.take(MH, L)
    k_tok = A.take(NT, MH, P)
    qk = A.take(NT, MH, P)
    dl = A.take(8, P)
    scT = A.take(8, P)
    kw = A.take(8, P)
    st, tot = A.take(8, P + 1), A.take(8, P + 1)
    hm = A.take(NT, MH, P)
    rope_tmp = Arena(mem.work, lg_at).take(4, 8, 32)
    sq = Arena(mem.work, lg_at).take(KC, L)
    hid = Arena(mem.work, hid_at).take(FC, L)
    sq_down = cat
    F = Arena(mem.work, hid_at + FC * L + 600)
    taps = F.take(3, 2, L)
    SM = Arena(mem.small)
    li, lf, lfx = SM.take(2, 8), SM.take(2, 8), SM.take(2, 8)
    bcum, btot, r = SM.take(2, 8), SM.take(2, 8), SM.take(2, 8)
    mxr, md, inter, mt, mst, mnew, den = (SM.take(8) for _ in range(7))
    ex3 = SM.take(3, 8)
    mx, sm = SM.take(8), SM.take(8)
    hs = SM.take(8)

    block = ctx.enter_context(nc.Block())

    @block.sync
    def _(sp):
        with sp.Fori(0, LAYERS) as l:
            def used(name, j):
                kind = name[0]
                if kind == "win":
                    last = (("aq", 1), ("ak", 1), ("av", 1), ("mqk", 1), ("mqk", 3), ("mv", 1), ("mo", 1))[name[1]]
                    return B.ready(*last, it=l)
                if kind == "wout":
                    return B.ready("mix", 2 * name[1] + 1, it=l)
                if kind == "up":
                    return B.ready("up", 2 * name[1] + 1, it=l)
                return down_used[name[2]], l * 4 + 4 + name[1] + 1

            for i, name in enumerate(LAYER_SLOTS):
                kind, j = name[0], name[1]
                if i == 0:
                    sp.wait_ge(down_used[0], l * 4 + 4)
                elif i in (1, 3):
                    sp.wait_ge(down_used[1], l * 4 + 3 + i // 2)
                elif i >= SLOTS:
                    sp.wait_ge(*used(LAYER_SLOTS[i - SLOTS], i))
                lay = bass.ds(l, 1)
                if kind == "up":
                    dst = slot(S.no(name), KC, 512)
                    for part in range(2):
                        src = io["w_up_2"][lay, :, part * FF + 256 * j:part * FF + 256 * j + 256]
                        sp.dma_start(dst[:, :, part * 256:part * 256 + 256], src.rearrange("a (k p) n -> p (a k) n", p=P))\
                          .then_inc(*S.fills(*name))
                    continue
                if kind == "down":
                    half = name[2]
                    src = io["w_down_2"][lay, half * FF // 2:(half + 1) * FF // 2, 256 * j:256 * j + 256]
                    dst = slot(S.no(name), FC // 2, 256)
                else:
                    w = io["w_in_2"] if kind == "win" else io["w_out_2"]
                    src, dst = w[lay, :, 512 * j:512 * j + 512], slot(S.no(name), KC, 512)
                sp.dma_start(dst, src.rearrange("a (k p) n -> p (a k) n", p=P)).then_inc(*S.fills(*name))
        sp.wait_ge(x_ready, 4 + 8 * LAYERS)
        sp.dma_start(out, xT).then_inc(out_done, 16)
        sp.wait_ge(out_done, 16)

    @block.gpsimd
    def _(pool):
        step = Steps(pool, pool_step)
        pool.wait_ge(x_ready, 4)
        pool.memset(mqk_pad[:, :, 0:2], 0.0).then_inc(pads_ready, 1)
        pool.memset(mqk_pad[:, :, L + 2:], 0.0).then_inc(pads_ready, 1)
        pool.memset(v_aug[:, :, :, P:], 1.0).then_inc(pads_ready, 1)
        with pool.Fori(0, LAYERS) as l:
            pool.wait_ge(x_ready, l * 8 + 4)
            pool.wait_ge(mem.staged_in, 32 * LAYERS)
            pool.tensor_copy(mem.route[:, 0:PARAMS2.n], mem.staged[:, bass.ds(l * PARAMS2.n, PARAMS2.n)]).then_inc(params_in, 1)
            pool.tensor_copy(w_g.rearrange("p k n -> p (k n)"), mem.staged_gates[:, bass.ds(l * (KC * 16), KC * 16)]).then_inc(params_in, 1)
            for i in range(2):
                for t in range(NT):
                    pool.wait_ge(*B.released(("aq", "ak")[i], t, it=l))
                    v = aqk[:, i, t].rearrange("p (h c n) -> p h c n", h=HEADS, c=2)
                    cos = across(K("cos")[:, 32 * t:32 * t + 32], HEADS)
                    sin = across(K("sin")[:, 32 * t:32 * t + 32], HEADS)
                    step(pool.tensor_tensor(rope_tmp[:, 0], v[:, :, 0], cos, ALU.mult))
                    step(pool.tensor_tensor(rope_tmp[:, 1], v[:, :, 1], sin, ALU.mult))
                    step(pool.tensor_tensor(rope_tmp[:, 2], v[:, :, 1], cos, ALU.mult))
                    step(pool.tensor_tensor(rope_tmp[:, 3], v[:, :, 0], sin, ALU.mult))
                    step(pool.tensor_tensor(v[:, :, 0], rope_tmp[:, 0], rope_tmp[:, 1], ALU.subtract))
                    step(pool.tensor_tensor(v[:, :, 1], rope_tmp[:, 2], rope_tmp[:, 3], ALU.add))
                    pool.nop().then_inc(rope_ready, 1)
            step.restart()

    @block.tensor
    def _(pe):
        pe.nop().then_inc(down_used[0], 4)
        for free in bank_free:
            pe.nop().then_inc(free, 1)
        with pe.Fori(0, LAYERS) as l:
            def bank(*name):
                return psum[:, B.no(name)]

            def empty(*name):
                pe.wait_ge(*B.empty(*name, it=l))

            def ready(*name):
                pe.wait_ge(*S.ready(*name, it=l))
                return slot(S.no(name), KC, 512)

            def evicted(*name):
                pe.wait_ge(*B.released(*name, it=l))

            def sum_squares(n):
                empty("ss", n)
                for k in range(KC):
                    if k % 2 == 0:
                        pe.wait_ge(sq_ready, l * 16 + (4 * n + k // 2 + 1))
                    ins = matmul(pe, bank("ss", n)[:, 0:L], ones, (sq_down if n == 3 else sq)[:, k], k == 0, k == KC - 1)
                ins.then_inc(*B.fills("ss", n))

            def by_token(name, w, n=512):
                for t in range(NT):
                    empty(name, t)
                    for k in range(KC):
                        ins = matmul(pe, bank(name, t)[:, 0:n], h[:, k, t * P:(t + 1) * P], w[:, k, 0:n], k == 0, k == KC - 1)
                    ins.then_inc(*B.fills(name, t))

            def by_feature(name, w, c0, rhs=h):
                empty(*name)
                for i in range(2):
                    for k in range(KC):
                        ins = matmul(pe, bank(*name)[:, i * L:(i + 1) * L], w[:, k, c0 + i * P:c0 + (i + 1) * P], rhs[:, k],
                                     k == 0, k == KC - 1)
                ins.then_inc(*B.fills(*name))

            def transposes(name, blocks):
                empty(*name)
                for i, b in enumerate(blocks):
                    ins = pe.transpose(bank(*name)[:, i * P:(i + 1) * P], b, ident)
                ins.then_inc(*B.fills(*name))

            sum_squares(0)
            pe.wait_ge(params_in, l * 2 + 2)
            empty("gates")
            for t in range(NT):
                for k in range(KC):
                    if t == 0:
                        pe.wait_ge(h_ready, l * (2 * KC) + (k + 1))
                    ins = matmul(pe, bank("gates")[:, t * 16:t * 16 + 16], h[:, k, t * P:(t + 1) * P], w_g[:, k], k == 0, k == KC - 1)
            ins.then_inc(*B.fills("gates"))
            for j in range(2):
                w = ready("win", 3 + j)
                by_feature(("mqk", 2 * j), w, 0)
                by_feature(("mqk", 2 * j + 1), w, 256)
            by_token("aq", ready("win", 0))
            pe.wait_ge(lf_ready, l + 1)
            empty("bc")
            for s in range(2):
                for d in range(2):
                    c = 8 * s + 4 * d
                    matmul(pe, bank("bc")[:, c:c + 4], K("tri_le") if d == 0 else K("tri_ge"), lf[:, s, 4 * d:4 * d + 4])
                ins = matmul(pe, bank("bc")[:, 16 + 8 * s:24 + 8 * s], ones, lf[:, s])
            ins.then_inc(*B.fills("bc"))
            by_token("ak", ready("win", 1))

            def logits(t):
                evicted("kT", 1)
                for g, h0 in enumerate(PAIRS_OF_HEADS):
                    empty("S", t, g)
                    for i in range(2):
                        hd = h0 + 2 * i
                        r_ = slice(64 * (hd % 2), 64 * (hd % 2) + 64)
                        ins = matmul(pe, bank("S", t, g)[:, i * L:(i + 1) * L], qT[r_, hd // 2, t * P:(t + 1) * P], kT[r_, hd // 2])
                    ins.then_inc(*B.fills("S", t, g))

            def attend(t):
                pe.wait_ge(probs_ready, l * 2 + t + 1)
                for j in range(4):
                    transposes(("PT", t, j), [lg[:, 2 * j + i, s * P:(s + 1) * P] for i in range(2) for s in range(2)])
                empty("O", t)
                evicted("PT", t, 3)
                for hd in range(HEADS):
                    r_ = slice(64 * (hd % 2), 64 * (hd % 2) + 64)
                    for s in range(2):
                        ins = matmul(pe, bank("O", t)[r_, (hd // 2) * P:(hd // 2 + 1) * P], av[:, s, hd * HD:(hd + 1) * HD],
                                     pt[:, 2 * hd + s], s == 0, s == 1)
                ins.then_inc(*B.fills("O", t))

            def r_rows(s):
                for d in range(2):
                    empty("r", s, d)
                    for i in range(MH):
                        ins = matmul(pe, bank("r", s, d)[:, i * P:(i + 1) * P],
                                     r[:, s, 4 * d + i:4 * d + i + 1].to_broadcast([P, P]), ident)
                    ins.then_inc(*B.fills("r", s, d))

            def numerators(s):
                pe.wait_ge(sc_ready, l * 2 + s + 1)
                for d in range(2):
                    transposes(("cT", s, d), [dl[:, 4 * d + i] for i in range(MH)])
                evicted("cT", s, 1)
                for j in range(4):
                    empty("num", s, j)
                    for i in range(2):
                        c = 2 * j + i
                        ins = matmul(pe, bank("num", s, j)[:, i * 129:(i + 1) * 129], scT[:, c], v_aug[:, chunk_of(c // 4, s), c % 4])
                    ins.then_inc(*B.fills("num", s, j))

            pe.wait_ge(r_ready, l + 1)
            r_rows(0)
            pe.wait_ge(silu_ready, l + 1)
            for c in range(NT):
                empty("qk", c)
                for i in range(MH):
                    ins = matmul(pe, bank("qk", c)[:, i * P:(i + 1) * P], mqk[:, i, c * P:(c + 1) * P], mqk[:, MH + i, c * P:(c + 1) * P])
                ins.then_inc(*B.fills("qk", c))
            for t in range(NT):
                transposes(("kt", t), [mqk[:, MH + i, t * P:(t + 1) * P] for i in range(MH)])
            by_token("mv", ready("win", 5))
            pe.wait_ge(rope_ready, l * 4 + 4)
            for t in range(NT):
                for i, name in enumerate(("qT", "kT")):
                    transposes((name, t), [aqk[:, i, t, c * P:(c + 1) * P] for c in range(4)])
            logits(0)
            numerators(0)
            pe.wait_ge(kw_ready, l + 1)
            for j in range(4):
                empty("st", j)
                for i in range(2):
                    c = 2 * j + i
                    ins = matmul(pe, bank("st", j)[:, i * 129:(i + 1) * 129], kw[:, c], v_aug[:, chunk_of(c // 4, 0), c % 4])
                ins.then_inc(*B.fills("st", j))
            r_rows(1)
            by_token("av", ready("win", 2))
            attend(0)
            logits(1)
            numerators(1)
            evicted("st", 3)
            for j in range(4):
                empty("ix", j)
                for i in range(2):
                    c = 2 * j + i
                    t = chunk_of(c // 4, 1)
                    ins = matmul(pe, bank("ix", j)[:, i * 129:(i + 1) * 129], mqk[:, c % 4, t * P:(t + 1) * P], st[:, c])
                ins.then_inc(*B.fills("ix", j))
            w = ready("win", 6)
            for p in range(2):
                by_feature(("mo", p), w, 256 * p)
            attend(1)
            pe.wait_ge(hm_ready, l + 1)
            for t in range(NT):
                transposes(("hT", t), [hm[:, t, i] for i in range(MH)])
            evicted("hT", 1)
            evicted("O", 1)
            for p in range(4):
                if p % 2 == 0:
                    w = ready("wout", p // 2)
                by_feature(("mix", p), w, 256 * (p % 2), cat)
            sum_squares(1)
            sum_squares(2)
            for c in range(FC):
                if c % 2 == 0:
                    w = ready("up", c // 2)
                empty("up", c)
                for part in range(2):
                    for k in range(KC):
                        if c == 0 and part == 0:
                            pe.wait_ge(h_ready, l * (2 * KC) + (KC + k + 1))
                        c0 = 256 * part + P * (c % 2)
                        ins = matmul(pe, bank("up", c)[:, part * L:(part + 1) * L], w[:, k, c0:c0 + P], h[:, k], k == 0, k == KC - 1)
                ins.then_inc(*B.fills("up", c))
            for j in range(4):
                empty("down", 2 * j)
                empty("down", 2 * j + 1)
                for half in range(2):
                    pe.wait_ge(hid_ready, l * FC + (half + 1) * FC // 2)
                    pe.wait_ge(*S.ready("down", j, half, it=l))
                    w = slot(S.no(("down", j, half)), FC // 2, 256)
                    for i in range(2):
                        for k in range(FC // 2):
                            ins = matmul(pe, bank("down", 2 * j + i)[:, 0:L], w[:, k, i * P:(i + 1) * P], hid[:, half * (FC // 2) + k],
                                         half == 0 and k == 0, half == 1 and k == FC // 2 - 1)
                        if half == 1:
                            ins.then_inc(*B.fills("down", 2 * j + i))
                    if half == 0:
                        ins.then_inc(down_used[0], 1)
            sum_squares(3)

    @block.scalar
    def _(act):
        step = Steps(act, act_step)
        act.nop().then_inc(down_used[1], 4)
        with act.Fori(0, LAYERS) as l:
            def bank(*name):
                return psum[:, B.no(name)]

            def take(out_, in_, *name, func=ACT.Copy, **kw_):
                act.wait_ge(*B.ready(*name, it=l))
                act.activation(out_, in_, func, **kw_).then_inc(*B.frees(*name))

            def cut(v, n):
                return v.rearrange("p (a b) -> p a b", a=n)

            def squares(v, p, into=sq):
                c = slice(2 * p, 2 * p + 2)
                act.activation(into[:, c], v[:, c], ACT.Square).then_inc(sq_ready, 1)

            def residual_squares(n):
                for p in range(4):
                    act.wait_ge(x_ready, l * 8 + (4 * n + p + 1))
                    squares(xT, p)

            def root(out_, in_, n):
                act.wait_ge(var_ready, l * 5 + n)
                act.activation(out_, in_, ACT.Sqrt).then_inc(rstd_ready, 1)

            residual_squares(0)
            root(rstd, rstd, 1)
            act.wait_ge(pads_ready, 3)
            for p in range(4):
                take(mqk_pad[:, 2 * p:2 * p + 2, 2:L + 2], cut(bank("mqk", p), 2), "mqk", p)
            act.wait_ge(gate_abs, l + 1)
            step(act.activation(lf, lf, ACT.Exp, scale=-1.0))
            act.activation(lf, lf, ACT.Ln, bias=1.0).then_inc(gate_log, 1)
            for t in range(NT):
                take(aqk[:, 0, t], bank("aq", t), "aq", t)
            act.wait_ge(conv_ready, l + 1)
            act.activation(mqk, mqk, ACT.Silu).then_inc(silu_ready, 1)
            for t in range(NT):
                take(aqk[:, 1, t], bank("ak", t), "ak", t)
            for c in range(NT):
                take(qk[:, c], cut(bank("qk", c), MH), "qk", c, scale=P ** -0.5)
            for t in range(NT):
                take(k_tok[:, t], cut(bank("kt", t), MH), "kt", t, scale=P ** -0.5)

            def exponentials(s):
                act.wait_ge(dlog_ready, l * 2 + s + 1)
                step(act.activation(ex3, ex3, ACT.Exp))
                act.activation(dl, dl, ACT.Exp).then_inc(dexp_ready, 1)

            def numerators(s):
                for d in range(2):
                    take(scT[:, 4 * d:4 * d + 4], cut(bank("cT", s, d), MH), "cT", s, d)
                if s == 1:
                    act.wait_ge(total_ready, l + 1)
                for j in range(4):
                    take(tot[:, 2 * j:2 * j + 2], cut(bank("num", s, j)[:, 0:258], 2), "num", s, j)

            def softmax_exp(t):
                act.wait_ge(logits_ready, l * 2 + t + 1)
                act.activation(lg, lg, ACT.Exp).then_inc(exp_ready, 1)

            def attended(t):
                for j in range(4):
                    take(pt[:, 4 * j:4 * j + 4], cut(bank("PT", t, j), 4), "PT", t, j)
                if t == 0:
                    exponentials(1)
                take(cat[:, 0:4, t * P:(t + 1) * P], cut(bank("O", t), 4), "O", t)

            exponentials(0)
            for t in range(NT):
                take(v_aug[:, t, :, 0:P], cut(bank("mv", t), MH), "mv", t)
            numerators(0)
            for j in range(4):
                take(st[:, 2 * j:2 * j + 2], cut(bank("st", j)[:, 0:258], 2), "st", j)
            softmax_exp(0)
            for t in range(NT):
                take(av[:, t], bank("av", t), "av", t)
            attended(0)
            numerators(1)
            softmax_exp(1)
            root(hs, hs, 2)
            for p in range(2):
                take(mo[:, 2 * p:2 * p + 2], cut(bank("mo", p), 2), "mo", p, func=ACT.Sigmoid)
            attended(1)
            for p in range(4):
                take(mixed[:, 2 * p:2 * p + 2], cut(bank("mix", p), 2), "mix", p)
                act.wait_ge(*B.released("mix", p, it=l))
                squares(mixed, p)
            root(rstd, rstd, 3)
            residual_squares(1)
            root(rstd, rstd, 4)

            def tap(c):
                act.wait_ge(*B.ready("up", c, it=l))
                if c >= 3:
                    act.wait_ge(hid_ready, l * FC + (c - 2))
                for part in range(2):
                    f = c + FC * part
                    ins = act.activation(taps[:, c % 3, part], bank("up", c)[:, part * L:(part + 1) * L], ACT.Identity,
                                         scale=prm("ffn_w")[:, 3 * f + 1:3 * f + 2], bias=prm("ffn_b")[:, f:f + 1])
                ins.then_inc(tap_ready, 1)

            def gelu(c):
                act.wait_ge(conv2_ready, l * FC + (c + 1))
                act.activation(taps[:, c % 3, 0], taps[:, c % 3, 0], ACT.Gelu_apprx_tanh).then_inc(gelu_ready, 1)

            for c in range(FC):
                tap(c)
                if c >= 1:
                    gelu(c - 1)
            gelu(FC - 1)
            for c in range(KC):
                take(mixed[:, c], bank("down", c)[:, 0:L], "down", c)
                if c % 2 == 1:
                    act.wait_ge(*B.released("down", c, it=l))
                    act.nop().then_inc(down_used[1], 1)
                    squares(mixed, c // 2, sq_down)
            root(rstd, rstd, 5)
            step.restart()

    @block.vector
    def _(dve):
        step = Steps(dve, dve_step)
        TS, TT, STT = dve.tensor_scalar, dve.tensor_tensor, dve.scalar_tensor_tensor
        for k in range(KC):
            ins = STT(out=xT[:, k], in0=first_sum[:, k], scalar=mem.mod[:, 40 + k:41 + k], in1=xT[:, k],
                      op0=ALU.mult, op1=ALU.add)
            if k % 2 == 1:
                ins.then_inc(x_ready, 1)
        dve.wait_ge(x_ready, 4)
        with dve.Fori(0, LAYERS) as l:
            def bank(*name):
                return psum[:, B.no(name)]

            def filled(*name):
                dve.wait_ge(*B.ready(*name, it=l))

            def take(ins, *name):
                ins.then_inc(*B.frees(*name))
                dve.wait_ge(*B.released(*name, it=l))

            def signal(ins, sem_, n):
                ins.then_inc(sem_, 1)
                dve.wait_ge(sem_, n)

            def cut(v, n):
                return v.rearrange("p (a b) -> p a b", a=n)

            def inverse_root(n, which):
                filled("ss", n)
                take(TS(rstd, bank("ss", n)[:, 0:L], 1.0 / D, EPS, ALU.mult, ALU.add), "ss", n)
                signal(dve.reciprocal(rstd, rstd), var_ready, l * 5 + which)
                dve.wait_ge(rstd_ready, l * 5 + which)

            def norm_input(g):
                for k in range(KC):
                    STT(out=h[:, k], in0=xT[:, k], scalar=g[:, k:k + 1], in1=rstd, op0=ALU.mult, op1=ALU.mult)\
                        .then_inc(h_ready, 1)

            def add_normed(g, n, last=False):
                for p in range(4):
                    for k in (2 * p, 2 * p + 1):
                        ins = STT(out=mixed[:, k], in0=mixed[:, k], scalar=g[:, k:k + 1], in1=rstd, op0=ALU.mult, op1=ALU.mult)
                    step(ins)
                    if last and p == 3:
                        step.restart()
                    x = xT[:, 2 * p:2 * p + 2]
                    TT(x, x, mixed[:, 2 * p:2 * p + 2], ALU.add).then_inc(x_ready, 1)
                dve.wait_ge(x_ready, l * 8 + 4 * n)

            inverse_root(0, 1)
            dve.wait_ge(params_in, l * 2 + 2)
            norm_input(prm("mix_pre"))
            filled("gates")
            for s in range(2):
                for d in range(2):
                    t = chunk_of(d, s)
                    c = slice(4 * d, 4 * d + 4)
                    a = 8 * d
                    step(TT(li[:, s, c], bank("gates")[:, 16 * t + a:16 * t + a + 4], prm("gate_b")[:, a:a + 4], ALU.add))
                    ins = TT(lfx[:, s, c], bank("gates")[:, 16 * t + a + 4:16 * t + a + 8], prm("gate_b")[:, a + 4:a + 8], ALU.add)
                    if (s, d) != (1, 1):
                        step(ins)
            take(ins, "gates")
            signal(STT(out=lf, in0=lfx, scalar=-1.0, in1=lfx, op0=ALU.mult, op1=ALU.max), gate_abs, l + 1)
            for k in range(8):
                if k % 2 == 0:
                    dve.wait_ge(*B.released("mqk", k // 2, it=l))
                cw = prm("conv_w")[:, 5 * k:5 * k + 5]
                step(TS(mqk[:, k], mqk_pad[:, k, 0:L], cw[:, 0:1], prm("conv_b")[:, k:k + 1], ALU.mult, ALU.add))
                for j in range(1, 5):
                    ins = STT(out=mqk[:, k], in0=mqk_pad[:, k, j:j + L], scalar=cw[:, j:j + 1], in1=mqk[:, k],
                              op0=ALU.mult, op1=ALU.add)
                    if (k, j) != (7, 4):
                        step(ins)
            signal(ins, conv_ready, l + 1)
            dve.wait_ge(gate_log, l + 1)
            step(TS(lfx, lfx, 0.0, None, ALU.min))
            signal(TT(lf, lfx, lf, ALU.subtract), lf_ready, l + 1)
            filled("bc")
            step(dve.tensor_copy(bcum, cut(bank("bc")[:, 0:16], 2)))
            take(dve.tensor_copy(btot, cut(bank("bc")[:, 16:32], 2)), "bc")
            signal(TT(r, li, bcum, ALU.subtract), r_ready, l + 1)
            def soften(t):
                for g, h0 in enumerate(PAIRS_OF_HEADS):
                    filled("S", t, g)
                    take(STT(out=lg[:, h0:h0 + 3:2], in0=cut(bank("S", t, g), 2), scalar=HD ** -0.5,
                             in1=across(K("log_count")[:, L * t:L * t + L], 2), op0=ALU.mult, op1=ALU.add), "S", t, g)
                step(dve.tensor_reduce(mx, lg, AX.X, ALU.max))
                signal(TT(lg, lg, rows(mx, L), ALU.subtract), logits_ready, l * 2 + t + 1)

            def normalise(t):
                dve.wait_ge(exp_ready, l * 2 + t + 1)
                step(dve.tensor_reduce(sm, lg, AX.X, ALU.add))
                step(dve.reciprocal(sm, sm))
                signal(TT(lg, lg, rows(sm, L), ALU.mult), probs_ready, l * 2 + t + 1)

            def weigh(s):
                if s == 0:
                    step(dve.memset(mst, 0.0))
                for d in range(2):
                    filled("r", s, d)
                    step(dve.tensor_reduce(mxr[:, 4 * d:4 * d + 4], cut(bank("r", s, d), MH), AX.X, ALU.max))
                    for i in range(MH):
                        c = 4 * d + i
                        ins = STT(out=dl[:, c], in0=bank("r", s, d)[:, i * P:(i + 1) * P], scalar=bcum[:, s, c:c + 1],
                                  in1=K("mask_fwd") if d == 0 else K("mask_bwd"), op0=ALU.add, op1=ALU.add)
                        if i < MH - 1:
                            step(ins)
                    take(ins, "r", s, d)
                step(dve.tensor_reduce(md, dl, AX.X, ALU.max))
                step(TT(inter, bcum[:, s], mst, ALU.add))
                step(TT(mt, inter, md, ALU.max))
                step(TT(mnew, btot[:, s], mst, ALU.add))
                step(TT(mxr, mxr, btot[:, s], ALU.add))
                step(TT(mnew, mnew, mxr, ALU.max))
                step(TT(ex3[:, 0], inter, mt, ALU.subtract))
                step(TS(ex3[:, 1], mt, -1.0, None, ALU.mult))
                step(TT(ex3[:, 2], r[:, s], btot[:, s], ALU.add))
                step(TT(ex3[:, 2], ex3[:, 2], mnew, ALU.subtract))
                step(dve.tensor_copy(mst, mnew))
                signal(TT(dl, dl, rows(mt, P), ALU.subtract), dlog_ready, l * 2 + s + 1)
                dve.wait_ge(dexp_ready, l * 2 + s + 1)
                dve.wait_ge(*B.released("qk", 1, it=l))
                for d in range(2):
                    v = dl[:, 4 * d:4 * d + 4]
                    ins = TT(v, v, qk[:, chunk_of(d, s)], ALU.mult)
                    if d == 0:
                        step(ins)
                signal(ins, sc_ready, l * 2 + s + 1)
                if s == 0:
                    dve.wait_ge(*B.released("kt", 1, it=l))
                    for d in range(2):
                        ins = TT(kw[:, 4 * d:4 * d + 4], k_tok[:, chunk_of(d, 0)], rows(ex3[:, 2, 4 * d:4 * d + 4], P), ALU.mult)
                        if d == 0:
                            step(ins)
                    signal(ins, kw_ready, l + 1)

            def divide(s):
                dve.wait_ge(*B.released("num", s, 3, it=l))
                if s == 1:
                    for j in range(4):
                        filled("ix", j)
                        for i in range(2):
                            c = 2 * j + i
                            ins = STT(out=tot[:, c], in0=bank("ix", j)[:, i * 129:(i + 1) * 129], scalar=ex3[:, 0, c:c + 1],
                                      in1=tot[:, c], op0=ALU.mult, op1=ALU.add)
                            if i == 0:
                                step(ins)
                        take(ins, "ix", j)
                d_ = tot[:, :, P:].rearrange("p a b -> p (a b)")
                step(STT(out=den, in0=d_, scalar=-1.0, in1=d_, op0=ALU.mult, op1=ALU.max))
                step(TT(den, den, ex3[:, 1], ALU.max))
                step(dve.reciprocal(den, den))
                for d in range(2):
                    v, rd = tot[:, 4 * d:4 * d + 4, 0:P], rows(den[:, 4 * d:4 * d + 4], P)
                    if s == 0:
                        step(TT(hm[:, chunk_of(d, 0)], v, rd, ALU.mult))
                    else:
                        step(TT(v, v, rd, ALU.mult))
                        step(TT(hm[:, chunk_of(d, 1)], hm[:, chunk_of(d, 1)], v, ALU.add))
                if s == 0:
                    dve.nop().then_inc(total_ready, 1)

            weigh(0)
            for t in range(NT):
                for dst, name in ((qT, "qT"), (kT, "kT")):
                    filled(name, t)
                    take(dve.tensor_copy(dst[:, :, t * P:(t + 1) * P], cut(bank(name, t), 4)), name, t)
            soften(0)
            normalise(0)
            divide(0)
            weigh(1)
            soften(1)
            divide(1)
            hm8 = hm.rearrange("p t h n -> p (t h) n")
            step(TT(kw, hm8, hm8, ALU.mult))
            step(dve.tensor_reduce(hs, kw, AX.X, ALU.add))
            step(TS(hs, hs, 1.0 / P, EPS, ALU.mult, ALU.add))
            signal(dve.reciprocal(hs, hs), var_ready, l * 5 + 2)
            normalise(1)
            dve.wait_ge(rstd_ready, l * 5 + 2)
            signal(TT(hm8, hm8, rows(hs, P), ALU.mult), hm_ready, l + 1)
            for t in range(NT):
                filled("hT", t)
                for i in range(MH):
                    ins = STT(out=cat[:, 4 + i, t * P:(t + 1) * P], in0=bank("hT", t)[:, i * P:(i + 1) * P],
                              scalar=prm("head_g")[:, i:i + 1], in1=mo[:, i, t * P:(t + 1) * P], op0=ALU.mult, op1=ALU.mult)
                    if i < MH - 1:
                        step(ins)
                take(ins, "hT", t)
            inverse_root(1, 3)
            add_normed(prm("mix_post"), 2)
            inverse_root(2, 4)
            norm_input(prm("ffn_pre"))

            def outer_taps(c):
                dve.wait_ge(tap_ready, l * FC + (c + 1))
                for part in range(2):
                    f = c + FC * part
                    u, v = bank("up", c)[:, part * L:(part + 1) * L], taps[:, c % 3, part]
                    fw = prm("ffn_w")[:, 3 * f:3 * f + 3]
                    step(STT(out=v[:, 1:], in0=u[:, 0:L - 1], scalar=fw[:, 0:1], in1=v[:, 1:], op0=ALU.mult, op1=ALU.add))
                    ins = STT(out=v[:, 0:L - 1], in0=u[:, 1:], scalar=fw[:, 2:3], in1=v[:, 0:L - 1], op0=ALU.mult, op1=ALU.add)
                    if part == 0:
                        step(ins)
                take(ins, "up", c)
                dve.nop().then_inc(conv2_ready, 1)

            def hidden(c):
                dve.wait_ge(gelu_ready, l * FC + (c + 1))
                signal(TT(hid[:, c], taps[:, c % 3, 0], taps[:, c % 3, 1], ALU.mult), hid_ready, l * FC + (c + 1))

            for c in range(FC):
                outer_taps(c)
                if c >= 1:
                    hidden(c - 1)
            hidden(FC - 1)
            inverse_root(3, 5)
            add_normed(prm("ffn_post"), 3, last=True)


def program(nc, shapes):
    io = {name: nc.dram_tensor(name, shapes[name], F32, kind="ExternalInput").ap() for name in INPUTS}
    out = nc.dram_tensor("out", [P, KC, L], F32, kind="ExternalOutput").ap()
    with ExitStack() as ctx:
        mem = Memory(nc, ctx)
        with ExitStack() as c1:
            X = first_block(nc, c1, io, mem)
        second_block(nc, ctx, io, mem, out, X.y_sum)


def kernel(**inputs):
    import concourse.bacc as _bacc
    from concourse.bass_utils import run_bass_kernel_spmd as _run

    arrays = {name: np.ascontiguousarray(v) for name, v in lay_out(inputs).items()}
    nc = _bacc.Bacc("TRN2", target_bir_lowering=False, num_devices=1)
    program(nc, {name: v.shape for name, v in arrays.items()})
    r = _run(nc, [arrays], core_ids=[0])
    return r.results[0]["out"].transpose(2, 1, 0).reshape(1, L, D)
```
